# Optimizing a Trainium2 kernel written in Bass

```python
import math
import jax, jax.numpy as jnp
from jax import lax
import numpy as np

D_MODEL = 1024
BATCH = 1
SEQ = 1024
DEPTH = 2

N_MIXERS = 2
HEAD_DIM_A = 64
DIL_GROUPS = ((128, 1), (512, 4), (2048, 16))
HEADS_PER_GROUP_A = 6
N_HEADS_A = HEADS_PER_GROUP_A * len(DIL_GROUPS)
WIDTH_A = N_HEADS_A * HEAD_DIM_A
N_BUCKETS = 32
T5_MAX_DISTANCE = 1024
N_HEADS_B = 16
QK_NOPE_DIM = 64
QK_ROPE_DIM = 32
V_HEAD_DIM = 64
Q_LORA_RANK = 256
KV_LORA_RANK = 128
WIDTH_B = N_HEADS_B * V_HEAD_DIM
IN_B = Q_LORA_RANK + KV_LORA_RANK + QK_ROPE_DIM + WIDTH_B
ROPE_THETA = 10000.0
Q_BLOCK = 128
DEPTH_A = (DEPTH + N_MIXERS - 1) // N_MIXERS
DEPTH_B = DEPTH // N_MIXERS
DEEPNORM_ALPHA = (2.0 * DEPTH) ** 0.25
DEEPNORM_BETA = (8.0 * DEPTH) ** -0.25
LN_EPS = 1e-5
RMS_EPS = 1e-6
NEG_INF = -1e30


def layernorm(x, g, b):
    xf = x.astype(jnp.float32)
    mu = xf.mean(-1, keepdims=True)
    var = jnp.square(xf - mu).mean(-1, keepdims=True)
    return ((xf - mu) * lax.rsqrt(var + LN_EPS) * g.astype(jnp.float32) + b.astype(jnp.float32)).astype(x.dtype)

def rmsnorm(x, g):
    xf = x.astype(jnp.float32)
    return (xf * lax.rsqrt(jnp.square(xf).mean(-1, keepdims=True) + RMS_EPS) * g.astype(jnp.float32)).astype(x.dtype)

def t5_bucket(rel):
    half = N_BUCKETS // 2
    max_exact = half // 2
    base = jnp.where(rel > 0, half, 0)
    n = jnp.abs(rel)
    nf = jnp.maximum(n, 1).astype(jnp.float32)
    large = max_exact + (jnp.log(nf / max_exact) / math.log(T5_MAX_DISTANCE / max_exact)
                         * (half - max_exact)).astype(jnp.int32)
    large = jnp.minimum(large, half - 1)
    return base + jnp.where(n < max_exact, n, large)

def dilated_window_attention(q, k, v, bias_table, window, dil):
    B, S, H, Dh = q.shape
    R = window // (2 * dil)
    L = S // dil
    nb = -(-L // R)
    Lp = nb * R

    def to_sub(t):
        return t.reshape(B, L, dil, H, Dh).transpose(0, 2, 3, 1, 4)

    qs = jnp.pad(to_sub(q), ((0, 0), (0, 0), (0, 0), (0, Lp - L), (0, 0))).reshape(B, dil, H, nb, R, Dh)

    def key_blocks(t):
        tp = jnp.pad(to_sub(t), ((0, 0), (0, 0), (0, 0), (R, Lp - L + R), (0, 0))).reshape(B, dil, H, nb + 2, R, Dh)
        return jnp.concatenate([tp[:, :, :, :-2], tp[:, :, :, 1:-1], tp[:, :, :, 2:]], axis=4)

    kb = key_blocks(k)
    vb = key_blocks(v)
    a = jnp.arange(R)[:, None]
    bk = jnp.arange(3 * R)[None, :]
    off = bk - R - a
    kpos = jnp.arange(nb)[:, None, None] * R + bk[None] - R
    valid = (jnp.abs(off) <= R)[None] & (kpos >= 0) & (kpos < L)
    bias = bias_table[t5_bucket(off * dil)].transpose(2, 0, 1).astype(jnp.float32)

    s = jnp.einsum('bdhnqe,bdhnke->bdhnqk', qs, kb).astype(jnp.float32) * (Dh ** -0.5) + bias[:, None]
    s = jnp.where(valid, s, NEG_INF)
    m = s.max(-1, keepdims=True)
    p = jnp.exp(s - m)
    denom = p.sum(-1, keepdims=True)
    o = jnp.einsum('bdhnqk,bdhnke->bdhnqe', p, vb.astype(jnp.float32)) / denom
    lse = (m + jnp.log(denom))[..., 0]

    def from_sub(t):
        t = t.reshape(B, dil, H, Lp, *t.shape[5:])[:, :, :, :L]
        t = jnp.moveaxis(t, 3, 1)
        return t.reshape(B, S, H, *t.shape[4:])

    return from_sub(o).astype(q.dtype), from_sub(lse)

def mixer_dilated(u, w_in, w_out, rel_bias):
    B, S, _ = u.shape
    q, k, v, gate = jnp.split(u @ w_in, 4, axis=-1)
    q = q.reshape(B, S, N_HEADS_A, HEAD_DIM_A)
    k = k.reshape(B, S, N_HEADS_A, HEAD_DIM_A)
    v = v.reshape(B, S, N_HEADS_A, HEAD_DIM_A)
    outs, lses = [], []
    for g, (window, dil) in enumerate(DIL_GROUPS):
        hs = slice(g * HEADS_PER_GROUP_A, (g + 1) * HEADS_PER_GROUP_A)
        o, l = dilated_window_attention(q[:, :, hs], k[:, :, hs], v[:, :, hs], rel_bias[:, hs], window, dil)
        outs.append(o)
        lses.append(l)
    wts = jax.nn.softmax(jnp.stack(lses, axis=0), axis=0).astype(u.dtype)
    o = jnp.concatenate([outs[g] * wts[g][..., None] for g in range(len(DIL_GROUPS))], axis=2)
    y = o.reshape(B, S, WIDTH_A) * jax.nn.silu(gate)
    return y @ w_out

def rope(x, cos, sin):
    half = x.shape[-1] // 2
    x1, x2 = x[..., :half], x[..., half:]
    return jnp.concatenate([x1 * cos - x2 * sin, x2 * cos + x1 * sin], axis=-1)

def mixer_mla(u, w_in, q_norm, w_uq, kv_norm, w_ukv, w_out):
    B, S, _ = u.shape
    cq, ckv, k_rope, gate = jnp.split(
        u @ w_in, [Q_LORA_RANK, Q_LORA_RANK + KV_LORA_RANK, Q_LORA_RANK + KV_LORA_RANK + QK_ROPE_DIM], axis=-1)
    q = (rmsnorm(cq, q_norm) @ w_uq).reshape(B, S, N_HEADS_B, QK_NOPE_DIM + QK_ROPE_DIM)
    q_nope, q_rope = q[..., :QK_NOPE_DIM], q[..., QK_NOPE_DIM:]
    kv = (rmsnorm(ckv, kv_norm) @ w_ukv).reshape(B, S, N_HEADS_B, QK_NOPE_DIM + V_HEAD_DIM)
    k_nope, v = kv[..., :QK_NOPE_DIM], kv[..., QK_NOPE_DIM:]

    pos = jnp.arange(S, dtype=jnp.float32)
    inv_freq = ROPE_THETA ** (-jnp.arange(0, QK_ROPE_DIM, 2, dtype=jnp.float32) / QK_ROPE_DIM)
    ang = pos[:, None] * inv_freq[None, :]
    cos, sin = jnp.cos(ang).astype(u.dtype), jnp.sin(ang).astype(u.dtype)
    q_rope = rope(q_rope, cos[:, None], sin[:, None])
    k_rope = rope(k_rope, cos, sin)

    scale = (QK_NOPE_DIM + QK_ROPE_DIM) ** -0.5
    nq = S // Q_BLOCK
    qn_b = q_nope.reshape(B, nq, Q_BLOCK, N_HEADS_B, QK_NOPE_DIM).transpose(1, 0, 2, 3, 4)
    qr_b = q_rope.reshape(B, nq, Q_BLOCK, N_HEADS_B, QK_ROPE_DIM).transpose(1, 0, 2, 3, 4)

    def block(args):
        qn, qr = args
        s = (jnp.einsum('bqhd,bkhd->bhqk', qn, k_nope)
             + jnp.einsum('bqhd,bkd->bhqk', qr, k_rope)).astype(jnp.float32) * scale
        p = jax.nn.softmax(s, axis=-1).astype(v.dtype)
        return jnp.einsum('bhqk,bkhd->bqhd', p, v)

    o = lax.map(block, (qn_b, qr_b))
    o = o.transpose(1, 0, 2, 3, 4).reshape(B, S, WIDTH_B)
    y = o * jax.nn.silu(gate)
    return y @ w_out

def first_inputs(seed: int = 0) -> dict:
    key = jax.random.key(seed)
    ks = jax.random.split(key, 20)
    nrm = jax.random.normal
    D = D_MODEL
    x = nrm(ks[0], (BATCH, SEQ, D), jnp.float32)
    c = nrm(ks[1], (BATCH, D), jnp.float32)
    rel_bias = 0.2 * nrm(ks[2], (N_BUCKETS, N_HEADS_A), jnp.float32)
    ada_w = 0.5 * D ** -0.5 * nrm(ks[3], (DEPTH, D, 3 * D), jnp.float32)
    ada_b = 0.02 * nrm(ks[4], (DEPTH, 3 * D), jnp.float32)
    ln_g = 1.0 + 0.05 * nrm(ks[5], (DEPTH, D), jnp.float32)
    ln_b = 0.02 * nrm(ks[6], (DEPTH, D), jnp.float32)
    a_w_in = D ** -0.5 * nrm(ks[7], (DEPTH_A, D, 4 * WIDTH_A), jnp.float32)
    a_w_in = a_w_in.at[:, :, 2 * WIDTH_A:3 * WIDTH_A].multiply(DEEPNORM_BETA)
    a_w_out = DEEPNORM_BETA * WIDTH_A ** -0.5 * nrm(ks[8], (DEPTH_A, WIDTH_A, D), jnp.float32)
    b_w_in = D ** -0.5 * nrm(ks[9], (DEPTH_B, D, IN_B), jnp.float32)
    b_q_norm = 1.0 + 0.05 * nrm(ks[10], (DEPTH_B, Q_LORA_RANK), jnp.float32)
    b_w_uq = Q_LORA_RANK ** -0.5 * nrm(ks[11], (DEPTH_B, Q_LORA_RANK, N_HEADS_B * (QK_NOPE_DIM + QK_ROPE_DIM)), jnp.float32)
    b_kv_norm = 1.0 + 0.05 * nrm(ks[12], (DEPTH_B, KV_LORA_RANK), jnp.float32)
    b_w_ukv = KV_LORA_RANK ** -0.5 * nrm(ks[13], (DEPTH_B, KV_LORA_RANK, N_HEADS_B, QK_NOPE_DIM + V_HEAD_DIM), jnp.float32)
    b_w_ukv = b_w_ukv.at[..., QK_NOPE_DIM:].multiply(DEEPNORM_BETA).reshape(
        DEPTH_B, KV_LORA_RANK, N_HEADS_B * (QK_NOPE_DIM + V_HEAD_DIM))
    b_w_out = DEEPNORM_BETA * WIDTH_B ** -0.5 * nrm(ks[14], (DEPTH_B, WIDTH_B, D), jnp.float32)
    return {"x": x, "c": c, "rel_bias": rel_bias, "ada_w": ada_w, "ada_b": ada_b,
            "ln_g": ln_g, "ln_b": ln_b, "a_w_in": a_w_in, "a_w_out": a_w_out,
            "b_w_in": b_w_in, "b_q_norm": b_q_norm, "b_w_uq": b_w_uq, "b_kv_norm": b_kv_norm,
            "b_w_ukv": b_w_ukv, "b_w_out": b_w_out}

def first_block(x, c, rel_bias, ada_w, ada_b, ln_g, ln_b, a_w_in, a_w_out,
              b_w_in, b_q_norm, b_w_uq, b_kv_norm, b_w_ukv, b_w_out):
    for i in range(DEPTH):
        mod = jax.nn.silu(c) @ ada_w[i] + ada_b[i]
        shift, scale, gate = jnp.split(mod[:, None, :], 3, axis=-1)
        u = x * (1 + scale) + shift
        j = i // N_MIXERS
        if i % N_MIXERS == 0:
            y = mixer_dilated(u, a_w_in[j], a_w_out[j], rel_bias)
        else:
            y = mixer_mla(u, b_w_in[j], b_q_norm[j], b_w_uq[j], b_kv_norm[j], b_w_ukv[j], b_w_out[j])
        x = layernorm(DEEPNORM_ALPHA * x + gate * y, ln_g[i], ln_b[i])
    return x


DA_HEADS = 4
DA_QK_DIM = 64
DA_V_DIM = 2 * DA_QK_DIM
DA_ROT_DIM = DA_QK_DIM // 4
ROPE_THETA_2 = 500000.0
RET_HEADS = 4
RET_QK_DIM = 32
RET_V_DIM = 2 * RET_QK_DIM
RET_THETA = 10000.0
RET_CHUNK = 128
POOL_GROUPS = 4
POOL_DIM = 64
POOL_WINDOWS = (2, 4, 8, 16)
DA_WIDTH = DA_HEADS * DA_V_DIM
RET_WIDTH = RET_HEADS * RET_V_DIM
POOL_WIDTH = POOL_GROUPS * POOL_DIM
MIX_WIDTH = DA_WIDTH + RET_WIDTH + POOL_WIDTH
SPLIT_SIZES = (DA_HEADS * 2 * DA_QK_DIM, DA_HEADS * 2 * DA_QK_DIM, DA_WIDTH,
               RET_HEADS * RET_QK_DIM, RET_HEADS * RET_QK_DIM, RET_WIDTH, RET_WIDTH,
               POOL_WIDTH)
IN_WIDTH = 2560
D_FF = 2816
CONV_WIDTH = 3
EPS = 1e-6


def rms_norm(x, g):
    xf = x.astype(jnp.float32)
    y = xf * lax.rsqrt(jnp.mean(xf * xf, axis=-1, keepdims=True) + EPS)
    return (y * g).astype(x.dtype)

def rotary(x, pos, rot_dim, theta):
    inv = jnp.float32(theta) ** (-jnp.arange(0, rot_dim, 2, dtype=jnp.float32) / rot_dim)
    ang = pos[:, None] * inv[None, :]
    cos = jnp.cos(ang).astype(x.dtype)
    sin = jnp.sin(ang).astype(x.dtype)
    half = rot_dim // 2
    x1, x2, xp = x[..., :half], x[..., half:rot_dim], x[..., rot_dim:]
    return jnp.concatenate([x1 * cos - x2 * sin, x2 * cos + x1 * sin, xp], axis=-1)

def diff_attention(q, k, v, lq1, lk1, lq2, lk2, subln_g, lam_init):
    B, S, _ = q.shape
    pos = jnp.arange(S, dtype=jnp.float32)
    q = q.reshape(B, S, DA_HEADS, 2, DA_QK_DIM).transpose(0, 2, 3, 1, 4)
    k = k.reshape(B, S, DA_HEADS, 2, DA_QK_DIM).transpose(0, 2, 3, 1, 4)
    q = rotary(q, pos, DA_ROT_DIM, ROPE_THETA_2)
    k = rotary(k, pos, DA_ROT_DIM, ROPE_THETA_2)
    v = v.reshape(B, S, DA_HEADS, DA_V_DIM).transpose(0, 2, 1, 3)
    lam = (jnp.exp(jnp.sum(lq1.astype(jnp.float32) * lk1.astype(jnp.float32)))
           - jnp.exp(jnp.sum(lq2.astype(jnp.float32) * lk2.astype(jnp.float32))) + lam_init)
    scale = DA_QK_DIM ** -0.5
    nb = S // Q_BLOCK
    qb = q.reshape(B, DA_HEADS, 2, nb, Q_BLOCK, DA_QK_DIM).transpose(3, 0, 1, 2, 4, 5)
    kpos = jnp.arange(S)

    def block(args):
        q_blk, i = args
        s = jnp.einsum('bhmqd,bhmkd->bhmqk', q_blk, k).astype(jnp.float32) * scale
        qpos = i * Q_BLOCK + jnp.arange(Q_BLOCK)
        mask = kpos[None, :] <= qpos[:, None]
        p = jax.nn.softmax(jnp.where(mask, s, -jnp.inf), axis=-1)
        a = p[:, :, 0] - lam * p[:, :, 1]
        return jnp.einsum('bhqk,bhkd->bhqd', a.astype(v.dtype), v)

    o = lax.map(block, (qb, jnp.arange(nb)))
    o = o.transpose(1, 0, 3, 2, 4).reshape(B, S, DA_HEADS, DA_V_DIM)
    o = rms_norm(o, subln_g) * (1.0 - lam_init)
    return o.reshape(B, S, DA_WIDTH)

def retention(q, k, v, g, ret_g):
    B, S, _ = q.shape
    H, dk, dv, C = RET_HEADS, RET_QK_DIM, RET_V_DIM, RET_CHUNK
    pos = jnp.arange(S, dtype=jnp.float32)
    q = rotary(q.reshape(B, S, H, dk).transpose(0, 2, 1, 3), pos, dk, RET_THETA)
    k = rotary(k.reshape(B, S, H, dk).transpose(0, 2, 1, 3), pos, dk, RET_THETA) * (dk ** -0.5)
    v = v.reshape(B, S, H, dv).transpose(0, 2, 1, 3)
    log_g = jnp.log(1.0 - 2.0 ** (-5.0 - jnp.arange(H, dtype=jnp.float32)))
    idx = jnp.arange(C, dtype=jnp.float32)
    diff = idx[:, None] - idx[None, :]
    decay = jnp.where(diff >= 0, jnp.exp(jnp.maximum(diff, 0.0) * log_g[:, None, None]), 0.0)
    xi = jnp.exp((idx + 1.0) * log_g[:, None])[..., None]
    zeta = jnp.exp((C - 1.0 - idx) * log_g[:, None])[..., None]
    chunk_decay = jnp.exp(C * log_g)[:, None, None]
    nc = S // C

    def to_chunks(t):
        return t.reshape(B, H, nc, C, t.shape[-1]).transpose(2, 0, 1, 3, 4).astype(jnp.float32)

    def step(state, inp):
        qi, ki, vi = inp
        inner = jnp.einsum('bhqd,bhkd->bhqk', qi, ki) * decay
        o = (jnp.einsum('bhqk,bhkv->bhqv', inner, vi)
             + jnp.einsum('bhqd,bhdv->bhqv', qi * xi, state))
        state = state * chunk_decay + jnp.einsum('bhkd,bhkv->bhdv', ki * zeta, vi)
        return state, o

    state0 = jnp.zeros((B, H, dk, dv), jnp.float32)
    _, o = lax.scan(step, state0, (to_chunks(q), to_chunks(k), to_chunks(v)))
    o = o.transpose(1, 0, 3, 2, 4).reshape(B, S, H, dv)
    mu = jnp.mean(o, axis=-1, keepdims=True)
    var = jnp.mean(jnp.square(o - mu), axis=-1, keepdims=True)
    o = (o - mu) * lax.rsqrt(var + EPS) * ret_g.reshape(H, dv)
    return jax.nn.silu(g) * o.reshape(B, S, RET_WIDTH).astype(g.dtype)

def pool_mixer(u, pool_w, pool_scale):
    B, S, _ = u.shape
    ug = u.reshape(B, S, POOL_GROUPS, POOL_DIM).astype(jnp.float32)
    c = jnp.cumsum(ug, axis=1)
    t = jnp.arange(S, dtype=jnp.float32)
    means = []
    for gi, w in enumerate(POOL_WINDOWS):
        cg = c[:, :, gi]
        shifted = jnp.pad(cg, ((0, 0), (w, 0), (0, 0)))[:, :S]
        means.append((cg - shifted) / jnp.minimum(t + 1.0, float(w))[:, None])
    pooled = (jnp.stack(means, axis=2) - ug).astype(u.dtype)
    y = jnp.einsum('bsgp,gpq->bsgq', pooled, pool_w)
    return y.reshape(B, S, POOL_WIDTH) * pool_scale

def conv_mlp(h, w_up, conv_w, conv_b, w_down):
    S = h.shape[1]
    u = h @ w_up
    up = jnp.pad(u, ((0, 0), (CONV_WIDTH - 1, 0), (0, 0)))
    uc = conv_b + sum(conv_w[j] * up[:, j:j + S] for j in range(CONV_WIDTH))
    gate, val = jnp.split(uc, 2, axis=-1)
    return (jax.nn.gelu(gate, approximate=True) * val) @ w_down

def second_inputs(seed: int = 0) -> dict:
    key = jax.random.key(seed)
    ks = jax.random.split(key, 24)
    f32 = jnp.float32

    def nrm(k, shape, scale):
        return jax.random.normal(k, shape, f32) * scale

    def gain(k, shape):
        return 1.0 + 0.05 * jax.random.normal(k, shape, f32)

    L = DEPTH
    return {
        "x": nrm(ks[0], (BATCH, SEQ, D_MODEL), 1.0),
        "norm_mix_pre": gain(ks[1], (L, D_MODEL)),
        "norm_mix_post": gain(ks[2], (L, D_MODEL)),
        "w_in": nrm(ks[3], (L, D_MODEL, IN_WIDTH), D_MODEL ** -0.5),
        "lambda_q1": nrm(ks[4], (L, DA_QK_DIM), 0.1),
        "lambda_k1": nrm(ks[5], (L, DA_QK_DIM), 0.1),
        "lambda_q2": nrm(ks[6], (L, DA_QK_DIM), 0.1),
        "lambda_k2": nrm(ks[7], (L, DA_QK_DIM), 0.1),
        "diff_subln": gain(ks[8], (L, DA_V_DIM)),
        "ret_norm": gain(ks[9], (L, RET_WIDTH)),
        "pool_w": nrm(ks[10], (L, POOL_GROUPS, POOL_DIM, POOL_DIM), POOL_DIM ** -0.5),
        "pool_scale": 0.5 + 0.1 * jax.random.normal(ks[11], (L, POOL_WIDTH), f32),
        "w_out": nrm(ks[12], (L, MIX_WIDTH, D_MODEL), MIX_WIDTH ** -0.5),
        "norm_mlp_pre": gain(ks[13], (L, D_MODEL)),
        "norm_mlp_post": gain(ks[14], (L, D_MODEL)),
        "w_up": nrm(ks[15], (L, D_MODEL, 2 * D_FF), D_MODEL ** -0.5),
        "conv_w": nrm(ks[16], (L, CONV_WIDTH, 2 * D_FF), CONV_WIDTH ** -0.5),
        "conv_b": nrm(ks[17], (L, 2 * D_FF), 0.02),
        "w_down": nrm(ks[18], (L, D_FF, D_MODEL), D_FF ** -0.5),
    }

def second_block(x, norm_mix_pre, norm_mix_post, w_in, lambda_q1, lambda_k1, lambda_q2, lambda_k2,
              diff_subln, ret_norm, pool_w, pool_scale, w_out, norm_mlp_pre, norm_mlp_post,
              w_up, conv_w, conv_b, w_down):
    split_points = []
    acc = 0
    for s in SPLIT_SIZES[:-1]:
        acc += s
        split_points.append(acc)
    for l in range(DEPTH):
        lam_init = 0.8 - 0.6 * math.exp(-0.3 * l)
        h = rms_norm(x, norm_mix_pre[l])
        proj = h @ w_in[l]
        q_da, k_da, v_da, q_r, k_r, v_r, g_r, u_pool = jnp.split(proj, split_points, axis=-1)
        o_da = diff_attention(q_da, k_da, v_da, lambda_q1[l], lambda_k1[l], lambda_q2[l],
                              lambda_k2[l], diff_subln[l], lam_init)
        o_ret = retention(q_r, k_r, v_r, g_r, ret_norm[l])
        o_pool = pool_mixer(u_pool, pool_w[l], pool_scale[l])
        mix = jnp.concatenate([o_da, o_ret, o_pool], axis=-1) @ w_out[l]
        x = x + rms_norm(mix, norm_mix_post[l])
        h = rms_norm(x, norm_mlp_pre[l])
        y = conv_mlp(h, w_up[l], conv_w[l], conv_b[l], w_down[l])
        x = x + rms_norm(y, norm_mlp_post[l])
    return x


def setup_inputs(seed=0):
    out = dict(first_inputs(seed))
    for name, value in second_inputs(seed + 1).items():
        if name != "x":
            out[name + "_2"] = value
    return out


def reference(
    x, c, rel_bias, ada_w, ada_b, ln_g, ln_b, a_w_in, a_w_out, b_w_in, b_q_norm, b_w_uq,
    b_kv_norm, b_w_ukv, b_w_out, norm_mix_pre_2, norm_mix_post_2, w_in_2, lambda_q1_2,
    lambda_k1_2, lambda_q2_2, lambda_k2_2, diff_subln_2, ret_norm_2, pool_w_2, pool_scale_2,
    w_out_2, norm_mlp_pre_2, norm_mlp_post_2, w_up_2, conv_w_2, conv_b_2, w_down_2,
):
    x = first_block(
        x, c, rel_bias, ada_w, ada_b, ln_g, ln_b, a_w_in, a_w_out, b_w_in, b_q_norm, b_w_uq,
        b_kv_norm, b_w_ukv, b_w_out,
    )
    return second_block(
        x, norm_mix_pre_2, norm_mix_post_2, w_in_2, lambda_q1_2, lambda_k1_2, lambda_q2_2,
        lambda_k2_2, diff_subln_2, ret_norm_2, pool_w_2, pool_scale_2, w_out_2, norm_mlp_pre_2,
        norm_mlp_post_2, w_up_2, conv_w_2, conv_b_2, w_down_2,
    )


_drawn_inputs = setup_inputs


def setup_inputs(seed=0):
    import zlib

    import numpy as np

    out = dict(_drawn_inputs(seed))
    spreads = {}
    factors = {'rel_bias': 8.0, 'ada_b': 8.0, 'b_q_norm': 8.0, 'b_w_uq': 7.866, 'b_kv_norm': 8.0}
    for name, (base, spread) in spreads.items():
        noise = np.random.default_rng([zlib.crc32(name.encode()), seed]).standard_normal(out[name].shape)
        drawn = base * np.exp(spread * noise) if base else spread * noise
        out[name] = __import__('jax').numpy.asarray(drawn.astype(out[name].dtype))
    for name, factor in factors.items():
        out[name] = (out[name] * factor).astype(out[name].dtype)
    return out
```

```python
import math
from contextlib import ExitStack

import numpy as np

import concourse.bass as bass
from concourse import mybir

F32 = mybir.dt.float32
F32R = mybir.dt.float32r
BF16 = mybir.dt.bfloat16
ALU = mybir.AluOpType
ACT = mybir.ActivationFunctionType
AXX = mybir.AxisListType.X

ALPHA = 4.0 ** 0.25
NS = 11
NMISC = 40
MASKED = -8e30


def host_constants():
    f = np.float32
    c = {}
    c["k_ident"] = np.eye(128, dtype=f)
    oh = np.zeros((32, 3, 512), f)
    mk = np.zeros((6, 3, 512), f)
    for g, dil in enumerate((1, 4, 8)):
        for n in range(512):
            off = n - 256
            if abs(off) > (127 if dil == 8 else 64) or (dil == 8 and off % 2):
                mk[:, g, 511 - n] = MASKED
                continue
            rel = off * dil
            a = abs(rel)
            large = 8 + int(f(np.log(f(max(a, 1)) / f(8))) / f(math.log(128.0)) * f(8))
            b = (16 if rel > 0 else 0) + (a if a < 8 else min(large, 15))
            oh[b, g, 511 - n] = 1.0
    c["k_oh"], c["k_msk"] = oh, mk

    def angles(dim, theta):
        inv = f(theta) ** (-np.arange(0, dim, 2, dtype=f) / f(dim))
        ang = np.arange(1024, dtype=f)[:, None] * inv[None, :].astype(f)
        return np.cos(ang).astype(f), np.sin(ang).astype(f)

    def natural(t):
        return np.ascontiguousarray(t.reshape(8, 128, -1).transpose(1, 0, 2))

    co, si = angles(32, 10000.0)
    c["k_rope"] = np.ascontiguousarray(np.stack([natural(co), natural(si)], 2))
    tab = np.ones((128, 1024), f)
    tab[64:80], tab[80:96] = co.T, co.T
    tab[96:112], tab[112:128] = -si.T, si.T
    c["k_qtab"] = tab
    co, si = angles(16, 500000.0)
    c["k_rope2"] = np.ascontiguousarray(np.stack([natural(co), natural(si)], 2))
    lg = np.log(1.0 - 2.0 ** (-5.0 - np.arange(4))).astype(np.float64)
    idx = np.arange(128)
    sc = 32.0 ** -0.5
    dec = np.zeros((128, 4, 128))
    for h in range(4):
        d = idx[None, :] - idx[:, None]
        dec[:, h, :] = np.where(d >= 0, np.exp(np.maximum(d, 0) * lg[h]), 0.0) * sc
    c["k_decay"] = dec.astype(f)
    hd = np.repeat(np.arange(4), 32)
    c["k_xi"] = np.exp((idx[None, :] + 1.0) * lg[hd][:, None]).astype(f)
    c["k_zeta"] = (np.exp((127.0 - idx[:, None]) * lg[hd][None, :]) * sc).astype(f)
    c["k_cd"] = np.exp(128.0 * lg[hd])[:, None].astype(f)
    c["k_blk"] = (hd[:, None] == np.repeat(np.arange(4), 64)[None, :]).astype(f)
    c["k_causal"] = np.where(idx[None, :] <= idx[:, None], 0.0, -1e30).astype(f)
    w = np.array([[2, 4], [8, 16]])
    inv = np.zeros((128, 2, 17), f)
    for t in range(2):
        for half in range(2):
            ww = w[t, half]
            inv[64 * half:64 * half + 64, t, 0:16] = 1.0 / np.minimum(np.arange(16) + 1.0, ww)
            inv[64 * half:64 * half + 64, t, 16] = 1.0 / ww
    c["k_inv"] = inv
    return c


def flat(waits):
    for w in waits:
        if w is None:
            continue
        if isinstance(w, tuple) and len(w) == 2 and isinstance(w[0], str):
            yield w
        else:
            yield from flat(w)


class Prog:

    def __init__(self, nc, ctx):
        self.q = {e: [] for e in ("pe", "dve", "act", "pool", "sp")}
        self.sem = {e: ctx.enter_context(nc.semaphore("s_" + e)) for e in self.q}
        self.n = {}
        self.nc, self.ctx = nc, ctx
        self.misc = 0
        self.last_misc = {}

    def op(self, e, f, *waits, mark=True):
        tok = None
        if mark:
            self.n[e] = self.n.get(e, 0) + 1
            tok = (e, self.n[e])
        self.q[e].append((list(flat(waits)), f, e if mark else None, 1))
        return tok

    def dma(self, e, out, in_, *waits, sem=None):
        if sem is None:
            sem = f"d{self.misc % NMISC}"
            self.misc += 1
            waits = (*waits, self.last_misc.get(sem))
        if sem not in self.sem:
            self.sem[sem] = self.ctx.enter_context(self.nc.semaphore(sem))
        self.n[sem] = self.n.get(sem, 0) + 16
        tok = (sem, self.n[sem])
        self.last_misc[sem] = tok
        self.q[e].append((list(flat(waits)), lambda eng: eng.dma_start(out, in_), sem, 16))
        return tok

    def emit(self, e, eng):
        seen = {}
        for waits, f, sem, by in self.q[e]:
            for s, v in waits:
                if seen.get(s, 0) < v:
                    eng.wait_ge(self.sem[s], v)
                    seen[s] = v
            ins = f(eng)
            if sem is not None:
                ins.then_inc(self.sem[sem], by)


class Kernel:
    def __init__(self, nc, I, out, stop):
        self.nc, self.I, self.out, self.stop = nc, I, out, stop

    def mm(self, out, terms, *waits):
        last = len(terms) - 1
        for i, t in enumerate(terms):
            tok = self.P.op(
                "pe", lambda e, t=t, i=i: e.matmul(out, t[0], t[1], start=(i == 0), stop=(i == last)),
                waits if i == 0 else None, t[2:], mark=(i == last))
        return tok

    def tr(self, out, in_, *waits, mark=True):
        k = in_.shape[0]
        return self.P.op("pe", lambda e: e.transpose(out, in_, self.ident[0:k, 0:k]), waits, mark=mark)

    def copy(self, out, in_, *waits):
        return self.P.op("act", lambda e: e.activation(out, in_, ACT.Copy), waits)

    def act(self, out, in_, fn, *waits, **kw):
        return self.P.op("act", lambda e: e.activation(out, in_, fn, **kw), waits)

    def vcopy(self, out, in_, *waits):
        return self.P.op("dve", lambda e: e.tensor_copy(out, in_), waits)

    def tt(self, out, a, b, op, *waits, eng="dve"):
        return self.P.op(eng, lambda e: e.tensor_tensor(out, a, b, op), waits)

    def ts(self, out, a, s1, s2, o1, o2, *waits, eng="dve"):
        if o2 is None:
            return self.P.op(eng, lambda e: e.tensor_scalar(out, a, s1, None, o1), waits)
        return self.P.op(eng, lambda e: e.tensor_scalar(out, a, s1, s2, o1, o2), waits)

    def stt(self, out, a, s, b, o1, o2, *waits, eng="dve"):
        return self.P.op(eng, lambda e: e.scalar_tensor_tensor(out=out, in0=a, scalar=s, in1=b, op0=o1, op1=o2),
                         waits)

    def red(self, out, a, op, *waits):
        return self.P.op("dve", lambda e: e.tensor_reduce(out, a, AXX, op), waits)

    def rec(self, out, a, *waits):
        return self.P.op("dve", lambda e: e.reciprocal(out, a), waits)

    def zero(self, out, *waits, value=0.0, eng="dve"):
        return self.P.op(eng, lambda e: e.memset(out, value), waits)

    def at(self, name, shape, dt, off):
        size = int(np.prod(shape[1:])) * (2 if dt == BF16 else 4)
        assert off % 32 == 0 and off + size <= self.end, (name, off, size, self.end)
        return self.nc.alloc_sbuf_tensor_at(name, list(shape), dt, offset=off)

    class Region:
        def __init__(self, k, off, end, tag):
            self.k, self.off, self.end, self.tag = k, off, end, tag

        def new(self, name, shape, dt=F32):
            t = self.k.at(f"{self.tag}_{name}", shape, dt, self.off)
            size = int(np.prod(shape[1:])) * (2 if dt == BF16 else 4)
            self.off += (size + 31) // 32 * 32
            assert self.off <= self.end, (self.tag, name, self.off - self.end)
            return t

    def take(self, ring):
        b = self.rings[ring][self.ring_at.get(ring, 0) % len(self.rings[ring])]
        self.ring_at[ring] = self.ring_at.get(ring, 0) + 1
        n = b if isinstance(b, tuple) else (b,)
        waits = []
        for x in n:
            assert self.free[x] is not None, ("bank in use", ring, x)
            waits.append(self.free[x])
            self.free[x] = None
        return n, waits

    def give(self, banks, *toks):
        for x in banks:
            self.free[x] = list(toks)

    def weight(self, pieces):
        n = self.wn
        self.wn += 1
        s = n % NS
        assert n < NS or self.wfree.get(n - NS) is not None, "slot in use"
        freed = self.wfree.pop(n - NS, None)
        w = 0
        for c, ap in pieces:
            ww = int(np.prod(ap.shape[1:]))
            dst = self.wst[:, s, c:c + ww]
            if len(ap.shape) == 3:
                dst = dst.rearrange("p (a b) -> p a b", a=ap.shape[1])
            t = self.P.dma("sp", dst, ap, freed, sem=f"w{s}")
            w = max(w, c + ww)
        hi = self.P.op("pool", lambda e: e.tensor_copy(self.whi[:, s, 0:w], self.wst[:, s, 0:w]), t)
        lo = self.P.op("pool", lambda e: e.tensor_tensor(
            self.wlo[:, s, 0:w], self.wst[:, s, 0:w], self.whi[:, s, 0:w], ALU.subtract), hi)
        return n, s, lo

    def release(self, ws, tok):
        for n, _, _ in ws:
            self.wfree[n] = tok

    def proj_nat(self, nk, src, w, sels, ready, evac, act=None, ring="proj"):
        hi, lo = act or (self.thi, self.tlo)
        ws = [self.weight(src(k)) for k in range(nk)]
        for j, sel in enumerate(sels):
            b, fw = self.take(ring)
            terms = []
            for k in range(nk):
                _, s, wt = ws[k]
                h, l = sel(hi, k), sel(lo, k)
                terms += [(h, self.whi[:, s, 0:w], wt), (h, self.wlo[:, s, 0:w]), (l, self.whi[:, s, 0:w])]
            tok = self.mm(self.ps[:, b[0], 0:w], terms, fw, ready[j])
            self.last_mm = tok
            evac(j, b, self.ps[:, b[0], 0:w], tok)
        self.release(ws, tok)

    def proj_T(self, nk, src, nm, ready, evac, act=None, ring="proj"):
        hi, lo = act or (self.thi, self.tlo)
        ws = [self.weight(src(k)) for k in range(nk)]
        for m in range(nm):
            c = slice(m * 128, m * 128 + 128)
            for hf in range(2):
                r = slice(hf * 512, hf * 512 + 512)
                b, fw = self.take(ring)
                terms = []
                for k in range(nk):
                    _, s, wt = ws[k]
                    terms += [(self.whi[:, s, c], hi[:, k, r], wt), (self.whi[:, s, c], lo[:, k, r]),
                              (self.wlo[:, s, c], hi[:, k, r])]
                tok = self.mm(self.ps[:, b[0], :], terms, fw, ready[hf])
                evac(m, hf, b, self.ps[:, b[0], :], tok)
        self.release(ws, tok)

    def split(self, hi, lo, src, *waits):
        a = self.copy(hi, src, waits)
        d = self.tt(lo, src, hi.bitcast(F32), ALU.subtract, a)
        return a, d

    def to_T(self, blocks, j, tok, ring="tr", kt0=0):
        toks = []
        js = slice(j * 128, j * 128 + 128)
        done = []
        for q in range(0, len(blocks), 4):
            part = blocks[q:q + 4]
            b, fw = self.take(ring)
            for i, blk in enumerate(part):
                t = self.tr(self.ps[:, b[0], i * 128:i * 128 + 128], blk, fw if i == 0 else None, tok,
                            mark=(i == len(part) - 1))
            done.append((q, len(part), b, t))
        for q, n, b, t in done:
            src = self.ps[:, b[0], 0:128 * n].rearrange("p (a b) -> p a b", a=n)
            k = slice(kt0 + q, kt0 + q + n)
            pair = self.split(self.thi[:, k, js], self.tlo[:, k, js], src, t, done[-1][3])
            self.give(b, *pair)
            toks += pair
        return toks

    def small(self, n):
        w = 32
        assert n <= w
        i = self.sm_at % self.sm_n
        self.sm_at += 1
        return self.sm[:, i * w:i * w + n]

    def rms_scale(self, ss, n, eps, tok):
        sd = self.small(ss.shape[1])
        r = self.small(ss.shape[1])
        t = self.act(sd, ss, ACT.Sqrt, tok, scale=1.0 / n, bias=self.eps[eps])
        return r, self.rec(r, sd, t)

    def build(self):
        nc = self.nc
        with ExitStack() as ctx:
            self.ctx = ctx
            P = self.P = Prog(nc, ctx)
            base = (nc.sbuf_base + 31) // 32 * 32
            self.end = nc.sbuf_usable_end // 32 * 32
            self.ps = ctx.enter_context(nc.psum_tensor("ps", [128, 8, 512], F32))
            self.free = {b: [] for b in range(8)}
            self.rings = {"proj": [0, 1, 2, 3], "tr": [4, 5], "tr4": [4, 5, 6, 7], "s1": [0, 1, 2],
                          "t1": [3, 4, 5], "o1": [6, 7], "s2": [(0, 1), (2, 3)], "t2": [(4, 5)], "o2": [6, 7],
                          "pt": [4, 5, 6, 7]}
            self.ring_at = {}
            off = base
            self.thi = self.at("thi", [128, 9, 1024], F32R, off)
            self.tfi = self.at("tfi", [128, 9, 1024], F32, off)
            off += 36864
            self.tlo = self.at("tlo", [128, 9, 1024], F32R, off)
            self.tfl = self.at("tfl", [128, 9, 1024], F32, off)
            self.t_lo_off = off
            off += 36864
            self.whi = self.at("whi", [128, NS, 512], F32R, off)
            off += NS * 2048
            self.wlo = self.at("wlo", [128, NS, 512], F32R, off)
            self.wst = self.at("wst", [128, NS, 512], F32, off)
            off += NS * 2048
            self.wn, self.wfree = 0, {}
            cr = Kernel.Region(self, off, off + 10240, "cst")
            self.ident = cr.new("ident", [128, 128])
            self.ones = cr.new("ones", [128, 128])
            self.sm_n, self.sm_at = 16, 0
            self.sm = cr.new("sm", [128, 16 * 32])
            self.epst = cr.new("eps", [128, 2])
            self.eps = {1e-5: self.epst[:, 0:1], 1e-6: self.epst[:, 1:2]}
            self.rope = cr.new("rope", [128, 8, 2, 16])
            self.rope2 = cr.new("rope2", [128, 8, 2, 8])
            self.idb = cr.new("idb", [128, 128], BF16)
            self.cmask = cr.new("cmask", [128, 128], BF16)
            self.lamt = cr.new("lam", [128, 8])
            self.cc = cr.new("cc", [128, 16])
            off += 10240
            mr = Kernel.Region(self, off, off + 16384, "mod")
            self.mod_off = off
            self.gate = [mr.new("g0", [128, 1024]), None]
            self.msh = mr.new("sh", [128, 1024])
            self.msc = mr.new("sc", [128, 1024])
            self.gate[1] = mr.new("g1", [128, 1024])
            off += 16384
            self.gen = off
            self.rot_tok = None

            self.d_y = nc.dram_tensor("scr_y", [1024, 3, 396], F32, kind="Internal").ap()
            self.d_v = nc.dram_tensor("scr_v", [3, 6, 512], F32, kind="Internal").ap()
            self.d_x = [nc.dram_tensor(f"scr_x{i}", [8, 128, 1024], F32, kind="Internal").ap() for i in range(5)]
            self.d_tok = [[None] * 8 for _ in range(5)]
            self.all_dram = []

            self.setup()
            self.block1_a()
            if self.stop > 1:
                self.block1_b()
            for l in range(2):
                if self.stop > 2 + 2 * l:
                    self.block2_mix(l)
                if self.stop > 3 + 2 * l:
                    self.block2_mlp(l)
            P.op("sp", lambda e: e.nop(), self.all_dram, mark=False)

            block = ctx.enter_context(nc.Block())

            @block.tensor
            def _(e):
                P.emit("pe", e)

            @block.vector
            def _(e):
                P.emit("dve", e)

            @block.scalar
            def _(e):
                P.emit("act", e)

            @block.gpsimd
            def _(e):
                P.emit("pool", e)

            @block.sync
            def _(e):
                P.emit("sp", e)

    def fence(self):
        return [(e, n) for e, n in self.P.n.items() if n]

    def region(self, tag, mod=False):
        return Kernel.Region(self, self.mod_off if mod else self.gen, self.end, tag)

    def bc(self, out, row, *waits, e="act"):
        return self.P.dma(e, out, row.partition_broadcast(128), waits)

    def setup(self):
        P, I = self.P, self.I
        t = [P.dma("act", self.ident[:], I["k_ident"])]
        self.r = R = self.region("ada")
        cT = R.new("cT", [128, 8])
        sc = R.new("sc", [128, 8])
        tc = P.dma("act", cT[:], I["c"].rearrange("o (p k) -> p (o k)", k=8))
        self.ctok = self.act(self.cc[:, 0:8], cT[:], ACT.Silu, tc)
        for i, l in ((self.rope, "k_rope"), (self.rope2, "k_rope2")):
            t.append(P.dma("act", i[:], I[l]))
        a = self.zero(self.ones[:], value=1.0)
        e1 = self.zero(self.epst[:, 0:1], value=1e-5)
        e2 = self.zero(self.epst[:, 1:2], value=1e-6)
        self.base_tok = [t, a, e1, e2]
        self.ada(0, R, 512)

    def ada(self, layer, R, w, chunks=None, state=None):
        P, I = self.P, self.I
        if state is None:
            state = {"buf": [R.new(f"aw{i}", [128, 8, w]) for i in range(2)],
                     "acc": [R.new(f"aa{i}", [128, w]) for i in range(2)],
                     "bt": [], "at": [None, None], "wt": [None, None], "n": 0, "tok": {}, "f": None}
            dst = [self.msh, self.msc, self.gate[layer]]
            state["f"] = self.fence() if layer else None
            for n, d in enumerate(dst):
                state["bt"].append(self.bc(d[:], I["ada_b"][layer, n * 1024:n * 1024 + 1024], state["f"]))
        total = 3072 // w
        src = I["ada_w"][layer].rearrange("(p k) n -> p k n", k=8)
        for _ in range(total if chunks is None else chunks):
            n = state["n"]
            if n >= total:
                break
            state["n"] += 1
            buf, acc = state["buf"][n % 2], state["acc"][n % 2]
            t = P.dma("sp" if layer == 0 else "act", buf[:], src[:, :, n * w:n * w + w], state["wt"][n % 2],
                      state["f"])
            d = self.ts(acc[:], buf[:, 0, :], self.cc[:, 0:1], None, ALU.mult, None, t, self.ctok,
                        state["at"][n % 2])
            for k in range(1, 8):
                d = self.stt(acc[:], buf[:, k, :], self.cc[:, k:k + 1], acc[:], ALU.mult, ALU.add, d)
            state["wt"][n % 2] = d
            b, fw = self.take("proj")
            m = self.mm(self.ps[:, b[0], 0:w], [(self.ones[:], acc[:])], fw, d, self.base_tok)
            state["at"][n % 2] = m
            which, c0 = n * w // 1024, n * w % 1024
            o = [self.msh, self.msc, self.gate[layer]][which][:, c0:c0 + w]
            z = self.stt(o, self.ps[:, b[0], 0:w], 1.0 if which == 1 else 0.0, o, ALU.add, ALU.add, m,
                         state["bt"][which])
            self.give(b, z)
            state["tok"].setdefault(which, []).append(z)
        return state if state["n"] < total else self._ada_done(state)

    def _ada_done(self, state):
        self.mod_tok = state["tok"]
        return state

    def block1_a(self):
        P, I = self.P, self.I
        R = Kernel.Region(self, self.gen + 40960, self.end, "xin")
        xb = [R.new(f"x{i}", [128, 1024]) for i in range(4)]
        ready = []
        freed = [None] * 4
        for j in range(8):
            x = xb[j % 4]
            t = P.dma("act", x[:], I["x"][0, j * 128:j * 128 + 128, :], freed[j % 4])
            t = self.tt(x[:], x[:], self.msc[:], ALU.mult, t, self.mod_tok[1])
            t = self.tt(x[:], x[:], self.msh[:], ALU.add, t, self.mod_tok[0])
            toks = self.to_T([x[:, k * 128:k * 128 + 128] for k in range(8)], j, [t, self.base_tok], ring="tr4")
            freed[j % 4] = toks
            ready.append(toks)
        halves = [ready[0:4], ready[4:8]]

        f0 = self.fence()
        R = self.region("da")
        qT = R.new("q", [128, 3, 1024])
        kT = R.new("k", [128, 3, 1024])
        v = R.new("v", [128, 9, 384])
        sg = R.new("sg", [128, 8, 384])
        bias = R.new("bias", [128, 6, 320])
        yb = [R.new(f"y{i}", [128, 396]) for i in range(2)]
        sb = [R.new(f"s{i}", [128, 256]) for i in range(3)]
        pt = [R.new(f"p{i}", [128, 256]) for i in range(2)]
        V = Kernel.Region(self, self.gen, self.end, "tp")
        ohs = V.new("oh", [32, 3, 512])
        rb = V.new("rb", [32, 18])
        mk = V.new("mk", [6, 3, 512])
        vv = V.new("vv", [6, 3, 512])
        t1 = P.dma("act", ohs[:], I["k_oh"], f0)
        t2 = P.dma("act", rb[:], I["rel_bias"], f0)
        t3 = P.dma("act", mk[:], I["k_msk"], f0)
        vt = []
        for g in range(3):
            b, fw = self.take("proj")
            m = self.mm(self.ps[0:6, b[0], :], [(rb[:, g * 6:g * 6 + 6], ohs[:, g, :])], fw, t1, t2)
            d = self.stt(vv[:, g, :], self.ps[0:6, b[0], :], 8.0, mk[:, g, :], ALU.mult, ALU.add, m, t3)
            self.give(b, d)
            vt.append(P.dma("act", self.d_v[g], vv[:, g, :], d))
        self.all_dram += vt
        f1 = [f0, vt, vt]
        dv = self.d_v

        def toeplitz(g, off0, w):
            a = dv[g]
            return bass.AP(a.tensor, a.offset + 256 - off0 - w, [[1, 128], [512, 6], [1, w]])

        dils = (1, 4, 8)
        win = I["a_w_in"][0]
        units_end = None
        ytok = []
        y_free = [None, None]
        sb_free, pt_free = [None] * 3, [None] * 2
        stn = 0
        for g in range(3):
            dil = dils[g]
            L = 1024 // dil
            fz = [f1, units_end]
            bt = []
            if g == 0:
                bt.append(P.dma("act", bias[:, :, 0:256], toeplitz(0, -64, 256), fz))
            elif g == 1:
                bt.append(P.dma("act", bias[:, :, 0:320], toeplitz(1, -128, 320), fz))
            else:
                bt.append(P.dma("act", bias[:, :, 0:128], toeplitz(2, 0, 128), fz))

            def cols(c0):
                return lambda k: [(0, win[k * 128:k * 128 + 128, c0:c0 + 384])]

            qk_tok = {}

            def evac_T(dst, name):
                def f(m, hf, b, src, tok):
                    if dil == 1:
                        o, s = dst[:, m, hf * 512:hf * 512 + 512], src
                    else:
                        o = dst[:, m, :].rearrange("p (r i) -> p r i", r=dil)[:, :, hf * (L // 2):(hf + 1) * (L // 2)]
                        s = src.rearrange("p (i r) -> p r i", r=dil)
                    t = (self.copy if name == "q" else self.vcopy)(o, s, tok, fz)
                    self.give(b, t)
                    qk_tok.setdefault((name, m), []).append(t)
                return f

            self.proj_T(8, cols(g * 384), 3, halves, evac_T(qT, "q"))
            self.proj_T(8, cols(1152 + g * 384), 3, halves, evac_T(kT, "k"))

            def rows(t):
                if dil == 1:
                    return lambda a, k: a[:, k, t * 128:t * 128 + 128]
                if dil == 4:
                    r, i0 = t // 2, 128 * (t % 2)
                    return lambda a, k: a[:, k, r + 4 * i0:r + 4 * (i0 + 127) + 1:4]
                return lambda a, k: a[:, k, t:1024:8]

            if g == 0:
                starts = [0, 64, 192, 320, 448, 576, 704, 832, 896]
                vsel = [lambda a, k, s=s: a[:, k, s:s + 128] for s in starts]
            else:
                vsel = [rows(t) for t in range(8)]
            v_tok = [None] * 9

            def evac_v(j, b, src, tok):
                v_tok[j] = self.copy(v[:, j, :], src, tok, fz)
                self.give(b, v_tok[j])

            self.proj_nat(8, cols(2304 + g * 384), 384, vsel, [ready] * 9, evac_v)
            sg_tok = [None] * 8

            def evac_g(j, b, src, tok):
                sg_tok[j] = self.act(sg[:, j, :], src, ACT.Silu, tok, fz)
                self.give(b, sg_tok[j])

            self.proj_nat(8, cols(3456 + g * 384), 384, [rows(t) for t in range(8)], [ready] * 8, evac_g)

            def geometry(j):
                if g == 0:
                    if j == 0:
                        return 0, 192, 64, [(0, 64, 0), (64, 128, 1)]
                    if j == 7:
                        return 832, 192, 0, [(0, 64, 7), (64, 128, 8)]
                    return 128 * j - 64, 256, 0, [(0, 128, j), (128, 128, j + 1)]
                if g == 1:
                    if j % 2 == 0:
                        return 128 * j, 192, 128, [(0, 128, j), (128, 64, j + 1)]
                    return 128 * j - 128, 256, 0, [(0, 128, j - 1), (128, 128, j)]
                return 128 * j, 128, 0, [(0, 128, j)]

            units = [(j, h) for j in range(8) for h in range(6)]
            st = [dict() for _ in units]
            ob = {}

            def s_qk(i):
                j, h = units[i]
                k0, W, _, _ = geometry(j)
                p = slice(64 * (h % 2), 64 * (h % 2) + 64)
                b, fw = self.take("s1")
                st[i]["b"] = b
                st[i]["qk"] = self.mm(self.ps[:, b[0], 0:W],
                                      [(qT[p, h // 2, j * 128:j * 128 + 128], kT[p, h // 2, k0:k0 + W])],
                                      fw, qk_tok["q", h // 2], qk_tok["k", h // 2])

            def s_max(i):
                j, h = units[i]
                _, W, c0, _ = geometry(j)
                b = st[i]["b"]
                y = yb[j % 2]
                s = sb[i % 3]
                n = (256, 320, 128)[g]
                e1 = n - c0 - W
                bv = bias[:, h, n - 1 - c0:e1 - 1 if e1 else None:-1]
                t = P.op("dve", lambda e: e.tensor_tensor_reduce(
                    s[:, 0:W], self.ps[:, b[0], 0:W], bv, -0.125, 3.0e38, ALU.add, ALU.min,
                    y[:, 384 + h:385 + h]), st[i]["qk"], bt, sb_free[i % 3], y_free[j % 2], fz)
                self.give(b, t)
                st[i]["e"] = self.act(s[:, 0:W], s[:, 0:W], ACT.Exp, t, scale=-1.0,
                                      bias=y[:, 384 + h:385 + h], accum_out=y[:, 390 + h:391 + h])

            def s_tr(i):
                j, h = units[i]
                _, W, _, ch = geometry(j)
                b, fw = self.take("t1")
                for n, (c, w, _) in enumerate(ch):
                    t = self.tr(self.ps[0:w, b[0], n * 128:n * 128 + 128], sb[i % 3][:, c:c + w], fw, st[i]["e"],
                                mark=(n == len(ch) - 1))
                sb_free[i % 3] = t
                cp = self.vcopy if i % 2 else self.copy
                rows_ = [w for _, w, _ in ch]
                if min(rows_) == 128 or len(rows_) == 1:
                    x = cp(pt[i % 2][:, 0:128 * len(ch)], self.ps[:, b[0], 0:128 * len(ch)], t, pt_free[i % 2], fz)
                else:
                    for n, w in enumerate(rows_):
                        x = cp(pt[i % 2][0:w, n * 128:n * 128 + 128], self.ps[0:w, b[0], n * 128:n * 128 + 128], t,
                               pt_free[i % 2], fz)
                self.give(b, x)
                st[i]["pt"] = x

            def s_pv(i):
                j, h = units[i]
                _, _, _, ch = geometry(j)
                if h == 0:
                    ob[j] = self.take("o1")
                b, fw = ob[j]
                t = self.mm(self.ps[:, b[0], h * 64:h * 64 + 64],
                            [(pt[i % 2][0:w, n * 128:n * 128 + 128], v[0:w, vt_, h * 64:h * 64 + 64], v_tok[vt_])
                             for n, (_, w, vt_) in enumerate(ch)], fw, st[i]["pt"])
                pt_free[i % 2] = t
                if h == 5:
                    y = yb[j % 2]
                    d = self.tt(y[:, 0:384], self.ps[:, b[0], 0:384], sg[:, j, :], ALU.mult, t, sg_tok[j])
                    self.give(b, d)
                    if dil == 1:
                        dst = self.d_y[j * 128:j * 128 + 128, g, :]
                    elif dil == 4:
                        r, i0 = j // 2, 128 * (j % 2)
                        dst = self.d_y.rearrange("(i r) g n -> r i g n", r=4)[r, i0:i0 + 128, g, :]
                    else:
                        dst = self.d_y.rearrange("(i r) g n -> r i g n", r=8)[j, :, g, :]
                    w = P.dma("act", dst, y[:], d, st[i]["e"])
                    y_free[j % 2] = w
                    ytok.append(w)
                    st[i]["end"] = d

            n = len(units)
            for i in range(n + 4):
                if i < n:
                    s_qk(i)
                    s_max(i)
                if 2 <= i < n + 2:
                    s_tr(i - 2)
                if 3 <= i < n + 3:
                    s_pv(i - 3)
            units_end = [st[n - 1]["end"], self.fence()]
        self.all_dram += ytok

        f2 = self.fence()
        R = self.region("mix")
        z = self.z = R.new("z", [128, 8, 1024])
        G = Kernel.Region(self, self.gen, self.gen + 32768, "gt")
        yr = [G.new(f"yr{i}", [128, 1188]) for i in range(3)]
        sa = G.new("sa", [128, 8, 3, 12])
        sl = G.new("sl", [128, 8, 3, 6])
        se = G.new("se", [128, 8, 3, 6])
        s1 = G.new("s1", [128, 8, 6])
        fac = R.new("fac", [128, 8, 3, 6])
        st_ = [P.dma("act", sa[:, :, g, :], self.d_y[:, g, 384:396].rearrange("(j p) n -> p j n", p=128), f2, ytok)
               for g in range(3)]
        t = self.act(sl[:], sa[:, :, :, 6:12], ACT.Ln, st_)
        t = self.tt(sl[:], sl[:], sa[:, :, :, 0:6], ALU.subtract, t, st_)
        t = self.tt(s1[:], sl[:, :, 0, :], sl[:, :, 1, :], ALU.max, t)
        t = self.tt(s1[:], s1[:], sl[:, :, 2, :], ALU.max, t)
        t = self.tt(sl[:], sl[:], s1[:].unsqueeze(2).to_broadcast([128, 8, 3, 6]), ALU.subtract, t)
        te = self.act(se[:], sl[:], ACT.Exp, t)
        t = self.tt(s1[:], se[:, :, 0, :], se[:, :, 1, :], ALU.add, te)
        t = self.tt(s1[:], s1[:], se[:, :, 2, :], ALU.add, t)
        t = self.tt(sl[:], sa[:, :, :, 6:12], s1[:].unsqueeze(2).to_broadcast([128, 8, 3, 6]), ALU.mult, t)
        t = self.rec(sl[:], sl[:], t)
        tf = self.tt(fac[:], se[:], sl[:], ALU.mult, t)
        fr = [None] * 3
        yT = []
        for j in range(8):
            y = yr[j % 3]
            t = P.dma("act", y[:], self.d_y[j * 128:j * 128 + 128].rearrange("p g n -> p (g n)"), f2, ytok, fr[j % 3])
            y4 = y[:].rearrange("p (g n) -> p g n", g=3)[:, :, 0:384].rearrange("p g (h e) -> p g h e", h=6)
            for g in range(3):
                d = self.tt(y4[:, g], y4[:, g], fac[:, j, g, :].unsqueeze(2).to_broadcast([128, 6, 64]), ALU.mult,
                            t, tf)
            tk = self.to_T([y[:, (q // 3) * 396 + (q % 3) * 128:(q // 3) * 396 + (q % 3) * 128 + 128]
                            for q in range(9)], j, d, ring="tr4")
            fr[j % 3] = tk
            yT.append(tk)

        f3 = self.fence()
        lg = R.new("lg", [128, 1024])
        lb = R.new("lb", [128, 1024])
        xr = [R.new(f"xr{i}", [128, 512]) for i in range(2)]
        tg = [self.bc(lg[:], I["ln_g"][0], f3), self.bc(lb[:], I["ln_b"][0], f3)]
        A2 = Kernel.Region(self, R.off, self.end, "ad2")
        self.ada_state = None
        xf = [None, None]
        wo = I["a_w_out"][0]
        ut = []
        cnt = [0]

        def evac(half):
            def f(j, b, src, tok):
                c = slice(half * 512, half * 512 + 512)
                x = cnt[0] % 2
                cnt[0] += 1
                t = P.dma("act", xr[x][:], I["x"][0, j * 128:j * 128 + 128, c], f3, xf[x])
                d = self.tt(z[:, j, c], src, self.gate[0][:, c], ALU.mult, tok, f3, self.mod0)
                self.give(b, d)
                d = self.stt(z[:, j, c], xr[x][:], ALPHA, z[:, j, c], ALU.mult, ALU.add, d, t)
                xf[x] = d
                if half == 1:
                    self.ln_rows(j, d, lg, lb, tg, 0, ut)
                elif j >= 0:
                    self.ada_state = self.ada(1, A2, 128, 3, self.ada_state)
            return f

        self.mod0 = self.mod_tok[2]
        sels = [lambda a, k, j=j: a[:, k, j * 128:j * 128 + 128] for j in range(8)]
        self.sels = sels
        for half in range(2):
            self.proj_nat(9, lambda k: [(0, wo[k * 128:k * 128 + 128, half * 512:half * 512 + 512])], 512, sels, yT,
                          evac(half))
        self.uT = ut

    def ln_rows(self, j, tok, lg, lb, tg, nx, ut):
        P = self.P
        z = self.z[:, j, :]
        st = self.small(12)
        mv = self.small(2)
        a = P.op("dve", lambda e: e.bn_stats(st[:, 0:6], z[:, 0:512]), tok)
        b = P.op("dve", lambda e: e.bn_stats(st[:, 6:12], z[:, 512:1024]), tok)
        t = P.op("dve", lambda e: e.bn_aggr(mv, st), a, b)
        sd, r = self.small(1), self.small(1)
        s = self.act(sd, mv[:, 1:2], ACT.Sqrt, t, bias=self.eps[1e-5])
        s = self.rec(r, sd, s)
        t = self.ts(z, z, mv[:, 0:1], r, ALU.subtract, ALU.mult, s)
        t = self.tt(z, z, lg[:], ALU.mult, t, tg)
        t = self.tt(z, z, lb[:], ALU.add, t)
        w = P.dma("act", self.d_x[nx][j], z, t)
        self.all_dram.append(w)
        self.d_tok[nx][j] = w
        if nx == 0:
            t = self.tt(z, z, self.msc[:], ALU.mult, t, w, self.mod_tok[1])
            t = self.tt(z, z, self.msh[:], ALU.add, t, self.mod_tok[0])
            ut.append(self.to_T([z[:, k * 128:k * 128 + 128] for k in range(8)], j, t, ring="tr4"))
        else:
            self.pre_rows(j, t, w, ut)

    def pre_rows(self, j, tok, stored, ut):
        z = self.z[:, j, :]
        ss = self.small(1)
        t = self.act(self.junk[:], z, ACT.Square, tok, accum_out=ss)
        r, t = self.rms_scale(ss, 1024, 1e-6, t)
        t = self.stt(z, z, r, self.gpre[0][:], ALU.mult, ALU.mult, t, stored, self.gpre[1])
        ut.append(self.to_T([z[:, k * 128:k * 128 + 128] for k in range(8)], j, t, ring="tr4"))

    def rotate(self, x1, x2, co, si, tmp, tok):
        a = self.tt(tmp[0], x1, si, ALU.mult, tok, self.rot_tok)
        b = self.tt(tmp[1], x2, si, ALU.mult, tok)
        c = self.tt(x1, x1, co, ALU.mult, a)
        d = self.tt(x2, x2, co, ALU.mult, b)
        c = self.tt(x1, x1, tmp[1], ALU.subtract, c, b)
        d = self.tt(x2, x2, tmp[0], ALU.add, d, a)
        self.rot_tok = [c, d]
        return [c, d]

    def block1_b(self):
        P, I = self.P, self.I
        f0 = self.fence()
        R = self.region("mla")
        cqh, cql = R.new("cqh", [128, 2, 1024], F32R), R.new("cql", [128, 2, 1024], F32R)
        ckh, ckl = R.new("ckh", [128, 1, 1024], F32R), R.new("ckl", [128, 1, 1024], F32R)
        kT = [R.new(f"kT{i}", [128, 1024]) for i in range(2)]
        B = R.off
        v = [R.new(f"v{i}", [128, 8, 128]) for i in range(2)]
        qT = [R.new(f"qT{i}", [128, 1024]) for i in range(2)]
        pp = [R.new(f"p{i}", [128, 1024]) for i in range(2)]
        pt = [R.new(f"t{i}", [128, 1024]) for i in range(2)]
        T = Kernel.Region(self, B, self.end, "ml0")
        g0 = T.new("g0", [128, 8, 512])
        cn = [T.new(f"cn{i}", [128, 512]) for i in range(3)]
        tmp = T.new("tmp", [128, 4, 16])
        jk = T.new("jk", [128, 256])
        qg = T.new("qg", [128, 256])
        kg = T.new("kg", [128, 128])
        tg = [self.bc(qg[:], I["b_q_norm"][0], f0), self.bc(kg[:], I["b_kv_norm"][0], f0)]
        qtab = self.msh
        tq = P.dma("act", qtab[:], I["k_qtab"], f0)
        win = I["b_w_in"][0]
        ready = self.uT
        cfree = [None] * 3
        lat = {"q": [], "c": [], "r": []}

        def evac_c(j, b, src, tok):
            x = cn[j % 3]
            js = slice(j * 128, j * 128 + 128)
            t = self.copy(x[:, 0:416], src, tok, cfree[j % 3], f0)
            self.give(b, t)
            s1, s2 = self.small(1), self.small(1)
            a1 = self.act(jk[:, 0:256], x[:, 0:256], ACT.Square, t, accum_out=s1)
            a2 = self.act(jk[:, 0:128], x[:, 256:384], ACT.Square, t, a1, accum_out=s2)
            r1, t1 = self.rms_scale(s1, 256, 1e-6, a1)
            r2, t2 = self.rms_scale(s2, 128, 1e-6, a2)
            t1 = self.stt(x[:, 0:256], x[:, 0:256], r1, qg[:], ALU.mult, ALU.mult, t1, tg)
            t2 = self.stt(x[:, 256:384], x[:, 256:384], r2, kg[:], ALU.mult, ALU.mult, t2, tg)
            ro = self.rotate(x[:, 384:400], x[:, 400:416], self.rope[:, j, 0, :], self.rope[:, j, 1, :],
                             [tmp[:, i, :] for i in range(4)], [t, self.base_tok])
            t3 = self.vcopy(x[:, 416:448], x[:, 384:416], ro)
            z = self.zero(x[:, 448:512], t)
            bb, fw = self.take("tr4")
            for i in range(3):
                m = self.tr(self.ps[:, bb[0], i * 128:i * 128 + 128], x[:, i * 128:i * 128 + 128], fw, t1, t2,
                            mark=False)
            m = P.op("pe", lambda e: e.transpose(self.ps[:, bb[0], 384:512], x[:, 320:448], self.ident[:]), t3, z)
            cfree[j % 3] = m
            p = self.ps
            pq = p[:, bb[0], 0:256].rearrange("p (a b) -> p a b", a=2)
            pk = p[:, bb[0], 256:384]
            k1 = self.copy(kT[0][64:128, js], p[64:128, bb[0], 384:512], m, f0)
            k2 = self.copy(kT[1][64:128, js], p[64:128, bb[0], 384:512])
            a1 = self.copy(cqh[:, :, js], pq)
            a2 = self.copy(ckh[:, 0, js], pk)
            d1 = self.tt(cql[:, :, js], pq, cqh[:, :, js].bitcast(F32), ALU.subtract, a1, a2)
            d2 = self.tt(ckl[:, 0, js], pk, ckh[:, 0, js].bitcast(F32), ALU.subtract, a2)
            q1, q2 = [a1, d1], [a2, d2]
            self.give(bb, k1, k2, q1, q2)
            lat["q"].append(q1)
            lat["c"].append(q2)
            lat["r"].append([k1, k2])

        self.proj_nat(8, lambda k: [(0, win[k * 128:k * 128 + 128, 0:416])], 416, self.sels, ready, evac_c)
        gt = [[], []]

        def evac_g(half):
            def f(j, b, src, tok):
                js = slice(j * 128, j * 128 + 128)
                if half == 0:
                    o = g0[:, j, :].rearrange("p (a b) -> p a b", a=4)
                else:
                    o = self.tfi[:, 0:4, js]
                t = self.act(o, src.rearrange("p (a b) -> p a b", a=4), ACT.Silu, tok, f0)
                self.give(b, t)
                gt[half].append(t)
                if half == 1:
                    gt[0][j] = self.P.dma("act", self.tfl[:, 0:4, js], g0[:, j, :].rearrange("p (a b) -> p a b", a=4),
                                          gt[0][j], tok)
            return f

        for half in range(2):
            c0 = 416 + 512 * half
            self.proj_nat(8, lambda k: [(0, win[k * 128:k * 128 + 128, c0:c0 + 512])], 512, self.sels, ready,
                          evac_g(half))

        f1 = [self.fence()]
        uq = I["b_w_uq"][0]
        ukv = I["b_w_ukv"][0]
        scale = 96.0 ** -0.5
        hs = [None] * 16
        vst = [None] * 8
        kfree, qfree, vfree = [None, None], [None, None], [None, None]
        pfree, tfree = [None, None], [None, None]
        lq = [lat["q"][0:4], lat["q"][4:8]]
        lc = [lat["c"][0:4], lat["c"][4:8]]

        def head(h):
            pc = []
            for k in range(2):
                r = uq[k * 128:k * 128 + 128, h * 96:h * 96 + 96]
                pc += [(k * 128, r), (k * 128 + 96, r[:, 80:96]), (k * 128 + 112, r[:, 64:80])]
            pc.append((256, ukv[:, h * 128:h * 128 + 128]))
            if h % 2 == 0:
                pc.append((384, ukv[:, h * 128 + 64:h * 128 + 128]))
                pc.append((448, ukv[:, h * 128 + 192:h * 128 + 256]))
            w = self.weight(pc)
            _, s, wt = w
            toks = []
            for hf in range(2):
                r = slice(hf * 512, hf * 512 + 512)
                b, fw = self.take("o2")
                terms = []
                for k in range(2):
                    c = slice(k * 128, k * 128 + 128)
                    terms += [(self.whi[:, s, c], cqh[:, k, r], wt), (self.whi[:, s, c], cql[:, k, r]),
                              (self.wlo[:, s, c], cqh[:, k, r])]
                m = self.mm(self.ps[:, b[0], :], terms, fw, lq[hf])
                t = self.tt(qT[h % 2][:, r], self.ps[:, b[0], :], qtab[:, r], ALU.mult, m, tq, qfree[h % 2], f1)
                self.give(b, t)
                toks.append(t)
                b, fw = self.take("o2")
                c = slice(256, 384)
                m = self.mm(self.ps[:, b[0], :], [(self.whi[:, s, c], ckh[:, 0, r], wt), (self.whi[:, s, c], ckl[:, 0, r]),
                                                  (self.wlo[:, s, c], ckh[:, 0, r])], fw, lc[hf])
                t = self.copy(kT[h % 2][0:64, r], self.ps[0:64, b[0], :], m, kfree[h % 2], f0)
                self.give(b, t)
                toks.append(t)
            hs[h] = [toks, lat["r"]]
            if h % 2 == 0:
                vt = []
                c = slice(384, 512)
                for q in range(2):
                    b, fw = self.take("o2")
                    for i in range(4):
                        j = 4 * q + i
                        js = slice(j * 128, j * 128 + 128)
                        m = self.mm(self.ps[:, b[0], i * 128:i * 128 + 128],
                                    [(ckh[:, 0, js], self.whi[:, s, c], wt), (ckh[:, 0, js], self.wlo[:, s, c]),
                                     (ckl[:, 0, js], self.whi[:, s, c])], fw, lat["c"][j])
                    t = self.copy(v[h // 2 % 2][:, 4 * q:4 * q + 4, :],
                                  self.ps[:, b[0], :].rearrange("p (a b) -> p a b", a=4), m, vfree[h // 2 % 2], f1)
                    self.give(b, t)
                    vt.append(t)
                vst[h // 2] = vt
            self.release([w], m)

        units = [(h, j) for h in range(16) for j in range(8)]
        st = [dict() for _ in units]
        ytok = [[] for _ in range(8)]

        def s_qk(i):
            h, j = units[i]
            if j == 0 and h == 0:
                head(0)
            if j == 4 and h + 1 < 16:
                head(h + 1)
            b, fw = self.take("s2")
            for c in range(2):
                r = slice(c * 512, c * 512 + 512)
                t = self.mm(self.ps[:, b[c], :], [(qT[h % 2][:, j * 128:j * 128 + 128], kT[h % 2][:, r])], fw, hs[h])
            kfree[h % 2] = qfree[h % 2] = t
            st[i]["b"] = b
            sv = ps2(b)
            st[i]["m"] = m = self.small(4)
            t = self.red(m[:, 0:1], sv, ALU.max, t)
            t = self.ts(m[:, 1:2], m[:, 0:1], -scale, None, ALU.mult, None, t)
            t = self.act(pp[i % 2][:], sv, ACT.Exp, t, pfree[i % 2], f1, scale=scale, bias=m[:, 1:2],
                         accum_out=m[:, 2:3])
            self.give(b, t)
            st[i]["e"] = t
            st[i]["r"] = self.rec(m[:, 3:4], m[:, 2:3], t)

        def ps2(b):
            return self.ps[:, b[0]:b[0] + 2, :].rearrange("p a b -> p (a b)")

        def s_tr(i):
            b, fw = self.take("t2")
            for k in range(8):
                t = self.tr(self.ps[:, b[k // 4], k % 4 * 128:k % 4 * 128 + 128], pp[i % 2][:, k * 128:k * 128 + 128],
                            fw, st[i]["e"], mark=(k % 4 == 3))
                if k == 3:
                    x1 = self.copy(pt[i % 2][:, 0:512], self.ps[:, b[0], :], t, tfree[i % 2], f1)
            x2 = self.vcopy(pt[i % 2][:, 512:1024], self.ps[:, b[1], :], t, tfree[i % 2], f1)
            pfree[i % 2] = t
            self.free[b[0]], self.free[b[1]] = [x1], [x2]
            st[i]["pt"] = [x1, x2]

        def s_pv(i):
            h, j = units[i]
            b, fw = self.take("o2")
            o = self.ps[:, b[0], 0:64]
            t = self.mm(o, [(pt[i % 2][:, k * 128:k * 128 + 128], v[h // 2 % 2][:, k, h % 2 * 64:h % 2 * 64 + 64])
                            for k in range(8)], fw, st[i]["pt"], vst[h // 2])
            tfree[i % 2] = t
            vfree[h // 2 % 2] = t
            kt = h // 2
            y = (self.tfl if kt < 4 else self.tfi)[:, kt % 4, j * 128 + h % 2 * 64:j * 128 + h % 2 * 64 + 64]
            d = self.stt(y, o, st[i]["m"][:, 3:4], y, ALU.mult, ALU.mult, t, st[i]["r"], gt[0][j], gt[1][j])
            self.give(b, d)
            ytok[j].append(d)

        n = len(units)
        for i in range(n + 3):
            if i < n:
                s_qk(i)
            if 1 <= i < n + 1:
                s_tr(i - 1)
            if 2 <= i < n + 2:
                s_pv(i - 2)

        yT = []
        for j in range(8):
            js = slice(j * 128, j * 128 + 128)
            blocks = [(self.tfl if k < 4 else self.tfi)[:, k % 4, js] for k in range(8)]
            yT.append(self.to_T(blocks, j, ytok[j], ring="tr4"))

        f2 = self.fence()
        R = self.region("mlo")
        z = self.z = R.new("z", [128, 8, 1024])
        lg, lb = R.new("lg", [128, 1024]), R.new("lb", [128, 1024])
        xr = [R.new(f"xr{i}", [128, 512]) for i in range(2)]
        self.junk = R.new("junk", [128, 1024])
        gp = R.new("gp", [128, 1024])
        self.gpre = (gp, self.bc(gp[:], I["norm_mix_pre_2"][0], f2))
        tg = [self.bc(lg[:], I["ln_g"][1], f2), self.bc(lb[:], I["ln_b"][1], f2)]
        wo = I["b_w_out"][0]
        xf = [None, None]
        cnt = [0]
        ut = []

        def evac(half):
            def f(j, b, src, tok):
                c = slice(half * 512, half * 512 + 512)
                x = cnt[0] % 2
                cnt[0] += 1
                t = P.dma("act", xr[x][:], self.d_x[0][j][:, c], f2, xf[x], self.d_tok[0][j])
                d = self.tt(z[:, j, c], src, self.gate[1][:, c], ALU.mult, tok, f2, self.mod_tok[2])
                self.give(b, d)
                d = self.stt(z[:, j, c], xr[x][:], ALPHA, z[:, j, c], ALU.mult, ALU.add, d, t)
                xf[x] = d
                if half == 1:
                    self.ln_rows(j, d, lg, lb, tg, 1, ut)
            return f

        for half in range(2):
            self.proj_nat(8, lambda k: [(0, wo[k * 128:k * 128 + 128, half * 512:half * 512 + 512])], 512, self.sels,
                          yT, evac(half))
        self.uT = ut

    def block2_mix(self, l):
        P, I = self.P, self.I
        f0 = self.fence()
        p = self.ps
        R = self.region(f"c{l}", mod=True)
        qT, kT = R.new("q", [128, 4, 1024]), R.new("k", [128, 4, 1024])
        v = R.new("v", [128, 8, 512])
        C0 = R.off
        rn = R.new("rn", [128, 8, 512])
        gr = R.new("gr", [128, 8, 256])
        pu = R.new("pu", [128, 2, 1040])
        nt = [self.tfi[:, 8, 0:512], self.tfi[:, 8, 512:1024], self.tfl[:, 8, 0:512]]
        tmp = self.tfl[:, 8, 512:1024].rearrange("p (a b) -> p a b", a=4)
        win = I["w_in_2"][l]
        nfree = [None] * 3
        ready = self.uT
        halves = [ready[0:4], ready[4:8]]
        tl = self.lam(l, f0)
        f0 = self.fence()
        n = [0]
        qk_tok = {"q": [], "k": []}

        def cols(c0, w=512):
            return lambda k: [(0, win[k * 128:k * 128 + 128, c0:c0 + w])]

        def evac_qk(dst, name):
            def f(j, b, src, tok):
                i = n[0] % 3
                n[0] += 1
                x = nt[i]
                js = slice(j * 128, j * 128 + 128)
                t = self.copy(x, src, tok, nfree[i], f0)
                self.give(b, t)
                xv = x.rearrange("p (m e) -> p m e", e=64)
                co = self.rope2[:, j, 0:1, :].to_broadcast([128, 8, 8])
                si = self.rope2[:, j, 1:2, :].to_broadcast([128, 8, 8])
                tv = [tmp[:, a, 0:64].rearrange("p (m e) -> p m e", e=8) for a in range(4)]
                t = self.rotate(xv[:, :, 0:8], xv[:, :, 8:16], co, si, tv, [t, f0])
                b, fw = self.take("tr4")
                for h in range(4):
                    m = self.tr(p[:, b[0], h * 128:h * 128 + 128], x[:, h * 128:h * 128 + 128], fw, t, mark=(h == 3))
                nfree[i] = m
                t = self.copy(dst[:, :, js], p[:, b[0], :].rearrange("p (a b) -> p a b", a=4), m, f0)
                self.give(b, t)
                qk_tok[name].append(t)
            return f

        self.proj_nat(8, cols(0), 512, self.sels, ready, evac_qk(qT, "q"))
        self.proj_nat(8, cols(512), 512, self.sels, ready, evac_qk(kT, "k"))
        v_tok, r_tok, g_tok = [], [], []

        def evac_v(j, b, src, tok):
            t = self.copy(v[:, j, :], src, tok, f0)
            self.give(b, t)
            v_tok.append(t)

        self.proj_nat(8, cols(1024), 512, self.sels, ready, evac_v)

        def evac_r(j, b, src, tok):
            t = self.copy(rn[:, j, :], src, tok, f0)
            self.give(b, t)
            xv = rn[:, j, 0:256].rearrange("p (m e) -> p m e", e=32)
            co = self.rope[:, j, 0:1, :].to_broadcast([128, 8, 16])
            si = self.rope[:, j, 1:2, :].to_broadcast([128, 8, 16])
            tv = [tmp[:, a, :].rearrange("p (m e) -> p m e", e=16) for a in range(4)]
            r_tok.append([t, self.rotate(xv[:, :, 0:16], xv[:, :, 16:32], co, si, tv, [t, f0])])

        self.proj_nat(8, cols(1536), 512, self.sels, ready, evac_r)

        def evac_g(j, b, src, tok):
            t = self.act(gr[:, j, :], src, ACT.Silu, tok, f0)
            self.give(b, t)
            g_tok.append(t)

        self.proj_nat(8, cols(2048, 256), 256, self.sels, ready, evac_g)
        pu_tok = [self.zero(pu[:, :, 0:16], f0)]

        def evac_p(m, hf, b, src, tok):
            t = self.copy(pu[:, m, 16 + hf * 512:16 + hf * 512 + 512], src, tok, f0)
            self.give(b, t)
            pu_tok.append(t)

        self.proj_T(8, cols(2304, 256), 2, halves, evac_p)

        f1 = self.fence()
        S = Kernel.Region(self, self.tf_off(), self.tf_off() + 16384, f"r{l}")
        dec = S.new("dec", [128, 512])
        xi, ze, blk, cd = S.new("xi", [128, 128]), S.new("ze", [128, 128]), S.new("blk", [128, 256]), S.new("cd", [128, 8])
        inv = S.new("inv", [128, 2, 17])
        rg = S.new("rg", [128, 256])
        pw = S.new("pw", [128, 2, 128])
        psc = S.new("psc", [128, 8])
        tc = [P.dma("sp", a, I[b], f1) for a, b in (
            (dec[:], "k_decay2"), (xi[:], "k_xi"), (ze[:], "k_zeta"), (blk[:], "k_blk"), (cd[:, 0:1], "k_cd"),
            (inv[:], "k_inv"))]
        tc.append(self.bc(rg[:], I["ret_norm_2"][l], f1, e="sp"))
        tz = self.zero(pw[:], f1)
        tp = []
        for g in range(4):
            q = 64 * (g % 2)
            tp.append(P.dma("sp", pw[q:q + 64, g // 2, q:q + 64], I["pool_w_2"][l, g], tz))
        for t in range(2):
            tp.append(P.dma("sp", psc[:, t:t + 1], I["pool_scale_2"][l, t * 128:t * 128 + 128].rearrange("(p o) -> p o", o=1), f1))
        kt_ = [S.new(f"kt{i}", [128, 128]) for i in range(2)]
        qx = [S.new(f"qx{i}", [128, 128]) for i in range(2)]
        kz = [S.new(f"kz{i}", [128, 128]) for i in range(2)]
        um = S.new("um", [128, 256])
        state = [S.new(f"st{i}", [128, 256]) for i in range(2)]
        S2 = Kernel.Region(self, self.t_lo_off, self.t_lo_off + 16384, f"s{l}")
        qb = [S2.new(f"qb{i}", [128, 512]) for i in range(2)]
        it = [S2.new(f"it{i}", [128, 512]) for i in range(2)]
        on = S2.new("on", [128, 8, 256])
        zq = [self.zero(q[:], f1) for q in qb]
        zs = self.zero(state[0][:], f1)

        st_tok = zs
        it_free, qb_free, x_free = [None, None], [None, None], [None, None]
        o_tok = []
        for i in range(8):
            a = i % 2
            b, fw = self.take("tr4")
            m = self.tr(p[:, b[0], 0:128], rn[:, i, 0:128], fw, r_tok[i], mark=False)
            m = self.tr(p[:, b[0], 128:256], rn[:, i, 128:256])
            t1 = self.copy(kt_[a][:], p[:, b[0], 128:256], m, x_free[a], f1)
            tq = []
            for h in range(4):
                hp = slice(32 * h, 32 * h + 32)
                tq.append(self.copy(qb[a][hp, h * 128:h * 128 + 128], p[hp, b[0], 0:128], m, zq[a], qb_free[a]))
            t2 = self.tt(qx[a][:], p[:, b[0], 0:128], xi[:], ALU.mult, m, tq, tc, x_free[a], f1)
            self.give(b, t1, tq, t2)
            t3 = self.tt(kz[a][:], rn[:, i, 128:256], ze[:], ALU.mult, r_tok[i], tc, x_free[a], f1)
            b, fw = self.take("proj")
            m = self.mm(p[:, b[0], :], [(kt_[a][:], qb[a][:])], fw, t1, tq)
            qb_free[a] = m
            t4 = self.tt(it[a][:], p[:, b[0], :], dec[:], ALU.mult, m, tc, it_free[a], f1)
            self.give(b, t4)
            b, fw = self.take("proj")
            cross = P.op("pe", lambda e, b=b, a=a, s=state[i % 2]: e.matmul(
                p[:, b[0], 0:256], qx[a][:], s[:], start=True, stop=False, skip_group_check=True),
                fw, t2, st_tok, mark=True)
            for h in range(4):
                m = P.op("pe", lambda e, b=b, a=a, h=h, i=i: e.matmul(
                    p[:, b[0], h * 64:h * 64 + 64], it[a][:, h * 128:h * 128 + 128], rn[:, i, 256 + h * 64:320 + h * 64],
                    start=False, stop=(h == 3), skip_group_check=True), t4, r_tok[i], mark=(h == 3))
            it_free[a] = m
            t = self.copy(on[:, i, :], p[:, b[0], 0:256], m, f1)
            self.give(b, t)
            o_tok.append(t)
            if i < 7:
                b, fw = self.take("proj")
                m = self.mm(p[:, b[0], 0:256], [(kz[a][:], rn[:, i, 256:512])], fw, t3)
                x_free[a] = [m, cross]
                t = self.tt(um[:], p[:, b[0], 0:256], blk[:], ALU.mult, m, tc, st_tok)
                self.give(b, t)
                st_tok = self.stt(state[1 - a][:], state[a][:], cd[:, 0:1], um[:], ALU.mult, ALU.add, t, st_tok, zs,
                                  cross)
        f2 = self.fence()
        S3 = Kernel.Region(self, self.t_lo_off, self.t_lo_off + 8192, f"n{l}")
        sq = S3.new("sq", [128, 8, 256])
        mu, va, sd = self.small(32), self.small(32), self.small(32)
        o3 = on[:].rearrange("p j (h e) -> p (j h) e", h=4)
        q3 = sq[:].rearrange("p j (h e) -> p (j h) e", h=4)
        t = self.red(mu, o3, ALU.add, o_tok)
        t = self.ts(mu, mu, 1.0 / 64, None, ALU.mult, None, t)
        t = self.tt(o3, o3, mu.unsqueeze(2).to_broadcast([128, 32, 64]), ALU.subtract, t)
        t2 = self.tt(q3, o3, o3, ALU.mult, t, f2)
        t2 = self.red(va, q3, ALU.add, t2)
        t2 = self.act(sd, va, ACT.Sqrt, t2, scale=1.0 / 64, bias=self.eps[1e-6])
        t2 = self.rec(va, sd, t2)
        t = self.tt(o3, o3, va.unsqueeze(2).to_broadcast([128, 32, 64]), ALU.mult, t2)
        t = self.tt(on[:], on[:], rg[:].unsqueeze(1).to_broadcast([128, 8, 256]), ALU.mult, t, tc)
        t = self.tt(on[:], on[:], gr[:], ALU.mult, t, g_tok)
        mix = [[] for _ in range(8)]
        for j in range(8):
            mix[j] += self.to_T([on[:, j, 0:128], on[:, j, 128:256]], j, t, kt0=4)
        Q = Kernel.Region(self, self.t_lo_off + 4 * 4096 * 0, self.t_lo_off + 16384, f"q{l}")
        f3 = self.fence()
        wa = Q.new("wa", [128, 1040])
        wb = Q.new("wb", [128, 1040])
        pl = Q.new("pl", [128, 1024])
        tw = [self.zero(wa[:, 0:16], f3), self.zero(wb[:, 0:16], f3)]
        pm_tok = [None, None]
        t = [tw, pu_tok]
        lastp = None
        for m_ in range(2):
            u = pu[:, m_, :]
            a = self.tt(wa[:, 16:1040], u[:, 16:1040], u[:, 15:1039], ALU.add, t, lastp, f3)
            if m_ == 0:
                b2 = self.tt(wb[64:128, 16:1040], wa[64:128, 16:1040], wa[64:128, 14:1038], ALU.add, a, tw)
                b1 = self.vcopy(wb[0:64, 16:1040], wa[0:64, 16:1040], a, tw)
                w, wt = wb, [b1, b2]
            else:
                b1 = self.tt(wb[:, 16:1040], wa[:, 16:1040], wa[:, 14:1038], ALU.add, a, tw)
                a = self.tt(wa[:, 16:1040], wb[:, 16:1040], wb[:, 12:1036], ALU.add, b1)
                b2 = self.tt(wb[64:128, 16:1040], wa[64:128, 16:1040], wa[64:128, 8:1032], ALU.add, a)
                b1 = self.vcopy(wb[0:64, 16:1040], wa[0:64, 16:1040], a)
                w, wt = wb, [b1, b2]
            t1 = self.stt(pl[:, 16:1024], w[:, 32:1040], inv[:, m_, 16:17], u[:, 32:1040], ALU.mult, ALU.subtract, wt, tc,
                          lastp, f3)
            t2 = self.tt(pl[:, 0:16], w[:, 16:32], inv[:, m_, 0:16], ALU.mult, wt, tc, lastp, f3)
            t2 = self.tt(pl[:, 0:16], pl[:, 0:16], u[:, 16:32], ALU.subtract, t2)
            for hf in range(2):
                r = slice(hf * 512, hf * 512 + 512)
                b, fw = self.take("proj")
                mm_ = self.mm(p[:, b[0], :], [(pw[:, m_, :], pl[:, r])], fw, t1, t2, tp)
                s = self.act(self.thi[:, 6 + m_, r], p[:, b[0], :], ACT.Copy, mm_, tp, scale=psc[:, m_:m_ + 1])
                d = self.stt(self.tlo[:, 6 + m_, r], p[:, b[0], :], psc[:, m_:m_ + 1], self.thi[:, 6 + m_, r].bitcast(F32), ALU.mult,
                             ALU.subtract, s, tp)
                self.give(b, d)
                for j in range(4):
                    mix[4 * hf + j] += [s, d]
                lastp = mm_

        f4 = self.fence()
        A = Kernel.Region(self, C0, self.end, f"a{l}")
        pr = [[A.new(f"p{i}{m}", [128, 1024]) for m in range(2)] for i in range(2)]
        aT = [A.new(f"t{i}", [128, 1024]) for i in range(1)]
        ob = self.tfi[:, 0:4, :].rearrange("p a (j e) -> p j a e", e=128)
        sgm = [self.tfl[:, 8, 0:128]]
        ssq = self.tfl[:, 8, 128:160].rearrange("p (j h) -> p j h", h=4)
        rr = self.tfl[:, 8, 192:224].rearrange("p (j h) -> p j h", h=4)
        jk = self.tfl[:, 8, 256:384]
        lam_init = 0.8 - 0.6 * math.exp(-0.3 * l)
        ts_ = self.bc(sgm[0], I["diff_subln_2"][l], f4, e="sp")
        ts_ = self.ts(sgm[0], sgm[0], 1.0 - lam_init, None, ALU.mult, None, ts_)
        units = [(h, j) for h in range(4) for j in range(8)]
        st = [dict() for _ in units]
        pfree, tfree = [None, None], [None, None]
        scale = 64.0 ** -0.5
        otok = [[] for _ in range(8)]

        def wide(b, W):
            return p[:, b[0]:b[0] + 2, :].rearrange("p a b -> p (a b)")[:, 0:W]

        def s_qk(i):
            h, j = units[i]
            W = 128 * (j + 1)
            js = slice(j * 128, j * 128 + 128)
            m = st[i]["m"] = self.small(8)
            st[i]["e"] = []
            for mp in range(2):
                b, fw = self.take("s2")
                q = slice(64 * mp, 64 * mp + 64)
                for c in range(0, W, 512):
                    w = min(512, W - c)
                    last = c + w == W
                    t = P.op("pe", lambda e, b=b, c=c, w=w, q=q, last=last: e.matmul(
                        p[:, b[c // 512], 0:w], qT[q, h, js], kT[q, h, c:c + w], start=True, stop=not last,
                        skip_group_check=True), fw, qk_tok["q"][j], qk_tok["k"][:j + 1], mark=False)
                    if last:
                        t = P.op("pe", lambda e, b=b, c=c, w=w: e.matmul(
                            p[:, b[c // 512], w - 128:w], self.idb[:], self.cmask[:], start=False, stop=True,
                            skip_group_check=True), tl)
                sv = wide(b, W)
                t = self.red(m[:, mp:mp + 1], sv, ALU.max, t)
                t = self.ts(m[:, 2 + mp:3 + mp], m[:, mp:mp + 1], -scale, None, ALU.mult, None, t)
                t = self.act(pr[i % 2][mp][:, 0:W], sv, ACT.Exp, t, pfree[i % 2], f4, scale=scale, bias=m[:, 2 + mp:3 + mp],
                             accum_out=m[:, 4 + mp:5 + mp])
                self.give(b, t)
                st[i]["e"].append(t)

        def s_mix(i):
            h, j = units[i]
            W = 128 * (j + 1)
            m = st[i]["m"]
            t = self.rec(m[:, 6:8], m[:, 4:6], st[i]["e"])
            t2 = self.tt(m[:, 7:8], m[:, 7:8], self.lamt[:, 2:3], ALU.mult, t, tl)
            p1, p2 = pr[i % 2]
            t2 = self.ts(p2[:, 0:W], p2[:, 0:W], m[:, 7:8], None, ALU.mult, None, t2)
            t = self.stt(p1[:, 0:W], p1[:, 0:W], m[:, 6:7], p2[:, 0:W], ALU.mult, ALU.add, t2)
            b, fw = self.take("t2")
            for k in range(j + 1):
                x = self.tr(p[:, b[k // 4], k % 4 * 128:k % 4 * 128 + 128], p1[:, k * 128:k * 128 + 128], fw, t,
                            mark=(k == j))
            pfree[i % 2] = x
            w1 = min(W, 512)
            a = aT[0]
            c = [self.copy(a[:, 0:w1], p[:, b[0], 0:w1], x, tfree[0], f4)]
            if W > 512:
                c.append(self.vcopy(a[:, 512:W], p[:, b[1], 0:W - 512], x, tfree[0], f4))
            self.give(b, c)
            st[i]["t"] = c

        def s_pv(i):
            h, j = units[i]
            b, fw = self.take("o2")
            o = p[:, b[0], 0:128]
            t = self.mm(o, [(aT[0][:, k * 128:k * 128 + 128], v[:, k, h * 128:h * 128 + 128], v_tok[k])
                            for k in range(j + 1)], fw, st[i]["t"])
            tfree[0] = t
            d = self.copy(ob[:, j, h, :], o, t, f4)
            d2 = self.act(jk, ob[:, j, h, :], ACT.Square, d, accum_out=ssq[:, j, h:h + 1])
            self.give(b, d)
            otok[j] += [d, d2]

        nn = len(units)
        for i in range(nn + 2):
            if i < nn:
                s_qk(i)
            if 1 <= i < nn + 1:
                s_mix(i - 1)
                s_pv(i - 1)
        t = self.act(rr, ssq, ACT.Sqrt, otok, scale=1.0 / 128, bias=self.eps[1e-6])
        t = self.rec(rr, rr, t)
        for j in range(8):
            d = []
            for h in range(4):
                d.append(self.stt(ob[:, j, h, :], ob[:, j, h, :], rr[:, j, h:h + 1], sgm[0], ALU.mult, ALU.mult, t, ts_))
            mix[j] += self.to_T([ob[:, j, h, :] for h in range(4)], j, d, ring="tr4")

        f5 = self.fence()
        R = self.region(f"m{l}", mod=True)
        z = self.z = R.new("z", [128, 8, 1024])
        g1, g2 = R.new("g1", [128, 1024]), R.new("g2", [128, 1024])
        xr = [R.new(f"xr{i}", [128, 1024]) for i in range(2)]
        self.junk = R.new("junk", [128, 1024])
        self.post(l, z, g1, g2, xr, f5, I["norm_mix_post_2"][l], I["norm_mlp_pre_2"][l], 1 + 2 * l, 2 + 2 * l)
        wo = I["w_out_2"][l]

        def evac(half):
            def f(j, b, src, tok):
                c = slice(half * 512, half * 512 + 512)
                t = self.copy(z[:, j, c], src, tok, f5)
                self.give(b, t)
                self.zt[j].append(t)
                if half == 1:
                    self.post_rows(j)
            return f

        self.zt = [[] for _ in range(8)]
        for half in range(2):
            self.proj_nat(8, lambda k: [(0, wo[k * 128:k * 128 + 128, half * 512:half * 512 + 512])], 512, self.sels,
                          mix, evac(half))
        self.uT = self.ut

    def tf_off(self):
        return self.t_lo_off - 36864

    def lam(self, l, f0):
        P, I = self.P, self.I
        lq = self.tfl[0:64, 8, 0:8]
        t = []
        names = ("lambda_q1_2", "lambda_k1_2", "lambda_q2_2", "lambda_k2_2")
        for i, nme in enumerate(names):
            t.append(P.dma("act", self.lamt[0:64, 4 + i:5 + i], I[nme][l].rearrange("(p o) -> p o", o=1), f0))
        a = self.tt(self.lamt[0:64, 4:5], self.lamt[0:64, 4:5], self.lamt[0:64, 5:6], ALU.mult, t)
        a2 = self.tt(self.lamt[0:64, 5:6], self.lamt[0:64, 6:7], self.lamt[0:64, 7:8], ALU.mult, t, a)
        b, fw = self.take("proj")
        m = self.mm(self.ps[:, b[0], 0:2], [(self.ones[0:64, :], self.lamt[0:64, 4:6])], fw, a, a2, self.base_tok)
        e = self.act(self.lamt[:, 0:2], self.ps[:, b[0], 0:2], ACT.Exp, m, f0)
        self.give(b, e)
        lam_init = 0.8 - 0.6 * math.exp(-0.3 * l)
        d = self.tt(self.lamt[:, 2:3], self.lamt[:, 1:2], self.lamt[:, 0:1], ALU.subtract, e)
        d = self.ts(self.lamt[:, 2:3], self.lamt[:, 2:3], -lam_init, None, ALU.add, None, d)
        if l == 0:
            cm = self.tfl[:, 8, 512:640]
            c = P.dma("act", cm, I["k_causal"], f0)
            c = self.vcopy(self.cmask[:], cm, c)
            c2 = self.vcopy(self.idb[:], self.ident[:], self.base_tok)
            self.mask_tok = [c, c2]
        return [d, self.mask_tok]

    def post(self, l, z, g1, g2, xr, f, gpost, gpre, xin, xout):
        self.g1 = (g1, self.bc(g1[:], gpost, f))
        if gpre is not None:
            self.gpre = (g2, self.bc(g2[:], gpre, f))
        self.xr, self.xf, self.pf = xr, [None] * len(xr), f
        self.xin, self.xout = xin, xout
        self.ut = []

    def post_rows(self, j):
        P = self.P
        z = self.z[:, j, :]
        x = j % len(self.xr)
        tx = P.dma("act", self.xr[x][:], self.d_x[self.xin][j], self.pf, self.xf[x], self.d_tok[self.xin][j])
        ss = self.small(1)
        t = self.act(self.junk[:], z, ACT.Square, self.zt[j], self.pf, accum_out=ss)
        r, t = self.rms_scale(ss, 1024, 1e-6, t)
        t = self.stt(z, z, r, self.g1[0][:], ALU.mult, ALU.mult, t, self.g1[1])
        t = self.tt(z, z, self.xr[x][:], ALU.add, t, tx)
        self.xf[x] = t
        if self.xout is None:
            self.all_dram.append(P.dma("act", self.out[0, j * 128:j * 128 + 128, :], z, t))
            return
        w = P.dma("act", self.d_x[self.xout][j], z, t)
        self.all_dram.append(w)
        self.d_tok[self.xout][j] = w
        self.pre_rows(j, t, w, self.ut)

    def block2_mlp(self, l):
        P, I = self.P, self.I
        f0 = self.fence()
        p = self.ps
        R = self.region(f"f{l}", mod=True)
        z = self.z = R.new("z", [128, 8, 1024])
        gh = [R.new(f"gh{i}", [128, 2, 1024], F32R) for i in range(2)]
        self.gh_at = (R.off - 16384, R.off - 8192)
        gl = [R.new(f"gl{i}", [128, 2, 1024], F32R) for i in range(2)]
        ta = R.new("ta", [128, 1024])
        tb = R.new("tb", [128, 1024])
        ua = R.new("ua", [128, 1026])
        ub = self.at(f"f{l}_ub", [128, 1026], F32, R.off) if R.off + 4128 <= self.end else None
        assert ub is not None
        cw = self.tfi[:, 8, 0:132].rearrange("p (a b) -> p a b", a=3)
        cb = self.tfi[:, 8, 132:176]
        tcw = P.dma("act", self.tfi[:, 8, 0:176], I["conv"][l], f0)
        tz = [self.zero(ua[:, 0:2], f0), self.zero(ub[:, 0:2], f0)]
        wu, wd = I["w_up_2"][l], I["w_down_2"][l]
        ready = self.uT
        halves = [ready[0:4], ready[4:8]]
        g_tok = {}
        down_tok = {}
        free = {"ua": None, "ub": None, "ta": None, "tb": None}
        for c in range(12):
            if c < 11:
                fo = c * 256
                hold = {}

                def conv(u, name, tile, dst, tok):
                    o = [2 - i for i in range(3)]
                    t = self.ts(dst[:], u[:, 2:1026], cw[:, 2, tile:tile + 1], cb[:, tile:tile + 1], ALU.mult, ALU.add,
                                tok, tcw, tz, free["ta" if dst is ta else "tb"], f0)
                    t = self.stt(dst[:], u[:, 1:1025], cw[:, 1, tile:tile + 1], dst[:], ALU.mult, ALU.add, t)
                    t = self.stt(dst[:], u[:, 0:1024], cw[:, 0, tile:tile + 1], dst[:], ALU.mult, ALU.add, t)
                    free[name] = t
                    return t

                def evac(m, hf, b, src, tok, c=c):
                    u, name = (ua, "ua") if m % 2 == 0 else (ub, "ub")
                    t = self.copy(u[:, 2 + hf * 512:2 + hf * 512 + 512], src, tok, free[name], f0)
                    self.give(b, t)
                    hold.setdefault(m, []).append(t)
                    if hf == 0:
                        return
                    ft = 2 * c + m // 2
                    if m % 2 == 0:
                        t = conv(u, name, ft, ta, hold[m])
                        hold["g"] = self.act(ta[:], ta[:], ACT.Gelu_apprx_tanh, t)
                    else:
                        t = conv(u, name, 22 + ft, tb, hold[m])
                        x = c % 2
                        t = self.tt(tb[:], tb[:], ta[:], ALU.mult, t, hold["g"])
                        free["ta"] = t
                        a = self.copy(gh[x][:, m // 2, :], tb[:], t, down_tok.get(c - 2), f0)
                        d = self.tt(gl[x][:, m // 2, :], tb[:], gh[x][:, m // 2, :].bitcast(F32), ALU.subtract, a,
                                    down_tok.get(c - 2), f0)
                        free["tb"] = [a, d]
                        g_tok.setdefault(c, []).append([a, d])

                def src(k):
                    r = slice(k * 128, k * 128 + 128)
                    return [(0, wu[r, fo:fo + 128]), (128, wu[r, 2816 + fo:2816 + fo + 128]),
                            (256, wu[r, fo + 128:fo + 256]), (384, wu[r, 2816 + fo + 128:2816 + fo + 256])]

                self.proj_T(8, src, 4, halves, evac)
            if c >= 1:
                e = c - 1
                for half in range(2):
                    def evd(j, b, src, tok, half=half, e=e):
                        cc = slice(half * 512, half * 512 + 512)
                        if e == 0:
                            t = self.copy(z[:, j, cc], src, tok, f0)
                        else:
                            t = self.tt(z[:, j, cc], src, z[:, j, cc], ALU.add, tok, self.zt[j][half])
                        self.zt[j][half] = t
                        self.give(b, t)
                        if e == 10 and half == 1:
                            self.post_rows(j)
                    if e == 0 and half == 0:
                        self.zt = [[None, None] for _ in range(8)]
                    if e == 10 and half == 0:
                        fe = self.fence()
                        self.junk = ta
                        g1 = tb
                        xr = [self.at(f"h{l}_x", [128, 1024], F32, R.off - 4128),
                              self.at(f"h{l}_y", [128, 1024], F32, R.off)]
                        g2 = self.at(f"h{l}_g", [128, 1024], F32, self.gh_last(R, e))
                        nxt = I["norm_mix_pre_2"][l + 1] if l == 0 else None
                        self.post(l, z, g1, g2, xr, fe, I["norm_mlp_post_2"][l], nxt, 2 + 2 * l, 3 if l == 0 else None)
                    self.proj_nat(2, lambda k: [(0, wd[e * 256 + k * 128:e * 256 + k * 128 + 128,
                                                      half * 512:half * 512 + 512])], 512, self.sels,
                                  [g_tok[e]] * 8, evd, act=(gh[e % 2], gl[e % 2]))
                down_tok[e] = self.last_mm
        self.uT = self.ut

    def gh_last(self, R, e):
        return self.gh_at[(e + 1) % 2]


def build_program(nc, I, out, stop=9):
    Kernel(nc, I, out, stop).build()


_INS = ["x", "c", "rel_bias", "ada_w", "ada_b", "ln_g", "ln_b", "a_w_in", "a_w_out", "b_w_in", "b_q_norm", "b_w_uq",
        "b_kv_norm", "b_w_ukv", "b_w_out", "norm_mix_pre_2", "norm_mix_post_2", "w_in_2", "lambda_q1_2", "lambda_k1_2",
        "lambda_q2_2", "lambda_k2_2", "diff_subln_2", "ret_norm_2", "pool_w_2", "pool_scale_2", "w_out_2",
        "norm_mlp_pre_2", "norm_mlp_post_2", "w_up_2", "conv_w_2", "conv_b_2", "w_down_2"]


def declare(nc, inputs, stop=9):
    arrays = {n: np.ascontiguousarray(inputs[n]) for n in _INS}
    conv = np.concatenate([arrays.pop("conv_w_2"), arrays.pop("conv_b_2")[:, None]], 1)
    arrays["conv"] = np.ascontiguousarray(conv.reshape(2, 4, 44, 128).transpose(0, 3, 1, 2).reshape(2, 128, 176))
    arrays.update(host_constants())
    I = {n: nc.dram_tensor("in_" + n, list(a.shape), mybir.dt.from_np(a.dtype), kind="ExternalInput").ap()
         for n, a in arrays.items()}
    I["k_decay2"] = I["k_decay"].rearrange("p h q -> p (h q)")
    out = nc.dram_tensor("out_0", [1, 1024, 1024], F32, kind="ExternalOutput").ap()
    build_program(nc, I, out, stop)
    return {"in_" + n: a for n, a in arrays.items()}


def kernel(**inputs):
    import concourse.bacc as bacc
    from concourse.bass_utils import run_bass_kernel_spmd

    nc = bacc.Bacc("TRN2", target_bir_lowering=False, num_devices=1)
    arrays = declare(nc, inputs)
    r = run_bass_kernel_spmd(nc, [arrays], core_ids=[0])
    return r.results[0]["out_0"]
```

```python
import math
from contextlib import ExitStack

import numpy as np

import concourse.bass as bass
from concourse import mybir

F32 = mybir.dt.float32
F32R = mybir.dt.float32r
BF16 = mybir.dt.bfloat16
ALU = mybir.AluOpType
ACT = mybir.ActivationFunctionType
AXX = mybir.AxisListType.X

ALPHA = 4.0 ** 0.25
NS = 11
NMISC = 40
MASKED = -8e30


def host_constants():
    f = np.float32
    c = {}
    c["k_ident"] = np.eye(128, dtype=f)
    oh = np.zeros((32, 3, 512), f)
    mk = np.zeros((6, 3, 512), f)
    for g, dil in enumerate((1, 4, 8)):
        for n in range(512):
            off = n - 256
            if abs(off) > (127 if dil == 8 else 64) or (dil == 8 and off % 2):
                mk[:, g, 511 - n] = MASKED
                continue
            rel = off * dil
            a = abs(rel)
            large = 8 + int(f(np.log(f(max(a, 1)) / f(8))) / f(math.log(128.0)) * f(8))
            b = (16 if rel > 0 else 0) + (a if a < 8 else min(large, 15))
            oh[b, g, 511 - n] = 1.0
    c["k_oh"], c["k_msk"] = oh, mk

    def angles(dim, theta):
        inv = f(theta) ** (-np.arange(0, dim, 2, dtype=f) / f(dim))
        ang = np.arange(1024, dtype=f)[:, None] * inv[None, :].astype(f)
        return np.cos(ang).astype(f), np.sin(ang).astype(f)

    def natural(t):
        return np.ascontiguousarray(t.reshape(8, 128, -1).transpose(1, 0, 2))

    co, si = angles(32, 10000.0)
    c["k_rope"] = np.ascontiguousarray(np.stack([natural(co), natural(si)], 2))
    tab = np.ones((128, 1024), f)
    tab[64:80], tab[80:96] = co.T, co.T
    tab[96:112], tab[112:128] = -si.T, si.T
    c["k_qtab"] = tab
    co, si = angles(16, 500000.0)
    c["k_rope2"] = np.ascontiguousarray(np.stack([natural(co), natural(si)], 2))
    lg = np.log(1.0 - 2.0 ** (-5.0 - np.arange(4))).astype(np.float64)
    idx = np.arange(128)
    sc = 32.0 ** -0.5
    dec = np.zeros((128, 4, 128))
    for h in range(4):
        d = idx[None, :] - idx[:, None]
        dec[:, h, :] = np.where(d >= 0, np.exp(np.maximum(d, 0) * lg[h]), 0.0) * sc
    c["k_decay"] = dec.astype(f)
    hd = np.repeat(np.arange(4), 32)
    c["k_xi"] = np.exp((idx[None, :] + 1.0) * lg[hd][:, None]).astype(f)
    c["k_zeta"] = (np.exp((127.0 - idx[:, None]) * lg[hd][None, :]) * sc).astype(f)
    c["k_cd"] = np.exp(128.0 * lg[hd])[:, None].astype(f)
    c["k_blk"] = (hd[:, None] == np.repeat(np.arange(4), 64)[None, :]).astype(f)
    c["k_causal"] = np.where(idx[None, :] <= idx[:, None], 0.0, -1e30).astype(f)
    w = np.array([[2, 4], [8, 16]])
    inv = np.zeros((128, 2, 17), f)
    for t in range(2):
        for half in range(2):
            ww = w[t, half]
            inv[64 * half:64 * half + 64, t, 0:16] = 1.0 / np.minimum(np.arange(16) + 1.0, ww)
            inv[64 * half:64 * half + 64, t, 16] = 1.0 / ww
    c["k_inv"] = inv
    return c


def flat(waits):
    for w in waits:
        if w is None:
            continue
        if isinstance(w, tuple) and len(w) == 2 and isinstance(w[0], str):
            yield w
        else:
            yield from flat(w)


class Prog:

    def __init__(self, nc, ctx):
        self.q = {e: [] for e in ("pe", "dve", "act", "pool", "sp")}
        self.sem = {e: ctx.enter_context(nc.semaphore("s_" + e)) for e in self.q}
        self.n = {}
        self.nc, self.ctx = nc, ctx
        self.misc = 0
        self.last_misc = {}

    def op(self, e, f, *waits, mark=True):
        tok = None
        if mark:
            self.n[e] = self.n.get(e, 0) + 1
            tok = (e, self.n[e])
        self.q[e].append((list(flat(waits)), f, e if mark else None, 1))
        return tok

    def dma(self, e, out, in_, *waits, sem=None):
        if sem is None:
            sem = f"d{self.misc % NMISC}"
            self.misc += 1
            waits = (*waits, self.last_misc.get(sem))
        if sem not in self.sem:
            self.sem[sem] = self.ctx.enter_context(self.nc.semaphore(sem))
        self.n[sem] = self.n.get(sem, 0) + 16
        tok = (sem, self.n[sem])
        self.last_misc[sem] = tok
        self.q[e].append((list(flat(waits)), lambda eng: eng.dma_start(out, in_), sem, 16))
        return tok

    def emit(self, e, eng):
        seen = {}
        for waits, f, sem, by in self.q[e]:
            for s, v in waits:
                if seen.get(s, 0) < v:
                    eng.wait_ge(self.sem[s], v)
                    seen[s] = v
            ins = f(eng)
            if sem is not None:
                ins.then_inc(self.sem[sem], by)


class Kernel:
    def __init__(self, nc, I, out, stop):
        self.nc, self.I, self.out, self.stop = nc, I, out, stop

    def mm(self, out, terms, *waits):
        last = len(terms) - 1
        for i, t in enumerate(terms):
            tok = self.P.op(
                "pe", lambda e, t=t, i=i: e.matmul(out, t[0], t[1], start=(i == 0), stop=(i == last)),
                waits if i == 0 else None, t[2:], mark=(i == last))
        return tok

    def tr(self, out, in_, *waits, mark=True):
        k = in_.shape[0]
        return self.P.op("pe", lambda e: e.transpose(out, in_, self.ident[0:k, 0:k]), waits, mark=mark)

    def copy(self, out, in_, *waits):
        return self.P.op("act", lambda e: e.activation(out, in_, ACT.Copy), waits)

    def act(self, out, in_, fn, *waits, **kw):
        return self.P.op("act", lambda e: e.activation(out, in_, fn, **kw), waits)

    def vcopy(self, out, in_, *waits):
        return self.P.op("dve", lambda e: e.tensor_copy(out, in_), waits)

    def tt(self, out, a, b, op, *waits, eng="dve"):
        return self.P.op(eng, lambda e: e.tensor_tensor(out, a, b, op), waits)

    def ts(self, out, a, s1, s2, o1, o2, *waits, eng="dve"):
        if o2 is None:
            return self.P.op(eng, lambda e: e.tensor_scalar(out, a, s1, None, o1), waits)
        return self.P.op(eng, lambda e: e.tensor_scalar(out, a, s1, s2, o1, o2), waits)

    def stt(self, out, a, s, b, o1, o2, *waits, eng="dve"):
        return self.P.op(eng, lambda e: e.scalar_tensor_tensor(out=out, in0=a, scalar=s, in1=b, op0=o1, op1=o2),
                         waits)

    def red(self, out, a, op, *waits):
        return self.P.op("dve", lambda e: e.tensor_reduce(out, a, AXX, op), waits)

    def rec(self, out, a, *waits):
        return self.P.op("dve", lambda e: e.reciprocal(out, a), waits)

    def zero(self, out, *waits, value=0.0, eng="dve"):
        return self.P.op(eng, lambda e: e.memset(out, value), waits)

    def at(self, name, shape, dt, off):
        size = int(np.prod(shape[1:])) * (2 if dt == BF16 else 4)
        assert off % 32 == 0 and off + size <= self.end, (name, off, size, self.end)
        return self.nc.alloc_sbuf_tensor_at(name, list(shape), dt, offset=off)

    class Region:
        def __init__(self, k, off, end, tag):
            self.k, self.off, self.end, self.tag = k, off, end, tag

        def new(self, name, shape, dt=F32):
            t = self.k.at(f"{self.tag}_{name}", shape, dt, self.off)
            size = int(np.prod(shape[1:])) * (2 if dt == BF16 else 4)
            self.off += (size + 31) // 32 * 32
            assert self.off <= self.end, (self.tag, name, self.off - self.end)
            return t

    def take(self, ring):
        b = self.rings[ring][self.ring_at.get(ring, 0) % len(self.rings[ring])]
        self.ring_at[ring] = self.ring_at.get(ring, 0) + 1
        n = b if isinstance(b, tuple) else (b,)
        waits = []
        for x in n:
            assert self.free[x] is not None, ("bank in use", ring, x)
            waits.append(self.free[x])
            self.free[x] = None
        return n, waits

    def give(self, banks, *toks):
        for x in banks:
            self.free[x] = list(toks)

    def weight(self, pieces):
        n = self.wn
        self.wn += 1
        s = n % NS
        assert n < NS or self.wfree.get(n - NS) is not None, "slot in use"
        freed = self.wfree.pop(n - NS, None)
        w = 0
        for c, ap in pieces:
            ww = int(np.prod(ap.shape[1:]))
            dst = self.wst[:, s, c:c + ww]
            if len(ap.shape) == 3:
                dst = dst.rearrange("p (a b) -> p a b", a=ap.shape[1])
            t = self.P.dma("sp", dst, ap, freed, sem=f"w{s}")
            w = max(w, c + ww)
        hi = self.P.op("pool", lambda e: e.tensor_copy(self.whi[:, s, 0:w], self.wst[:, s, 0:w]), t)
        lo = self.P.op("pool", lambda e: e.tensor_tensor(
            self.wlo[:, s, 0:w], self.wst[:, s, 0:w], self.whi[:, s, 0:w], ALU.subtract), hi)
        return n, s, lo

    def release(self, ws, tok):
        for n, _, _ in ws:
            self.wfree[n] = tok

    def raw_weight(self, ap):
        n = self.wn
        self.wn += 1
        s = n % NS
        assert n < NS or self.wfree.get(n - NS) is not None, "slot in use"
        t = self.P.dma("sp", self.wst[:, s, :], ap, self.wfree.pop(n - NS, None), sem=f"w{s}")
        return n, s, t

    def borrow(self):
        while self.wn % NS:
            self.wfree[self.wn] = self.wfree.pop(self.wn - NS)
            self.wn += 1
        held = list(range(self.wn, self.wn + NS))
        for n in held:
            assert self.wfree.pop(n - NS) is not None
        self.wn += NS
        return held

    def give_back(self, held, toks):
        for n in held:
            self.wfree[n] = toks

    def tiles(self, nk, src, w, items, terms, ready, evac, ring, lag):
        ws = [self.weight(src(k)) for k in range(nk)]
        nb = 1 if lag else 4
        for q in range(0, len(items), nb):
            blk = items[q:q + nb]
            banks = [self.take(ring) for _ in blk]
            toks = [None] * len(blk)
            end = q + nb >= len(items)
            for k in range(nk):
                for i, it in enumerate(blk):
                    b, fw = banks[i]
                    for n, (x, y) in enumerate(terms(it, k, ws[k][1])):
                        first, fin = k == 0 and n == 0, k == nk - 1 and n == 2
                        tok = self.P.op(
                            "pe", lambda e, o=self.ps[:, b[0], 0:w], x=x, y=y, first=first, fin=fin:
                            e.matmul(o, x, y, start=first, stop=fin),
                            ws[k][2] if n == 0 else None, (fw, ready[q + i]) if first else None,
                            mark=fin or (end and n == 2 and i == len(blk) - 1))
                        if fin:
                            toks[i] = tok
                if end:
                    self.wfree[ws[k][0]] = tok
            self.last_mm = tok
            rest = [evac(it, banks[i][0], self.ps[:, banks[i][0][0], 0:w], toks[i]) for i, it in enumerate(blk)]
            late = [f() for f in rest if f is not None]
            self.flush(lag - 1 if lag else max(0, len(self.late) - self.late_n) if self.late_n else 0)
            self.late += [f for f in late if f is not None]

    def flush(self, keep=0):
        while len(self.late) > keep:
            self.late.pop(0)()

    def proj_nat(self, nk, src, w, sels, ready, evac, act=None, ring="proj", lag=0):
        hi, lo = act or (self.thi, self.tlo)

        def terms(j, k, s):
            h, l = sels[j](hi, k), sels[j](lo, k)
            return (h, self.whi[:, s, 0:w]), (h, self.wlo[:, s, 0:w]), (l, self.whi[:, s, 0:w])

        self.tiles(nk, src, w, list(range(len(sels))), terms, ready, evac, ring, lag)

    def proj_T(self, nk, src, nm, ready, evac, act=None, ring="proj", lag=0):
        hi, lo = act or (self.thi, self.tlo)

        def terms(it, k, s):
            c = slice(it[0] * 128, it[0] * 128 + 128)
            r = slice(it[1] * 512, it[1] * 512 + 512)
            return (self.whi[:, s, c], hi[:, k, r]), (self.whi[:, s, c], lo[:, k, r]), (self.wlo[:, s, c], hi[:, k, r])

        items = [(m, hf) for m in range(nm) for hf in range(2)]
        self.tiles(nk, src, 512, items, terms, [ready[hf] for _, hf in items],
                   lambda it, b, ps, tok: evac(it[0], it[1], b, ps, tok), ring, lag)

    def split(self, hi, lo, src, *waits):
        a = self.copy(hi, src, waits)
        d = self.tt(lo, src, hi.bitcast(F32), ALU.subtract, a)
        return a, d

    def to_T(self, blocks, j, tok, ring="tr", kt0=0):
        toks = []
        js = slice(j * 128, j * 128 + 128)
        done = []
        for q in range(0, len(blocks), 4):
            part = blocks[q:q + 4]
            b, fw = self.take(ring)
            for i, blk in enumerate(part):
                t = self.tr(self.ps[:, b[0], i * 128:i * 128 + 128], blk, fw if i == 0 else None, tok,
                            mark=(i == len(part) - 1))
            done.append((q, len(part), b, t))
        for q, n, b, t in done:
            src = self.ps[:, b[0], 0:128 * n].rearrange("p (a b) -> p a b", a=n)
            k = slice(kt0 + q, kt0 + q + n)
            pair = self.split(self.thi[:, k, js], self.tlo[:, k, js], src, t, done[-1][3])
            self.give(b, *pair)
            toks += pair
        return toks

    def small(self, n):
        w = (n + 3) // 4 * 4
        if self.sm_at + w > self.sm_n:
            self.sm_at = 0
        i = self.sm_at
        self.sm_at += w
        return self.sm[:, i:i + n]

    def rms_scale(self, ss, n, eps, tok):
        sd = self.small(ss.shape[1])
        r = self.small(ss.shape[1])
        t = self.act(sd, ss, ACT.Sqrt, tok, scale=1.0 / n, bias=self.eps[eps])
        return r, self.rec(r, sd, t)

    def build(self):
        nc = self.nc
        with ExitStack() as ctx:
            self.ctx = ctx
            P = self.P = Prog(nc, ctx)
            base = (nc.sbuf_base + 31) // 32 * 32
            self.end = nc.sbuf_usable_end // 32 * 32
            self.ps = ctx.enter_context(nc.psum_tensor("ps", [128, 8, 512], F32))
            self.free = {b: [] for b in range(8)}
            self.rings = {"proj": [0, 1, 2, 3], "tr": [4, 5], "tr4": [4, 5, 6, 7], "s1": [0, 1, 2],
                          "t1": [3, 4, 5], "o1": [6, 7], "s2": [(0, 1), (2, 3)], "t2": [(4, 5)], "o2": [6, 7],
                          "all": [0, 1, 2, 3, 4, 5, 6, 7]}
            self.ring_at = {}
            off = base
            self.thi = self.at("thi", [128, 9, 1024], F32R, off)
            self.tfi = self.at("tfi", [128, 9, 1024], F32, off)
            off += 36864
            self.tlo = self.at("tlo", [128, 9, 1024], F32R, off)
            self.tfl = self.at("tfl", [128, 9, 1024], F32, off)
            self.t_lo_off = off
            off += 36864
            self.w_off = off
            self.whi = self.at("whi", [128, NS, 512], F32R, off)
            off += NS * 2048
            self.wlo = self.at("wlo", [128, NS, 512], F32R, off)
            self.wst = self.at("wst", [128, NS, 512], F32, off)
            off += NS * 2048
            self.wn, self.wfree, self.late, self.late_n = 0, {}, [], None
            cr = Kernel.Region(self, off, off + 10240, "cst")
            self.ident = cr.new("ident", [128, 128])
            self.ones = cr.new("ones", [128, 128])
            self.sm_n, self.sm_at = 512, 0
            self.sm = cr.new("sm", [128, 16 * 32])
            self.epst = cr.new("eps", [128, 2])
            self.eps = {1e-5: self.epst[:, 0:1], 1e-6: self.epst[:, 1:2]}
            self.rope = cr.new("rope", [128, 8, 2, 16])
            self.rope2 = cr.new("rope2", [128, 8, 2, 8])
            self.idb = cr.new("idb", [128, 128], BF16)
            self.cmask = cr.new("cmask", [128, 128], BF16)
            self.lamt = cr.new("lam", [128, 8])
            self.cc = cr.new("cc", [128, 16])
            self.lamt_va = cr.new("va", [128, 64])
            self.cb = cr.new("cb", [128, 8, 128])
            off += 10240
            mr = Kernel.Region(self, off, off + 16384, "mod")
            self.mod_off = off
            self.gate = [mr.new("g0", [128, 1024]), None]
            self.msh = mr.new("sh", [128, 1024])
            self.msc = mr.new("sc", [128, 1024])
            self.gate[1] = mr.new("g1", [128, 1024])
            off += 16384
            self.gen = off
            self.rot_tok = None

            self.d_y = nc.dram_tensor("scr_y", [1024, 3, 396], F32, kind="Internal").ap()
            self.d_v = nc.dram_tensor("scr_v", [3, 6, 512], F32, kind="Internal").ap()
            self.d_x = [nc.dram_tensor(f"scr_x{i}", [8, 128, 1024], F32, kind="Internal").ap() for i in range(5)]
            self.d_tok = [[None] * 8 for _ in range(5)]
            self.all_dram = []

            self.setup()
            self.block1_a()
            if self.stop > 1:
                self.block1_b()
            for l in range(2):
                if self.stop > 2 + 2 * l:
                    self.block2_mix(l)
                if self.stop > 3 + 2 * l:
                    self.block2_mlp(l)
            P.op("sp", lambda e: e.nop(), self.all_dram, mark=False)

            block = ctx.enter_context(nc.Block())

            @block.tensor
            def _(e):
                P.emit("pe", e)

            @block.vector
            def _(e):
                P.emit("dve", e)

            @block.scalar
            def _(e):
                P.emit("act", e)

            @block.gpsimd
            def _(e):
                P.emit("pool", e)

            @block.sync
            def _(e):
                P.emit("sp", e)

    def fence(self):
        return [(e, n) for e, n in self.P.n.items() if n]

    def region(self, tag, mod=False):
        return Kernel.Region(self, self.mod_off if mod else self.gen, self.end, tag)

    def bc(self, out, row, *waits, e="act"):
        return self.P.dma(e, out, row.partition_broadcast(128), waits)

    def setup(self):
        P, I = self.P, self.I
        t = [P.dma("act", self.ident[:], I["k_ident"])]
        cT = self.lamt
        tc = P.dma("act", cT[:], I["c"].rearrange("o (p k) -> p (o k)", k=8))
        self.ctok = self.act(self.cc[:, 0:8], cT[:], ACT.Silu, tc)
        for i, l in ((self.rope, "k_rope"), (self.rope2, "k_rope2")):
            t.append(P.dma("act", i[:], I[l]))
        a = self.zero(self.ones[:], value=1.0)
        e1 = self.zero(self.epst[:, 0:1], value=1e-5)
        e2 = self.zero(self.epst[:, 1:2], value=1e-6)
        self.base_tok = [t, a, e1, e2]
        self.cb_tok = self.vcopy(self.cb[:], self.cc[:, 0:8].unsqueeze(2).to_broadcast([128, 8, 128]), self.ctok)
        self.ada_start(0)
        self.ada(0, [(0, 0), (1, 0), (0, 1), (1, 1)])

    def ada_start(self, layer, *waits):
        self.mod_dst = [self.msh, self.msc, self.gate[layer]]
        self.mod_bias = [self.bc(d[:], self.I["ada_b"][layer, n * 1024:n * 1024 + 1024], waits)
                         for n, d in enumerate(self.mod_dst)]
        self.mod_tok = {0: [], 1: [], 2: []}

    def ada(self, layer, parts):
        src = self.I["ada_w"][layer].rearrange("(p k) n -> p k n", k=8)
        for which, half in parts:
            n = which * 1024 + half * 512
            ws = [self.raw_weight(src[:, k, n:n + 512]) for k in range(8)]
            b, fw = self.take("proj")
            m = self.mm(self.ps[:, b[0], :], [(self.cb[:, k, :], self.wst[:, s, :], t) for k, (_, s, t) in enumerate(ws)],
                        fw, self.cb_tok)
            self.release(ws, m)
            o = self.mod_dst[which][:, half * 512:half * 512 + 512]
            z = self.stt(o, self.ps[:, b[0], :], 1.0 if which == 1 else 0.0, o, ALU.add, ALU.add, m,
                         self.mod_bias[which])
            self.give(b, z)
            self.mod_tok[which].append(z)

    def block1_a(self):
        P, I = self.P, self.I
        R = Kernel.Region(self, self.gen + 40960, self.end, "xin")
        xb = [R.new(f"x{i}", [128, 1024]) for i in range(4)]
        ready = []
        freed = [None] * 4
        for j in range(8):
            x = xb[j % 4]
            t = P.dma("act", x[:], I["x"][0, j * 128:j * 128 + 128, :], freed[j % 4])
            t = self.tt(x[:], x[:], self.msc[:], ALU.mult, t, self.mod_tok[1])
            t = self.tt(x[:], x[:], self.msh[:], ALU.add, t, self.mod_tok[0])
            toks = self.to_T([x[:, k * 128:k * 128 + 128] for k in range(8)], j, [t, self.base_tok], ring="tr4")
            freed[j % 4] = toks
            ready.append(toks)
        halves = [ready[0:4], ready[4:8]]

        f0 = self.fence()
        R = self.region("da")
        qT = R.new("q", [128, 3, 1024])
        kT = R.new("k", [128, 3, 1024])
        v = R.new("v", [128, 9, 384])
        sg = R.new("sg", [128, 8, 384])
        bias = R.new("bias", [128, 6, 320])
        yb = [R.new(f"y{i}", [128, 396]) for i in range(2)]
        sb = [R.new(f"s{i}", [128, 256]) for i in range(3)]
        pt = [R.new(f"p{i}", [128, 256]) for i in range(2)]
        V = Kernel.Region(self, self.gen, self.end, "tp")
        ohs = V.new("oh", [32, 3, 512])
        rb = V.new("rb", [32, 18])
        mk = V.new("mk", [6, 3, 512])
        vv = V.new("vv", [6, 3, 512])
        t1 = P.dma("act", ohs[:], I["k_oh"], f0)
        t2 = P.dma("act", rb[:], I["rel_bias"], f0)
        t3 = P.dma("act", mk[:], I["k_msk"], f0)
        vt = []
        for g in range(3):
            b, fw = self.take("proj")
            m = self.mm(self.ps[0:6, b[0], :], [(rb[:, g * 6:g * 6 + 6], ohs[:, g, :])], fw, t1, t2)
            d = self.stt(vv[:, g, :], self.ps[0:6, b[0], :], 8.0, mk[:, g, :], ALU.mult, ALU.add, m, t3)
            self.give(b, d)
            vt.append(P.dma("act", self.d_v[g], vv[:, g, :], d))
        self.all_dram += vt
        f1 = [f0, vt, vt]
        dv = self.d_v

        def toeplitz(g, off0, w):
            a = dv[g]
            return bass.AP(a.tensor, a.offset + 256 - off0 - w, [[1, 128], [512, 6], [1, w]])

        dils = (1, 4, 8)
        win = I["a_w_in"][0]
        units_end = None
        ytok = []
        y_free = [None, None]
        sb_free, pt_free = [None] * 3, [None] * 2
        stn = 0
        for g in range(3):
            dil = dils[g]
            L = 1024 // dil
            fz = [f1, units_end]
            bt = []
            if g == 0:
                bt.append(P.dma("act", bias[:, :, 0:256], toeplitz(0, -64, 256), fz))
            elif g == 1:
                bt.append(P.dma("act", bias[:, :, 0:320], toeplitz(1, -128, 320), fz))
            else:
                bt.append(P.dma("act", bias[:, :, 0:128], toeplitz(2, 0, 128), fz))

            def cols(c0):
                return lambda k: [(0, win[k * 128:k * 128 + 128, c0:c0 + 384])]

            qk_tok = {}

            def evac_T(dst, name):
                def f(m, hf, b, src, tok):
                    if dil == 1:
                        o, s = dst[:, m, hf * 512:hf * 512 + 512], src
                    else:
                        o = dst[:, m, :].rearrange("p (r i) -> p r i", r=dil)[:, :, hf * (L // 2):(hf + 1) * (L // 2)]
                        s = src.rearrange("p (i r) -> p r i", r=dil)
                    t = (self.copy if name == "q" else self.vcopy)(o, s, tok, fz)
                    self.give(b, t)
                    qk_tok.setdefault((name, m), []).append(t)
                return f

            self.proj_T(8, cols(g * 384), 3, halves, evac_T(qT, "q"))
            if g == 0:
                self.ada(0, [(2, 0), (2, 1)])
            self.proj_T(8, cols(1152 + g * 384), 3, halves, evac_T(kT, "k"))

            def rows(t):
                if dil == 1:
                    return lambda a, k: a[:, k, t * 128:t * 128 + 128]
                if dil == 4:
                    r, i0 = t // 2, 128 * (t % 2)
                    return lambda a, k: a[:, k, r + 4 * i0:r + 4 * (i0 + 127) + 1:4]
                return lambda a, k: a[:, k, t:1024:8]

            if g == 0:
                starts = [0, 64, 192, 320, 448, 576, 704, 832, 896]
                vsel = [lambda a, k, s=s: a[:, k, s:s + 128] for s in starts]
            else:
                vsel = [rows(t) for t in range(8)]
            v_tok = [None] * 9

            def evac_v(j, b, src, tok):
                v_tok[j] = self.copy(v[:, j, :], src, tok, fz)
                self.give(b, v_tok[j])

            self.proj_nat(8, cols(2304 + g * 384), 384, vsel, [ready] * 9, evac_v)
            sg_tok = [None] * 8

            def evac_g(j, b, src, tok):
                sg_tok[j] = self.act(sg[:, j, :], src, ACT.Silu, tok, fz)
                self.give(b, sg_tok[j])

            self.proj_nat(8, cols(3456 + g * 384), 384, [rows(t) for t in range(8)], [ready] * 8, evac_g)

            def geometry(j):
                if g == 0:
                    if j == 0:
                        return 0, 192, 64, [(0, 64, 0), (64, 128, 1)]
                    if j == 7:
                        return 832, 192, 0, [(0, 64, 7), (64, 128, 8)]
                    return 128 * j - 64, 256, 0, [(0, 128, j), (128, 128, j + 1)]
                if g == 1:
                    if j % 2 == 0:
                        return 128 * j, 192, 128, [(0, 128, j), (128, 64, j + 1)]
                    return 128 * j - 128, 256, 0, [(0, 128, j - 1), (128, 128, j)]
                return 128 * j, 128, 0, [(0, 128, j)]

            units = [(j, h) for j in range(8) for h in range(6)]
            st = [dict() for _ in units]
            ob = {}

            def s_qk(i):
                j, h = units[i]
                k0, W, _, _ = geometry(j)
                p = slice(64 * (h % 2), 64 * (h % 2) + 64)
                b, fw = self.take("s1")
                st[i]["b"] = b
                st[i]["qk"] = self.mm(self.ps[:, b[0], 0:W],
                                      [(qT[p, h // 2, j * 128:j * 128 + 128], kT[p, h // 2, k0:k0 + W])],
                                      fw, qk_tok["q", h // 2], qk_tok["k", h // 2])

            def s_max(i):
                j, h = units[i]
                _, W, c0, _ = geometry(j)
                b = st[i]["b"]
                y = yb[j % 2]
                s = sb[i % 3]
                n = (256, 320, 128)[g]
                e1 = n - c0 - W
                bv = bias[:, h, n - 1 - c0:e1 - 1 if e1 else None:-1]
                t = P.op("dve", lambda e: e.tensor_tensor_reduce(
                    s[:, 0:W], self.ps[:, b[0], 0:W], bv, -0.125, 3.0e38, ALU.add, ALU.min,
                    y[:, 384 + h:385 + h]), st[i]["qk"], bt, sb_free[i % 3], y_free[j % 2], fz)
                self.give(b, t)
                st[i]["e"] = self.act(s[:, 0:W], s[:, 0:W], ACT.Exp, t, scale=-1.0,
                                      bias=y[:, 384 + h:385 + h], accum_out=y[:, 390 + h:391 + h])

            def s_tr(i):
                j, h = units[i]
                _, W, _, ch = geometry(j)
                b, fw = self.take("t1")
                for n, (c, w, _) in enumerate(ch):
                    t = self.tr(self.ps[0:w, b[0], n * 128:n * 128 + 128], sb[i % 3][:, c:c + w], fw, st[i]["e"],
                                mark=(n == len(ch) - 1))
                sb_free[i % 3] = t
                cp = self.vcopy if i % 2 else self.copy
                rows_ = [w for _, w, _ in ch]
                if min(rows_) == 128 or len(rows_) == 1:
                    x = cp(pt[i % 2][:, 0:128 * len(ch)], self.ps[:, b[0], 0:128 * len(ch)], t, pt_free[i % 2], fz)
                else:
                    for n, w in enumerate(rows_):
                        x = cp(pt[i % 2][0:w, n * 128:n * 128 + 128], self.ps[0:w, b[0], n * 128:n * 128 + 128], t,
                               pt_free[i % 2], fz)
                self.give(b, x)
                st[i]["pt"] = x

            def s_pv(i):
                j, h = units[i]
                _, _, _, ch = geometry(j)
                if h == 0:
                    ob[j] = self.take("o1")
                b, fw = ob[j]
                t = self.mm(self.ps[:, b[0], h * 64:h * 64 + 64],
                            [(pt[i % 2][0:w, n * 128:n * 128 + 128], v[0:w, vt_, h * 64:h * 64 + 64], v_tok[vt_])
                             for n, (_, w, vt_) in enumerate(ch)], fw, st[i]["pt"])
                pt_free[i % 2] = t
                if h == 5:
                    y = yb[j % 2]
                    d = self.tt(y[:, 0:384], self.ps[:, b[0], 0:384], sg[:, j, :], ALU.mult, t, sg_tok[j])
                    self.give(b, d)
                    if dil == 1:
                        dst = self.d_y[j * 128:j * 128 + 128, g, :]
                    elif dil == 4:
                        r, i0 = j // 2, 128 * (j % 2)
                        dst = self.d_y.rearrange("(i r) g n -> r i g n", r=4)[r, i0:i0 + 128, g, :]
                    else:
                        dst = self.d_y.rearrange("(i r) g n -> r i g n", r=8)[j, :, g, :]
                    w = P.dma("act", dst, y[:], d, st[i]["e"])
                    y_free[j % 2] = w
                    ytok.append(w)
                    st[i]["end"] = d

            n = len(units)
            for i in range(n + 4):
                if i < n:
                    s_qk(i)
                    s_max(i)
                if 2 <= i < n + 2:
                    s_tr(i - 2)
                if 3 <= i < n + 3:
                    s_pv(i - 3)
            units_end = [st[n - 1]["end"], self.fence()]
        self.all_dram += ytok
        self.mod0 = self.mod_tok[2]

        f2 = self.fence()
        R = self.region("mix")
        z = self.z = R.new("z", [128, 8, 1024])
        G = Kernel.Region(self, self.gen, self.gen + 32768, "gt")
        yr = [G.new(f"yr{i}", [128, 1188]) for i in range(3)]
        sa = G.new("sa", [128, 8, 3, 12])
        sl = G.new("sl", [128, 8, 3, 6])
        se = G.new("se", [128, 8, 3, 6])
        s1 = G.new("s1", [128, 8, 6])
        fac = R.new("fac", [128, 8, 3, 6])
        st_ = [P.dma("act", sa[:, :, g, :], self.d_y[:, g, 384:396].rearrange("(j p) n -> p j n", p=128), f2, ytok)
               for g in range(3)]
        self.ada_start(1, f2)
        self.ada(1, [(0, 0), (0, 1), (1, 0), (1, 1), (2, 0), (2, 1)])
        t = self.act(sl[:], sa[:, :, :, 6:12], ACT.Ln, st_)
        t = self.tt(sl[:], sl[:], sa[:, :, :, 0:6], ALU.subtract, t, st_)
        t = self.tt(s1[:], sl[:, :, 0, :], sl[:, :, 1, :], ALU.max, t)
        t = self.tt(s1[:], s1[:], sl[:, :, 2, :], ALU.max, t)
        t = self.tt(sl[:], sl[:], s1[:].unsqueeze(2).to_broadcast([128, 8, 3, 6]), ALU.subtract, t)
        te = self.act(se[:], sl[:], ACT.Exp, t)
        t = self.tt(s1[:], se[:, :, 0, :], se[:, :, 1, :], ALU.add, te)
        t = self.tt(s1[:], s1[:], se[:, :, 2, :], ALU.add, t)
        t = self.tt(sl[:], sa[:, :, :, 6:12], s1[:].unsqueeze(2).to_broadcast([128, 8, 3, 6]), ALU.mult, t)
        t = self.rec(sl[:], sl[:], t)
        tf = self.tt(fac[:], se[:], sl[:], ALU.mult, t)
        fr = [None] * 3
        yT = []
        for j in range(8):
            y = yr[j % 3]
            t = P.dma("act", y[:], self.d_y[j * 128:j * 128 + 128].rearrange("p g n -> p (g n)"), f2, ytok, fr[j % 3])
            y4 = y[:].rearrange("p (g n) -> p g n", g=3)[:, :, 0:384].rearrange("p g (h e) -> p g h e", h=6)
            for g in range(3):
                d = self.tt(y4[:, g], y4[:, g], fac[:, j, g, :].unsqueeze(2).to_broadcast([128, 6, 64]), ALU.mult,
                            t, tf)
            tk = self.to_T([y[:, (q // 3) * 396 + (q % 3) * 128:(q // 3) * 396 + (q % 3) * 128 + 128]
                            for q in range(9)], j, d, ring="tr4")
            fr[j % 3] = tk
            yT.append(tk)

        f3 = self.fence()
        lg = R.new("lg", [128, 1024])
        lb = R.new("lb", [128, 1024])
        tg = [self.bc(lg[:], I["ln_g"][0], f3), self.bc(lb[:], I["ln_b"][0], f3)]
        self.rows_start(R, f3, lambda j: (I["x"][0, j * 128:j * 128 + 128, :], None), 0)
        tmp = R.new("lt", [128, 1024])
        t = self.tt(tmp[:], lb[:], self.msc[:], ALU.mult, tg, f3, self.mod_tok[1])
        t = self.tt(self.msh[:], self.msh[:], tmp[:], ALU.add, t, self.mod_tok[0])
        t2 = self.tt(self.msc[:], self.msc[:], lg[:], ALU.mult, tg, t)
        self.mod_tok[0] = self.mod_tok[1] = [t, t2]
        wo = I["a_w_out"][0]

        def evac(half):
            def f(j, b, src, tok):
                c = slice(half * 512, half * 512 + 512)
                d = self.tt(z[:, j, c], src, self.gate[0][:, c], ALU.mult, tok, f3, self.mod0)
                self.give(b, d)
                self.zt[j].append(d)
                if half == 1:
                    return lambda: self.ln_rows(j, lg, lb, tg)
            return f

        sels = [lambda a, k, j=j: a[:, k, j * 128:j * 128 + 128] for j in range(8)]
        self.sels = sels
        for half in range(2):
            self.proj_nat(9, lambda k: [(0, wo[k * 128:k * 128 + 128, half * 512:half * 512 + 512])], 512, sels, yT,
                          evac(half), lag=2 * half)
        self.flush()
        self.uT = self.ut

    def rows_start(self, R, f, xsrc, xout):
        self.xr = R if isinstance(R, list) else [R.new(f"xr{i}", [128, 1024]) for i in range(2)]
        self.hb = self.hb if isinstance(R, list) else [R.new(f"hb{i}", [128, 1024]) for i in range(3)]
        self.hfree = [None] * 3
        self.xsrc, self.xout, self.pf = xsrc, xout, f
        self.xt, self.xf = {}, [None, None]
        self.ut, self.zt = [], [[] for _ in range(8)]
        for j in range(2):
            self.xload(j)

    def xload(self, j):
        if j < 8:
            ap, w = self.xsrc(j)
            self.xt[j] = self.P.dma("act", self.xr[j % 2][:], ap, self.pf, self.xf[j % 2], w)

    def store(self, j, z, tok):
        w = self.P.dma("act", self.d_x[self.xout][j] if self.xout is not None else
                       self.out[0, j * 128:j * 128 + 128, :], z, tok)
        self.all_dram.append(w)
        if self.xout is not None:
            self.d_tok[self.xout][j] = w

    def row_tail(self, j, h, t):
        x = self.to_T([h[:, k * 128:k * 128 + 128] for k in range(8)], j, t, ring="tr4")
        self.hfree[j % 3] = x
        self.ut.append(x)

    def ln_rows(self, j, lg, lb, tg):
        P = self.P
        z = self.z[:, j, :]
        t = self.stt(z, self.xr[j % 2][:], ALPHA, z, ALU.mult, ALU.add, self.zt[j], self.xt[j])
        self.xf[j % 2] = t
        st = self.small(12)
        mv = self.small(2)
        a = P.op("dve", lambda e: e.bn_stats(st[:, 0:6], z[:, 0:512]), t)
        b = P.op("dve", lambda e: e.bn_stats(st[:, 6:12], z[:, 512:1024]), t)
        t = P.op("dve", lambda e: e.bn_aggr(mv, st), a, b)
        sd, r = self.small(1), self.small(1)
        self.xload(j + 2)
        s = self.act(sd, mv[:, 1:2], ACT.Sqrt, t, bias=self.eps[1e-5])
        s = self.rec(r, sd, s)
        t = self.ts(z, z, mv[:, 0:1], r, ALU.subtract, ALU.mult, s)
        h = self.hb[j % 3][:]
        if self.xout == 0:
            d = self.tt(h, z, self.msc[:], ALU.mult, t, self.mod_tok[1], self.hfree[j % 3], self.pf)
            t = self.tt(z, z, lg[:], ALU.mult, t, tg, d, eng="pool")
            t = self.tt(z, z, lb[:], ALU.add, t, eng="pool")
            d = self.tt(h, h, self.msh[:], ALU.add, d, self.mod_tok[0])
        else:
            t = self.tt(z, z, lg[:], ALU.mult, t, tg)
            t = self.tt(z, z, lb[:], ALU.add, t)
            d = self.pre_rows(j, t)

        def tail():
            self.store(j, z, t)
            self.row_tail(j, h, d)
        return tail

    def pre_rows(self, j, tok):
        z = self.z[:, j, :]
        ss = self.small(1)
        t = self.act(self.junk[:], z, ACT.Square, tok, self.pf, accum_out=ss)
        r, t = self.rms_scale(ss, 1024, 1e-6, t)
        return self.stt(self.hb[j % 3][:], z, r, self.gpre[0][:], ALU.mult, ALU.mult, t, self.gpre[1],
                        self.hfree[j % 3], self.pf)

    def rotate(self, x1, x2, co, si, tmp, tok):
        a = self.tt(tmp[0], x1, si, ALU.mult, tok, self.rot_tok)
        b = self.tt(tmp[1], x2, si, ALU.mult, tok)
        c = self.tt(x1, x1, co, ALU.mult, a)
        d = self.tt(x2, x2, co, ALU.mult, b)
        c = self.tt(x1, x1, tmp[1], ALU.subtract, c, b)
        d = self.tt(x2, x2, tmp[0], ALU.add, d, a)
        self.rot_tok = [c, d]
        return [c, d]

    def block1_b(self):
        P, I = self.P, self.I
        f0 = self.fence()
        R = self.region("mla")
        cqh, cql = R.new("cqh", [128, 2, 1024], F32R), R.new("cql", [128, 2, 1024], F32R)
        ckh, ckl = R.new("ckh", [128, 1, 1024], F32R), R.new("ckl", [128, 1, 1024], F32R)
        kT = [R.new(f"kT{i}", [128, 1024]) for i in range(2)]
        B = R.off
        v = [R.new(f"v{i}", [128, 8, 128]) for i in range(2)]
        qT = [R.new(f"qT{i}", [128, 1024]) for i in range(2)]
        pp = [R.new(f"p{i}", [128, 1024]) for i in range(2)]
        pt = [R.new(f"t{i}", [128, 1024]) for i in range(2)]
        T = Kernel.Region(self, B, self.end, "ml0")
        g0 = T.new("g0", [128, 8, 512])
        cn = [T.new(f"cn{i}", [128, 512]) for i in range(8)]
        tmp = T.new("tmp", [128, 4, 16])
        jk = self.msc[:, 384:640]
        qg = self.msc[:, 0:256]
        kg = self.msc[:, 256:384]
        tg = [self.bc(qg, I["b_q_norm"][0], f0), self.bc(kg, I["b_kv_norm"][0], f0)]
        qtab = self.msh
        tq = P.dma("act", qtab[:], I["k_qtab"], f0)
        win = I["b_w_in"][0]
        ready = self.uT
        lat = {"q": [], "c": [], "r": []}

        def evac_c(j, b, src, tok):
            x = cn[j]
            js = slice(j * 128, j * 128 + 128)
            t = self.copy(x[:, 0:416], src, tok, f0)
            self.give(b, t)

            def mid():
                s1, s2 = self.small(1), self.small(1)
                a1 = self.act(jk[:, 0:256], x[:, 0:256], ACT.Square, t, accum_out=s1)
                a2 = self.act(jk[:, 0:128], x[:, 256:384], ACT.Square, t, a1, accum_out=s2)
                r1, t1 = self.rms_scale(s1, 256, 1e-6, a1)
                r2, t2 = self.rms_scale(s2, 128, 1e-6, a2)
                t1 = self.stt(x[:, 0:256], x[:, 0:256], r1, qg, ALU.mult, ALU.mult, t1, tg)
                t2 = self.stt(x[:, 256:384], x[:, 256:384], r2, kg, ALU.mult, ALU.mult, t2, tg)
                ro = self.rotate(x[:, 384:400], x[:, 400:416], self.rope[:, j, 0, :], self.rope[:, j, 1, :],
                                 [tmp[:, i, :] for i in range(4)], [t, self.base_tok])
                t3 = self.vcopy(x[:, 416:448], x[:, 384:416], ro)
                z = self.zero(x[:, 448:512], t)

                def tail():
                    bb, fw = self.take("tr4")
                    for i in range(3):
                        m = self.tr(self.ps[:, bb[0], i * 128:i * 128 + 128], x[:, i * 128:i * 128 + 128], fw, t1, t2,
                                    mark=False)
                    m = P.op("pe", lambda e: e.transpose(self.ps[:, bb[0], 384:512], x[:, 320:448], self.ident[:]), t3, z)
                    p = self.ps
                    pq = p[:, bb[0], 0:256].rearrange("p (a b) -> p a b", a=2)
                    pk = p[:, bb[0], 256:384]
                    k1 = self.copy(kT[0][64:128, js], p[64:128, bb[0], 384:512], m, f0)
                    k2 = self.copy(kT[1][64:128, js], p[64:128, bb[0], 384:512])
                    a1 = self.copy(cqh[:, :, js], pq)
                    a2 = self.copy(ckh[:, 0, js], pk)
                    d1 = self.tt(cql[:, :, js], pq, cqh[:, :, js].bitcast(F32), ALU.subtract, a1, a2)
                    d2 = self.tt(ckl[:, 0, js], pk, ckh[:, 0, js].bitcast(F32), ALU.subtract, a2)
                    q1, q2 = [a1, d1], [a2, d2]
                    self.give(bb, k1, k2, q1, q2)
                    lat["q"].append(q1)
                    lat["c"].append(q2)
                    lat["r"].append([k1, k2])
                return tail
            return mid

        self.proj_nat(8, lambda k: [(0, win[k * 128:k * 128 + 128, 0:416])], 416, self.sels, ready, evac_c)
        gt = [[], []]

        def evac_g(half):
            def f(j, b, src, tok):
                js = slice(j * 128, j * 128 + 128)
                if half == 0:
                    o = g0[:, j, :].rearrange("p (a b) -> p a b", a=4)
                else:
                    o = self.tfi[:, 0:4, js]
                t = self.act(o, src.rearrange("p (a b) -> p a b", a=4), ACT.Silu, tok, f0)
                self.give(b, t)
                gt[half].append(t)
                if half == 1:
                    gt[0][j] = self.P.dma("act", self.tfl[:, 0:4, js], g0[:, j, :].rearrange("p (a b) -> p a b", a=4),
                                          gt[0][j], tok)
            return f

        for half in range(2):
            c0 = 416 + 512 * half
            self.proj_nat(8, lambda k: [(0, win[k * 128:k * 128 + 128, c0:c0 + 512])], 512, self.sels, ready,
                          evac_g(half))

        f1 = [self.fence()]
        uq = I["b_w_uq"][0]
        ukv = I["b_w_ukv"][0]
        scale = 96.0 ** -0.5
        hs = [None] * 16
        vst = [None] * 8
        kfree, qfree, vfree = [None, None], [None, None], [None, None]
        pfree, tfree = [None, None], [None, None]
        lq = [lat["q"][0:4], lat["q"][4:8]]
        lc = [lat["c"][0:4], lat["c"][4:8]]

        def head(h):
            pc = []
            for k in range(2):
                r = uq[k * 128:k * 128 + 128, h * 96:h * 96 + 96]
                pc += [(k * 128, r), (k * 128 + 96, r[:, 80:96]), (k * 128 + 112, r[:, 64:80])]
            pc.append((256, ukv[:, h * 128:h * 128 + 128]))
            if h % 2 == 0:
                pc.append((384, ukv[:, h * 128 + 64:h * 128 + 128]))
                pc.append((448, ukv[:, h * 128 + 192:h * 128 + 256]))
            w = self.weight(pc)
            _, s, wt = w
            toks = []
            for hf in range(2):
                r = slice(hf * 512, hf * 512 + 512)
                b, fw = self.take("o2")
                terms = []
                for k in range(2):
                    c = slice(k * 128, k * 128 + 128)
                    terms += [(self.whi[:, s, c], cqh[:, k, r], wt), (self.whi[:, s, c], cql[:, k, r]),
                              (self.wlo[:, s, c], cqh[:, k, r])]
                m = self.mm(self.ps[:, b[0], :], terms, fw, lq[hf])
                t = self.tt(qT[h % 2][:, r], self.ps[:, b[0], :], qtab[:, r], ALU.mult, m, tq, qfree[h % 2], f1)
                self.give(b, t)
                toks.append(t)
                b, fw = self.take("o2")
                c = slice(256, 384)
                m = self.mm(self.ps[:, b[0], :], [(self.whi[:, s, c], ckh[:, 0, r], wt), (self.whi[:, s, c], ckl[:, 0, r]),
                                                  (self.wlo[:, s, c], ckh[:, 0, r])], fw, lc[hf])
                t = self.copy(kT[h % 2][0:64, r], self.ps[0:64, b[0], :], m, kfree[h % 2], f0)
                self.give(b, t)
                toks.append(t)
            hs[h] = [toks, lat["r"]]
            if h % 2 == 0:
                vt = []
                c = slice(384, 512)
                for q in range(2):
                    b, fw = self.take("o2")
                    for i in range(4):
                        j = 4 * q + i
                        js = slice(j * 128, j * 128 + 128)
                        m = self.mm(self.ps[:, b[0], i * 128:i * 128 + 128],
                                    [(ckh[:, 0, js], self.whi[:, s, c], wt), (ckh[:, 0, js], self.wlo[:, s, c]),
                                     (ckl[:, 0, js], self.whi[:, s, c])], fw, lat["c"][j])
                    t = self.copy(v[h // 2 % 2][:, 4 * q:4 * q + 4, :],
                                  self.ps[:, b[0], :].rearrange("p (a b) -> p a b", a=4), m, vfree[h // 2 % 2], f1)
                    self.give(b, t)
                    vt.append(t)
                vst[h // 2] = vt
            self.release([w], m)

        units = [(h, j) for h in range(16) for j in range(8)]
        st = [dict() for _ in units]
        ytok = [[] for _ in range(8)]

        def s_qk(i):
            h, j = units[i]
            if j == 0 and h == 0:
                head(0)
            if j == 4 and h + 1 < 16:
                head(h + 1)
            b, fw = self.take("s2")
            for c in range(2):
                r = slice(c * 512, c * 512 + 512)
                t = self.mm(self.ps[:, b[c], :], [(qT[h % 2][:, j * 128:j * 128 + 128], kT[h % 2][:, r])], fw, hs[h])
            kfree[h % 2] = qfree[h % 2] = t
            st[i]["b"] = b
            sv = ps2(b)
            st[i]["m"] = m = self.small(4)
            t = self.red(m[:, 0:1], sv, ALU.max, t)
            t = self.ts(m[:, 1:2], m[:, 0:1], -scale, None, ALU.mult, None, t)
            t = self.act(pp[i % 2][:], sv, ACT.Exp, t, pfree[i % 2], f1, scale=scale, bias=m[:, 1:2],
                         accum_out=m[:, 2:3])
            self.give(b, t)
            st[i]["e"] = t
            st[i]["r"] = self.rec(m[:, 3:4], m[:, 2:3], t)

        def ps2(b):
            return self.ps[:, b[0]:b[0] + 2, :].rearrange("p a b -> p (a b)")

        def s_tr(i):
            b, fw = self.take("t2")
            for k in range(8):
                t = self.tr(self.ps[:, b[k // 4], k % 4 * 128:k % 4 * 128 + 128], pp[i % 2][:, k * 128:k * 128 + 128],
                            fw, st[i]["e"], mark=(k % 4 == 3))
                if k == 3:
                    x1 = self.copy(pt[i % 2][:, 0:512], self.ps[:, b[0], :], t, tfree[i % 2], f1)
            x2 = self.vcopy(pt[i % 2][:, 512:1024], self.ps[:, b[1], :], t, tfree[i % 2], f1)
            pfree[i % 2] = t
            self.free[b[0]], self.free[b[1]] = [x1], [x2]
            st[i]["pt"] = [x1, x2]

        def s_pv(i):
            h, j = units[i]
            b, fw = self.take("o2")
            o = self.ps[:, b[0], 0:64]
            t = self.mm(o, [(pt[i % 2][:, k * 128:k * 128 + 128], v[h // 2 % 2][:, k, h % 2 * 64:h % 2 * 64 + 64])
                            for k in range(8)], fw, st[i]["pt"], vst[h // 2])
            tfree[i % 2] = t
            vfree[h // 2 % 2] = t
            kt = h // 2
            y = (self.tfl if kt < 4 else self.tfi)[:, kt % 4, j * 128 + h % 2 * 64:j * 128 + h % 2 * 64 + 64]
            d = self.stt(y, o, st[i]["m"][:, 3:4], y, ALU.mult, ALU.mult, t, st[i]["r"], gt[0][j], gt[1][j])
            self.give(b, d)
            ytok[j].append(d)

        n = len(units)
        for i in range(n + 3):
            if i < n:
                s_qk(i)
            if 1 <= i < n + 1:
                s_tr(i - 1)
            if 2 <= i < n + 2:
                s_pv(i - 2)

        yT = []
        for j in range(8):
            js = slice(j * 128, j * 128 + 128)
            blocks = [(self.tfl if k < 4 else self.tfi)[:, k % 4, js] for k in range(8)]
            yT.append(self.to_T(blocks, j, ytok[j], ring="tr4"))

        f2 = self.fence()
        R = self.region("mlo")
        z = self.z = R.new("z", [128, 8, 1024])
        lg, lb = R.new("lg", [128, 1024]), R.new("lb", [128, 1024])
        self.junk, gp = self.msc, self.msh
        self.gpre = (gp, self.bc(gp[:], I["norm_mix_pre_2"][0], f2))
        tg = [self.bc(lg[:], I["ln_g"][1], f2), self.bc(lb[:], I["ln_b"][1], f2)]
        self.rows_start(R, f2, lambda j: (self.d_x[0][j], self.d_tok[0][j]), 1)
        wo = I["b_w_out"][0]

        def evac(half):
            def f(j, b, src, tok):
                c = slice(half * 512, half * 512 + 512)
                d = self.tt(z[:, j, c], src, self.gate[1][:, c], ALU.mult, tok, f2, self.mod_tok[2])
                self.give(b, d)
                self.zt[j].append(d)
                if half == 1:
                    return lambda: self.ln_rows(j, lg, lb, tg)
            return f

        for half in range(2):
            self.proj_nat(8, lambda k: [(0, wo[k * 128:k * 128 + 128, half * 512:half * 512 + 512])], 512, self.sels,
                          yT, evac(half), lag=2 * half)
        self.flush()
        self.uT = self.ut

    def block2_mix(self, l):
        P, I = self.P, self.I
        f0 = self.fence()
        p = self.ps
        R = self.region(f"c{l}", mod=True)
        qT, kT = R.new("q", [128, 4, 1024]), R.new("k", [128, 4, 1024])
        v = R.new("v", [128, 8, 512])
        C0 = R.off
        rn = R.new("rn", [128, 8, 512])
        gr = R.new("gr", [128, 8, 256])
        pu = R.new("pu", [128, 2, 1040])
        nt = [rn[:, i, :] for i in range(8)]
        tmp = self.tfl[:, 8, 512:1024].rearrange("p (a b) -> p a b", a=4)
        win = I["w_in_2"][l]
        nfree = [None] * 8
        ready = self.uT
        halves = [ready[0:4], ready[4:8]]
        tl = self.lam(l, f0)
        f0 = self.fence()
        qk_tok = {"q": [], "k": []}

        def cols(c0, w=512):
            return lambda k: [(0, win[k * 128:k * 128 + 128, c0:c0 + w])]

        def evac_qk(dst, name):
            def f(j, b, src, tok):
                i = j
                x = nt[i]
                js = slice(j * 128, j * 128 + 128)
                t = self.copy(x, src, tok, nfree[i], f0)
                self.give(b, t)
                xv = x.rearrange("p (m e) -> p m e", e=64)
                co = self.rope2[:, j, 0:1, :].to_broadcast([128, 8, 8])
                si = self.rope2[:, j, 1:2, :].to_broadcast([128, 8, 8])
                tv = [tmp[:, a, 0:64].rearrange("p (m e) -> p m e", e=8) for a in range(4)]
                def mid():
                    d = self.rotate(xv[:, :, 0:8], xv[:, :, 8:16], co, si, tv, [t, f0])

                    def tail():
                        b, fw = self.take("tr4")
                        for h in range(4):
                            m = self.tr(p[:, b[0], h * 128:h * 128 + 128], x[:, h * 128:h * 128 + 128], fw, d,
                                        mark=(h == 3))
                        nfree[i] = m
                        c = self.copy(dst[:, :, js], p[:, b[0], :].rearrange("p (a b) -> p a b", a=4), m, f0)
                        self.give(b, c)
                        qk_tok[name].append(c)
                    return tail
                return mid
            return f

        self.proj_nat(8, cols(0), 512, self.sels, ready, evac_qk(qT, "q"))
        self.proj_nat(8, cols(512), 512, self.sels, ready, evac_qk(kT, "k"))
        v_tok, r_tok, g_tok = [], [], []

        def evac_v(j, b, src, tok):
            t = self.copy(v[:, j, :], src, tok, f0)
            self.give(b, t)
            v_tok.append(t)

        self.proj_nat(8, cols(1024), 512, self.sels, ready, evac_v)

        def evac_r(j, b, src, tok):
            t = self.copy(rn[:, j, :], src, tok, f0, nfree[j])
            self.give(b, t)
            xv = rn[:, j, 0:256].rearrange("p (m e) -> p m e", e=32)
            co = self.rope[:, j, 0:1, :].to_broadcast([128, 8, 16])
            si = self.rope[:, j, 1:2, :].to_broadcast([128, 8, 16])
            tv = [tmp[:, a, :].rearrange("p (m e) -> p m e", e=16) for a in range(4)]
            r_tok.append([t, self.rotate(xv[:, :, 0:16], xv[:, :, 16:32], co, si, tv, [t, f0])])

        self.proj_nat(8, cols(1536), 512, self.sels, ready, evac_r)

        def evac_g(j, b, src, tok):
            t = self.act(gr[:, j, :], src, ACT.Silu, tok, f0)
            self.give(b, t)
            g_tok.append(t)

        self.proj_nat(8, cols(2048, 256), 256, self.sels, ready, evac_g)
        pu_tok = [self.zero(pu[:, :, 0:16], f0)]

        def evac_p(m, hf, b, src, tok):
            t = self.copy(pu[:, m, 16 + hf * 512:16 + hf * 512 + 512], src, tok, f0)
            self.give(b, t)
            pu_tok.append(t)

        self.proj_T(8, cols(2304, 256), 2, halves, evac_p)

        self.flush()
        f1 = self.fence()
        held = self.borrow()
        S = Kernel.Region(self, self.w_off, self.w_off + NS * 2048, f"r{l}")
        lo = self.w_off + NS * 2048
        S2 = Kernel.Region(self, lo, lo + 7 * 2048, f"s{l}")
        S3 = Kernel.Region(self, lo + 7 * 2048, lo + 11 * 2048, f"p{l}")
        dec = S.new("dec", [128, 512])
        xi, ze, blk, cd = S.new("xi", [128, 128]), S.new("ze", [128, 128]), S.new("blk", [128, 256]), S.new("cd", [128, 8])
        inv = S.new("inv", [128, 2, 17])
        rg = S.new("rg", [128, 256])
        pw = S.new("pw", [128, 2, 128])
        psc = S.new("psc", [128, 8])
        tc = [P.dma("sp", a, I[b], f1) for a, b in (
            (dec[:], "k_decay2"), (xi[:], "k_xi"), (ze[:], "k_zeta"), (blk[:], "k_blk"), (cd[:, 0:1], "k_cd"),
            (inv[:], "k_inv"))]
        tc.append(self.bc(rg[:], I["ret_norm_2"][l], f1, e="sp"))
        tz = self.zero(pw[:], f1)
        tp = []
        for g in range(4):
            q = 64 * (g % 2)
            tp.append(P.dma("sp", pw[q:q + 64, g // 2, q:q + 64], I["pool_w_2"][l, g], tz))
        for t in range(2):
            tp.append(P.dma("sp", psc[:, t:t + 1], I["pool_scale_2"][l, t * 128:t * 128 + 128].rearrange("(p o) -> p o", o=1), f1))
        kt_ = [S.new(f"kt{i}", [128, 128]) for i in range(2)]
        qx = [S.new(f"qx{i}", [128, 128]) for i in range(2)]
        kz = [S.new(f"kz{i}", [128, 128]) for i in range(2)]
        um = S.new("um", [128, 256])
        sq = S.new("sq", [128, 256])
        state = [S.new(f"st{i}", [128, 256]) for i in range(2)]
        qb = [S.new(f"qb{i}", [128, 512]) for i in range(2)]
        it = [S.new(f"it{i}", [128, 512]) for i in range(2)]
        wa = S2.new("wa", [128, 1040])
        wb = S2.new("wb", [128, 1040])
        zq = [self.zero(q[:], f1) for q in qb]
        zs = self.zero(state[0][:], f1)
        tw = [self.zero(wa[:, 0:16], f1), self.zero(wb[:, 0:16], f1)]
        mix = [[] for _ in range(8)]
        rt = {"st": zs, "o": [], "n": []}
        va, sd = self.lamt_va[:, 0:32], self.lamt_va[:, 32:64]
        on = [rn[:, i, 256:512] for i in range(8)]

        def retention():
            it_free, qb_free, x_free = [None, None], [None, None], [None, None]
            for i in range(8):
                a = i % 2
                b, fw = self.take("o2")
                m = self.tr(p[:, b[0], 0:128], rn[:, i, 0:128], fw, r_tok[i], mark=False)
                m = self.tr(p[:, b[0], 128:256], rn[:, i, 128:256])
                t1 = self.copy(kt_[a][:], p[:, b[0], 128:256], m, x_free[a], f1)
                tq = []
                for h in range(4):
                    hp = slice(32 * h, 32 * h + 32)
                    tq.append(self.copy(qb[a][hp, h * 128:h * 128 + 128], p[hp, b[0], 0:128], m, zq[a], qb_free[a]))
                t2 = self.tt(qx[a][:], p[:, b[0], 0:128], xi[:], ALU.mult, m, tq, tc, x_free[a], f1)
                self.give(b, t1, tq, t2)
                t3 = self.tt(kz[a][:], rn[:, i, 128:256], ze[:], ALU.mult, r_tok[i], tc, x_free[a], f1)
                yield
                b, fw = self.take("o2")
                m = self.mm(p[:, b[0], :], [(kt_[a][:], qb[a][:])], fw, t1, tq)
                qb_free[a] = m
                t4 = self.tt(it[a][:], p[:, b[0], :], dec[:], ALU.mult, m, tc, it_free[a], f1)
                self.give(b, t4)
                yield
                b, fw = self.take("o2")
                cross = P.op("pe", lambda e, b=b, a=a, s=state[i % 2]: e.matmul(
                    p[:, b[0], 0:256], qx[a][:], s[:], start=True, stop=False, skip_group_check=True),
                    fw, t2, rt["st"], mark=True)
                for h in range(4):
                    m = P.op("pe", lambda e, b=b, a=a, h=h, i=i: e.matmul(
                        p[:, b[0], h * 64:h * 64 + 64], it[a][:, h * 128:h * 128 + 128],
                        rn[:, i, 256 + h * 64:320 + h * 64], start=False, stop=(h == 3), skip_group_check=True),
                        t4, r_tok[i], mark=(h == 3))
                it_free[a] = m
                if i < 7:
                    b2, fw = self.take("o2")
                    m2 = self.mm(p[:, b2[0], 0:256], [(kz[a][:], rn[:, i, 256:512])], fw, t3)
                    x_free[a] = [m2, cross]
                    t = self.tt(um[:], p[:, b2[0], 0:256], blk[:], ALU.mult, m2, tc, rt["st"])
                    self.give(b2, t)
                    rt["st"] = self.stt(state[1 - a][:], state[a][:], cd[:, 0:1], um[:], ALU.mult, ALU.add, t,
                                        rt["st"], zs, cross)
                    m = m2
                t = self.copy(on[i], p[:, b[0], 0:256], m)
                self.give(b, t)
                o3 = on[i].rearrange("p (h e) -> p h e", h=4)
                q3 = sq[:].rearrange("p (h e) -> p h e", h=4)
                mu = self.small(4)
                t = self.red(mu, o3, ALU.add, t)
                t = self.ts(mu, mu, 1.0 / 64, None, ALU.mult, None, t)
                t = self.tt(o3, o3, mu.unsqueeze(2).to_broadcast([128, 4, 64]), ALU.subtract, t)
                t2 = self.tt(q3, o3, o3, ALU.mult, t, rt["n"][-1:], f1)
                rt["n"].append(self.red(va[:, i * 4:i * 4 + 4], q3, ALU.add, t2))
                rt["o"].append(t)
                yield

        def ret_scale():
            t = self.act(sd, va, ACT.Sqrt, rt["n"], scale=1.0 / 64, bias=self.eps[1e-6])
            tr_ = self.rec(va, sd, t)
            for i in range(8):
                o3 = on[i].rearrange("p (h e) -> p h e", h=4)
                t = self.tt(o3, o3, va[:, i * 4:i * 4 + 4].unsqueeze(2).to_broadcast([128, 4, 64]), ALU.mult, tr_,
                            rt["o"][i])
                t = self.tt(on[i], on[i], rg[:], ALU.mult, t, tc, eng="pool")
                rt["o"][i] = self.tt(on[i], on[i], gr[:, i, :], ALU.mult, t, g_tok, eng="pool")

        def ret_out():
            for j in range(8):
                mix[j] += self.to_T([on[j][:, 0:128], on[j][:, 128:256]], j, rt["o"][j], kt0=4, ring="o2")
                yield

        def pool():
            lastp = None
            t = [tw, pu_tok]
            for m_ in range(2):
                u = pu[:, m_, :]

                def add(o, x, y, *w):
                    return self.tt(o, x, y, ALU.add, w, eng="pool")

                def cp(o, x, *w):
                    return self.P.op("pool", lambda e: e.tensor_copy(o, x), w)

                a = add(wa[:, 16:1040], u[:, 16:1040], u[:, 15:1039], t, lastp, f1)
                if m_ == 0:
                    b2 = add(wb[64:128, 16:1040], wa[64:128, 16:1040], wa[64:128, 14:1038], a, tw)
                    b1 = cp(wb[0:64, 16:1040], wa[0:64, 16:1040], a, tw)
                else:
                    b1 = add(wb[:, 16:1040], wa[:, 16:1040], wa[:, 14:1038], a, tw)
                    a = add(wa[:, 16:1040], wb[:, 16:1040], wb[:, 12:1036], b1)
                    b2 = add(wb[64:128, 16:1040], wa[64:128, 16:1040], wa[64:128, 8:1032], a)
                    b1 = cp(wb[0:64, 16:1040], wa[0:64, 16:1040], a)
                pl = wa[:, 16:1040]
                mul = ALU.mult
                t1 = self.tt(pl[:, 16:1024], wb[:, 32:1040], inv[:, m_, 16:17].to_broadcast([128, 1008]), mul, b1, b2, tc,
                             eng="pool")
                t2 = self.tt(pl[:, 0:16], wb[:, 16:32], inv[:, m_, 0:16], mul, b1, b2, tc, eng="pool")
                t1 = self.tt(pl, pl, u[:, 16:1040], ALU.subtract, t1, t2, eng="pool")
                yield
                for hf in range(2):
                    r = slice(hf * 512, hf * 512 + 512)
                    b, fw = self.take("o2")
                    mm_ = self.mm(p[:, b[0], :], [(pw[:, m_, :], pl[:, r])], fw, t1, tp)
                    s = self.act(self.thi[:, 6 + m_, r], p[:, b[0], :], ACT.Copy, mm_, tp, scale=psc[:, m_:m_ + 1])
                    d = self.stt(self.tlo[:, 6 + m_, r], p[:, b[0], :], psc[:, m_:m_ + 1],
                                 self.thi[:, 6 + m_, r].bitcast(F32), ALU.mult, ALU.subtract, s, tp)
                    self.give(b, d)
                    for j in range(4):
                        mix[4 * hf + j] += [s, d]
                    lastp = mm_
                    yield

        p1 = [self.tfl[:, i, :] for i in range(3)]
        p2 = [S3.new(f"p{i}", [128, 1024]) for i in range(2)]
        aT = [self.tfl[:, 3, :], self.tfi[:, 8, :]]
        ob = self.tfi[:, 0:4, :].rearrange("p a (j e) -> p j a e", e=128)
        sgm = self.tfl[:, 8, 0:128]
        ssq = self.tfl[:, 8, 128:160].rearrange("p (h j) -> p h j", h=4)
        rr = self.tfl[:, 8, 192:224].rearrange("p (h j) -> p h j", h=4)
        jk = self.tfl[:, 8, 256:384]
        lam_init = 0.8 - 0.6 * math.exp(-0.3 * l)
        ts_ = self.bc(sgm, I["diff_subln_2"][l], f1, e="sp")
        ts_ = self.ts(sgm, sgm, 1.0 - lam_init, None, ALU.mult, None, ts_)
        units = [(h, j) for h in range(4) for j in (7, 0, 6, 1, 5, 2, 4, 3)]
        st = [dict() for _ in units]
        p1_free, p2_free, tfree = [None] * 3, [None] * 2, [None] * 2
        scale = 64.0 ** -0.5
        otok = [[] for _ in range(4)]
        on_tok = [[None] * 8 for _ in range(4)]

        def s_qk(i):
            h, j = units[i]
            W = 128 * (j + 1)
            js = slice(j * 128, j * 128 + 128)
            m = st[i]["m"] = self.small(8)
            st[i]["e"] = []
            for mp in range(2):
                b, fw = self.take("s2")
                q = slice(64 * mp, 64 * mp + 64)
                for c in range(0, W, 512):
                    w = min(512, W - c)
                    last = c + w == W
                    t = P.op("pe", lambda e, b=b, c=c, w=w, q=q, last=last: e.matmul(
                        p[:, b[c // 512], 0:w], qT[q, h, js], kT[q, h, c:c + w], start=True, stop=not last,
                        skip_group_check=True), fw, qk_tok["q"][j], qk_tok["k"][:j + 1], mark=False)
                    if last:
                        t = P.op("pe", lambda e, b=b, c=c, w=w: e.matmul(
                            p[:, b[c // 512], w - 128:w], self.idb[:], self.cmask[:], start=False, stop=True,
                            skip_group_check=True), tl)
                sv = p[:, b[0]:b[0] + 2, :].rearrange("p a b -> p (a b)")[:, 0:W]
                t = self.red(m[:, mp:mp + 1], sv, ALU.max, t)
                t = self.ts(m[:, 2 + mp:3 + mp], m[:, mp:mp + 1], -scale, None, ALU.mult, None, t)
                dst, fr = (p1[i % 3], p1_free[i % 3]) if mp == 0 else (p2[i % 2][:], p2_free[i % 2])
                t = self.act(dst[:, 0:W], sv, ACT.Exp, t, fr, f1, scale=scale, bias=m[:, 2 + mp:3 + mp],
                             accum_out=m[:, 4 + mp:5 + mp])
                self.give(b, t)
                st[i]["e"].append(t)

        def s_mix(i):
            h, j = units[i]
            W = 128 * (j + 1)
            m = st[i]["m"]
            t = self.rec(m[:, 6:8], m[:, 4:6], st[i]["e"])
            t2 = self.stt(m[:, 7:8], m[:, 4:5], m[:, 7:8], self.lamt[:, 2:3], ALU.mult, ALU.mult, t, tl)
            a = p1[i % 3][:, 0:W]
            st[i]["a"] = p2_free[i % 2] = self.stt(a, p2[i % 2][:, 0:W], m[:, 7:8], a, ALU.mult, ALU.add, t2)

        def s_tr(i):
            h, j = units[i]
            W = 128 * (j + 1)
            b, fw = self.take("t2")
            for k in range(j + 1):
                x = self.tr(p[:, b[k // 4], k % 4 * 128:k % 4 * 128 + 128], p1[i % 3][:, k * 128:k * 128 + 128], fw,
                            st[i]["a"], mark=(k == j or k == 3))
                if k == min(j, 3):
                    c = [self.copy(aT[i % 2][:, 0:min(W, 512)], p[:, b[0], 0:min(W, 512)], x, tfree[i % 2], f1)]
            p1_free[i % 3] = x
            if W > 512:
                c.append(self.vcopy(aT[i % 2][:, 512:W], p[:, b[1], 0:W - 512], x, tfree[i % 2], f1))
            self.give(b[0:1], c[0])
            self.give(b[1:2], c[-1])
            st[i]["t"] = c

        def s_pv(i):
            h, j = units[i]
            b, fw = self.take("o2")
            o = p[:, b[0], 0:128]
            t = self.mm(o, [(aT[i % 2][:, k * 128:k * 128 + 128], v[:, k, h * 128:h * 128 + 128], v_tok[k])
                            for k in range(j + 1)], fw, st[i]["t"])
            tfree[i % 2] = t
            d = self.act(ob[:, j, h, :], o, ACT.Copy, t, f1, scale=st[i]["m"][:, 6:7])
            d2 = self.act(jk, ob[:, j, h, :], ACT.Square, d, accum_out=ssq[:, h, j:j + 1])
            self.give(b, d)
            otok[h] += [d, d2]

        def head_scale(h):
            t = self.act(rr[:, h], ssq[:, h], ACT.Sqrt, otok[h], scale=1.0 / 128, bias=self.eps[1e-6])
            t = self.rec(rr[:, h], rr[:, h], t)
            for j in range(8):
                on_tok[h][j] = self.stt(ob[:, j, h, :], ob[:, j, h, :], rr[:, h, j:j + 1], sgm, ALU.mult, ALU.mult, t,
                                        ts_)

        nn = len(units)
        ret, pol, out = retention(), pool(), ret_out()
        for i in range(nn + 3):
            if i < nn:
                s_qk(i)
            if 1 <= i <= 25:
                next(ret, None)
            if i in (1, 5, 6, 7, 11, 12, 13):
                next(pol, None)
            if 28 <= i < 32:
                next(out)
                next(out)
            if 1 <= i < nn + 1:
                s_mix(i - 1)
            if 2 <= i < nn + 2:
                s_tr(i - 2)
            if 3 <= i < nn + 3:
                s_pv(i - 3)
                if (i - 3) % 8 == 7:
                    head_scale((i - 3) // 8)
            if i == 26:
                ret_scale()
            if i == 32:
                self.give_back(held[:7], self.fence())
        self.give_back(held[7:], self.fence())
        for q in range(2):
            r = slice(q * 512, q * 512 + 512)
            for h in range(4):
                b, fw = self.take("tr4")
                for k in range(4):
                    t = self.tr(p[:, b[0], k * 128:k * 128 + 128], ob[:, 4 * q + k, h, :], fw, on_tok[h][4 * q + k],
                                mark=(k == 3))
                pair = self.split(self.thi[:, h, r], self.tlo[:, h, r], p[:, b[0], :], t)
                self.give(b, *pair)
                for k in range(4):
                    mix[4 * q + k] += pair

        f5 = self.fence()
        R = self.region(f"m{l}", mod=True)
        z = self.z = R.new("z", [128, 8, 1024])
        g1, g2 = R.new("g1", [128, 1024]), R.new("g2", [128, 1024])
        self.junk = R.new("junk", [128, 1024])
        self.post(R, g1, g2, f5, I["norm_mix_post_2"][l], I["norm_mlp_pre_2"][l], 1 + 2 * l, 2 + 2 * l)
        wo = I["w_out_2"][l]

        def evac(half):
            def f(j, b, src, tok):
                c = slice(half * 512, half * 512 + 512)
                t = self.copy(z[:, j, c], src, tok, f5)
                self.give(b, t)
                self.zt[j].append(t)
                if half == 1:
                    return lambda: self.post_rows(j)
            return f

        for half in range(2):
            self.proj_nat(8, lambda k: [(0, wo[k * 128:k * 128 + 128, half * 512:half * 512 + 512])], 512, self.sels,
                          mix, evac(half), lag=2 * half)
        self.flush()
        self.uT = self.ut

    def tf_off(self):
        return self.t_lo_off - 36864

    def lam(self, l, f0):
        P, I = self.P, self.I
        lq = self.tfl[0:64, 8, 0:8]
        t = []
        names = ("lambda_q1_2", "lambda_k1_2", "lambda_q2_2", "lambda_k2_2")
        for i, nme in enumerate(names):
            t.append(P.dma("act", self.lamt[0:64, 4 + i:5 + i], I[nme][l].rearrange("(p o) -> p o", o=1), f0))
        a = self.tt(self.lamt[0:64, 4:5], self.lamt[0:64, 4:5], self.lamt[0:64, 5:6], ALU.mult, t)
        a2 = self.tt(self.lamt[0:64, 5:6], self.lamt[0:64, 6:7], self.lamt[0:64, 7:8], ALU.mult, t, a)
        b, fw = self.take("proj")
        m = self.mm(self.ps[:, b[0], 0:2], [(self.ones[0:64, :], self.lamt[0:64, 4:6])], fw, a, a2, self.base_tok)
        e = self.act(self.lamt[:, 0:2], self.ps[:, b[0], 0:2], ACT.Exp, m, f0)
        self.give(b, e)
        lam_init = 0.8 - 0.6 * math.exp(-0.3 * l)
        d = self.tt(self.lamt[:, 2:3], self.lamt[:, 1:2], self.lamt[:, 0:1], ALU.subtract, e)
        d = self.ts(self.lamt[:, 2:3], self.lamt[:, 2:3], -lam_init, None, ALU.add, None, d)
        if l == 0:
            cm = self.tfl[:, 8, 512:640]
            c = P.dma("act", cm, I["k_causal"], f0)
            c = self.vcopy(self.cmask[:], cm, c)
            c2 = self.vcopy(self.idb[:], self.ident[:], self.base_tok)
            self.mask_tok = [c, c2]
        return [d, self.mask_tok]

    def post(self, R, g1, g2, f, gpost, gpre, xin, xout):
        self.g1 = (g1, self.bc(g1[:], gpost, f))
        if gpre is not None:
            self.gpre = (g2, self.bc(g2[:], gpre, f))
        self.rows_start(R, f, lambda j: (self.d_x[xin][j], self.d_tok[xin][j]), xout)

    def post_rows(self, j):
        z = self.z[:, j, :]
        ss = self.small(1)
        t = self.act(self.junk[:], z, ACT.Square, self.zt[j], self.pf, accum_out=ss)
        r, t = self.rms_scale(ss, 1024, 1e-6, t)
        t = self.stt(z, z, r, self.g1[0][:], ALU.mult, ALU.mult, t, self.g1[1])
        t = self.tt(z, z, self.xr[j % 2][:], ALU.add, t, self.xt[j])
        self.xf[j % 2] = t
        self.xload(j + 2)
        if self.xout is None:
            return lambda: self.store(j, z, t)
        d = self.pre_rows(j, t)

        def tail():
            self.store(j, z, t)
            self.row_tail(j, self.hb[j % 3][:], d)
        return tail

    def block2_mlp(self, l):
        P, I = self.P, self.I
        f0 = self.fence()
        p = self.ps
        R = self.region(f"f{l}", mod=True)
        z = self.z = R.new("z", [128, 8, 1024])
        gh = [R.new(f"gh{i}", [128, 2, 1024], F32R) for i in range(2)]
        gh_at = (R.off - 16384, R.off - 8192)
        gl = [R.new(f"gl{i}", [128, 2, 1024], F32R) for i in range(2)]
        gl_at = (R.off - 16384, R.off - 8192)
        ta = R.new("ta", [128, 1024])
        tb = R.new("tb", [128, 1024])
        ua = R.new("ua", [128, 1026])
        ub = self.at(f"f{l}_ub", [128, 1026], F32, R.off) if R.off + 4128 <= self.end else None
        assert ub is not None
        cw = self.tfi[:, 8, 0:132].rearrange("p (a b) -> p a b", a=3)
        cb = self.tfi[:, 8, 132:176]
        tcw = P.dma("act", self.tfi[:, 8, 0:176], I["conv"][l], f0)
        tz = [self.zero(ua[:, 0:2], f0), self.zero(ub[:, 0:2], f0)]
        wu, wd = I["w_up_2"][l], I["w_down_2"][l]
        ready = self.uT
        halves = [ready[0:4], ready[4:8]]
        g_tok = {}
        down_tok = {}
        free = {"ua": None, "ub": None, "ta": None, "tb": None}
        for c in range(12):
            if c < 11:
                fo = c * 256
                hold = {}

                def conv(u, name, tile, dst, t):
                    t = self.stt(dst[:], u[:, 1:1025], cw[:, 1, tile:tile + 1], dst[:], ALU.mult, ALU.add, t)
                    t = self.stt(dst[:], u[:, 0:1024], cw[:, 0, tile:tile + 1], dst[:], ALU.mult, ALU.add, t)
                    free[name] = t
                    return t

                def evac(m, hf, b, src, tok, c=c):
                    u, name = (ua, "ua") if m % 2 == 0 else (ub, "ub")
                    t = self.copy(u[:, 2 + hf * 512:2 + hf * 512 + 512], src, tok, free[name], f0)
                    tile = 22 * (m % 2) + 2 * c + m // 2
                    dst = (ta, tb)[m % 2]
                    t2 = self.act(dst[:, hf * 512:hf * 512 + 512], src, ACT.Identity, tok, tcw, tz,
                                  free["t" + name[1]], f0, scale=cw[:, 2, tile:tile + 1], bias=cb[:, tile:tile + 1])
                    self.give(b, t2)
                    hold.setdefault(m, []).extend([t, t2])
                    if hf == 1:
                        return (lambda: rest(m)) if m < 2 else lambda: lambda: rest(m)

                def rest(m, c=c):
                    u, name = (ua, "ua") if m % 2 == 0 else (ub, "ub")
                    ft = 2 * c + m // 2
                    if m % 2 == 0:
                        t = conv(u, name, ft, ta, hold[m])
                        hold["g"] = self.act(ta[:], ta[:], ACT.Gelu_apprx_tanh, t)
                    else:
                        t = conv(u, name, 22 + ft, tb, hold[m])
                        x = c % 2
                        t = self.tt(tb[:], tb[:], ta[:], ALU.mult, t, hold["g"])
                        free["ta"] = t
                        a = self.copy(gh[x][:, m // 2, :], tb[:], t, down_tok.get(c - 2), f0)
                        d = self.tt(gl[x][:, m // 2, :], tb[:], gh[x][:, m // 2, :].bitcast(F32), ALU.subtract, a,
                                    down_tok.get(c - 2), f0)
                        free["tb"] = [a, d]
                        g_tok.setdefault(c, []).append([a, d])

                def src(k):
                    r = slice(k * 128, k * 128 + 128)
                    return [(0, wu[r, fo:fo + 128]), (128, wu[r, 2816 + fo:2816 + fo + 128]),
                            (256, wu[r, fo + 128:fo + 256]), (384, wu[r, 2816 + fo + 128:2816 + fo + 256])]

                self.late_n = 1
                self.proj_T(8, src, 4, halves, evac, ring="all")
                if c == 0:
                    self.flush()
            if c >= 1:
                e = c - 1
                for half in range(2):
                    def evd(j, b, src, tok, half=half, e=e):
                        cc = slice(half * 512, half * 512 + 512)
                        if e == 0:
                            t = self.copy(z[:, j, cc], src, tok, f0)
                        else:
                            t = self.tt(z[:, j, cc], src, z[:, j, cc], ALU.add, tok, self.zt[j][half])
                        self.zt[j][half] = t
                        self.give(b, t)
                        if e == 10 and half == 1:
                            return lambda: self.post_rows(j)
                    if e == 0 and half == 0:
                        self.zt = [[None, None] for _ in range(8)]
                    if e == 10 and half == 0:
                        fe = self.fence()
                        self.junk = ta
                        g1 = tb
                        xr = [self.at(f"h{l}_x", [128, 1024], F32, R.off - 4128),
                              self.at(f"h{l}_y", [128, 1024], F32, R.off)]
                        x = (e + 1) % 2
                        g2, *self.hb = [self.at(f"h{l}_g{i}", [128, 1024], F32, o + 4096 * i2)
                                        for i, (o, i2) in enumerate(((gh_at[x], 0), (gh_at[x], 1), (gl_at[x], 0), (gl_at[x], 1)))]
                        nxt = I["norm_mix_pre_2"][l + 1] if l == 0 else None
                        zt = self.zt
                        self.post(xr, g1, g2, fe, I["norm_mlp_post_2"][l], nxt, 2 + 2 * l, 3 if l == 0 else None)
                        self.zt = zt
                    self.proj_nat(2, lambda k: [(0, wd[e * 256 + k * 128:e * 256 + k * 128 + 128,
                                                      half * 512:half * 512 + 512])], 512, self.sels,
                                  [g_tok[e]] * 8, evd, act=(gh[e % 2], gl[e % 2]),
                                  lag=2 if e == 10 and half == 1 else 0,
                                  ring="proj" if e == 10 and half == 1 else "all")
                if half == 1:
                    self.late_n = None
                down_tok[e] = self.last_mm
        self.flush()
        self.uT = self.ut


def build_program(nc, I, out, stop=9):
    Kernel(nc, I, out, stop).build()


_INS = ["x", "c", "rel_bias", "ada_w", "ada_b", "ln_g", "ln_b", "a_w_in", "a_w_out", "b_w_in", "b_q_norm", "b_w_uq",
        "b_kv_norm", "b_w_ukv", "b_w_out", "norm_mix_pre_2", "norm_mix_post_2", "w_in_2", "lambda_q1_2", "lambda_k1_2",
        "lambda_q2_2", "lambda_k2_2", "diff_subln_2", "ret_norm_2", "pool_w_2", "pool_scale_2", "w_out_2",
        "norm_mlp_pre_2", "norm_mlp_post_2", "w_up_2", "conv_w_2", "conv_b_2", "w_down_2"]


def declare(nc, inputs, stop=9):
    arrays = {n: np.ascontiguousarray(inputs[n]) for n in _INS}
    conv = np.concatenate([arrays.pop("conv_w_2"), arrays.pop("conv_b_2")[:, None]], 1)
    arrays["conv"] = np.ascontiguousarray(conv.reshape(2, 4, 44, 128).transpose(0, 3, 1, 2).reshape(2, 128, 176))
    arrays.update(host_constants())
    I = {n: nc.dram_tensor("in_" + n, list(a.shape), mybir.dt.from_np(a.dtype), kind="ExternalInput").ap()
         for n, a in arrays.items()}
    I["k_decay2"] = I["k_decay"].rearrange("p h q -> p (h q)")
    out = nc.dram_tensor("out_0", [1, 1024, 1024], F32, kind="ExternalOutput").ap()
    build_program(nc, I, out, stop)
    return {"in_" + n: a for n, a in arrays.items()}


def kernel(**inputs):
    import concourse.bacc as bacc
    from concourse.bass_utils import run_bass_kernel_spmd

    nc = bacc.Bacc("TRN2", target_bir_lowering=False, num_devices=1)
    arrays = declare(nc, inputs)
    r = run_bass_kernel_spmd(nc, [arrays], core_ids=[0])
    return r.results[0]["out_0"]
```

```python
import math
from contextlib import ExitStack

import numpy as np

import concourse.bass as bass
from concourse import mybir

F32 = mybir.dt.float32
F32R = mybir.dt.float32r
BF16 = mybir.dt.bfloat16
ALU = mybir.AluOpType
ACT = mybir.ActivationFunctionType
AXX = mybir.AxisListType.X

ALPHA = 4.0 ** 0.25
NS = 11
NMISC = 40
MASKED = -8e30


def host_constants():
    f = np.float32
    c = {}
    c["k_ident"] = np.eye(128, dtype=f)
    oh = np.zeros((32, 3, 512), f)
    mk = np.zeros((6, 3, 512), f)
    for g, dil in enumerate((1, 4, 8)):
        for n in range(512):
            off = n - 256
            if abs(off) > (127 if dil == 8 else 64) or (dil == 8 and off % 2):
                mk[:, g, 511 - n] = MASKED
                continue
            rel = off * dil
            a = abs(rel)
            large = 8 + int(f(np.log(f(max(a, 1)) / f(8))) / f(math.log(128.0)) * f(8))
            b = (16 if rel > 0 else 0) + (a if a < 8 else min(large, 15))
            oh[b, g, 511 - n] = 1.0
    c["k_oh"], c["k_msk"] = oh, mk

    def angles(dim, theta):
        inv = f(theta) ** (-np.arange(0, dim, 2, dtype=f) / f(dim))
        ang = np.arange(1024, dtype=f)[:, None] * inv[None, :].astype(f)
        return np.cos(ang).astype(f), np.sin(ang).astype(f)

    def natural(t):
        return np.ascontiguousarray(t.reshape(8, 128, -1).transpose(1, 0, 2))

    co, si = angles(32, 10000.0)
    c["k_rope"] = np.ascontiguousarray(np.stack([natural(co), natural(si)], 2))
    tab = np.ones((128, 1024), f)
    tab[64:80], tab[80:96] = co.T, co.T
    tab[96:112], tab[112:128] = -si.T, si.T
    c["k_qtab"] = tab
    co, si = angles(16, 500000.0)
    c["k_rope2"] = np.ascontiguousarray(np.stack([natural(co), natural(si)], 2))
    lg = np.log(1.0 - 2.0 ** (-5.0 - np.arange(4))).astype(np.float64)
    idx = np.arange(128)
    sc = 32.0 ** -0.5
    dec = np.zeros((128, 4, 128))
    for h in range(4):
        d = idx[None, :] - idx[:, None]
        dec[:, h, :] = np.where(d >= 0, np.exp(np.maximum(d, 0) * lg[h]), 0.0) * sc
    c["k_decay"] = dec.astype(f)
    hd = np.repeat(np.arange(4), 32)
    c["k_xi"] = np.exp((idx[None, :] + 1.0) * lg[hd][:, None]).astype(f)
    c["k_zeta"] = (np.exp((127.0 - idx[:, None]) * lg[hd][None, :]) * sc).astype(f)
    c["k_cd"] = np.exp(128.0 * lg[hd])[:, None].astype(f)
    c["k_blk"] = (hd[:, None] == np.repeat(np.arange(4), 64)[None, :]).astype(f)
    c["k_causal"] = np.where(idx[None, :] <= idx[:, None], 0.0, -1e30).astype(f)
    w = np.array([[2, 4], [8, 16]])
    inv = np.zeros((128, 2, 17), f)
    for t in range(2):
        for half in range(2):
            ww = w[t, half]
            inv[64 * half:64 * half + 64, t, 0:16] = 1.0 / np.minimum(np.arange(16) + 1.0, ww)
            inv[64 * half:64 * half + 64, t, 16] = 1.0 / ww
    c["k_inv"] = inv
    return c


class Tail:

    def __init__(self, j, f):
        self.j, self.f = j, f

    def __call__(self):
        return self.f()


def flat(waits):
    for w in waits:
        if w is None:
            continue
        if isinstance(w, tuple) and len(w) == 2 and isinstance(w[0], str):
            yield w
        else:
            yield from flat(w)


class Prog:

    def __init__(self, nc, ctx):
        self.q = {e: [] for e in ("pe", "dve", "act", "pool", "sp")}
        self.sem = {e: ctx.enter_context(nc.semaphore("s_" + e)) for e in self.q}
        self.n = {}
        self.nc, self.ctx = nc, ctx
        self.misc = 0
        self.last_misc = {}

    def op(self, e, f, *waits, mark=True):
        tok = None
        if mark:
            self.n[e] = self.n.get(e, 0) + 1
            tok = (e, self.n[e])
        self.q[e].append((list(flat(waits)), f, e if mark else None, 1))
        return tok

    def dma(self, e, out, in_, *waits, sem=None):
        if sem is None:
            sem = f"d{self.misc % NMISC}"
            self.misc += 1
            waits = (*waits, self.last_misc.get(sem))
        if sem not in self.sem:
            self.sem[sem] = self.ctx.enter_context(self.nc.semaphore(sem))
        self.n[sem] = self.n.get(sem, 0) + 16
        tok = (sem, self.n[sem])
        self.last_misc[sem] = tok
        self.q[e].append((list(flat(waits)), lambda eng: eng.dma_start(out, in_), sem, 16))
        return tok

    def emit(self, e, eng):
        seen = {}
        for waits, f, sem, by in self.q[e]:
            for s, v in waits:
                if seen.get(s, 0) < v:
                    eng.wait_ge(self.sem[s], v)
                    seen[s] = v
            ins = f(eng)
            if sem is not None:
                ins.then_inc(self.sem[sem], by)


class Kernel:
    def __init__(self, nc, I, out, stop):
        self.nc, self.I, self.out, self.stop = nc, I, out, stop

    def mm(self, out, terms, *waits):
        last = len(terms) - 1
        for i, t in enumerate(terms):
            tok = self.P.op(
                "pe", lambda e, t=t, i=i: e.matmul(out, t[0], t[1], start=(i == 0), stop=(i == last)),
                waits if i == 0 else None, t[2:], mark=(i == last))
        return tok

    def tr(self, out, in_, *waits, mark=True):
        k = in_.shape[0]
        return self.P.op("pe", lambda e: e.transpose(out, in_, self.ident[0:k, 0:k]), waits, mark=mark)

    def copy(self, out, in_, *waits):
        return self.P.op("act", lambda e: e.activation(out, in_, ACT.Copy), waits)

    def act(self, out, in_, fn, *waits, **kw):
        return self.P.op("act", lambda e: e.activation(out, in_, fn, **kw), waits)

    def vcopy(self, out, in_, *waits):
        return self.P.op("dve", lambda e: e.tensor_copy(out, in_), waits)

    def tt(self, out, a, b, op, *waits, eng="dve"):
        return self.P.op(eng, lambda e: e.tensor_tensor(out, a, b, op), waits)

    def ts(self, out, a, s1, s2, o1, o2, *waits, eng="dve"):
        if o2 is None:
            return self.P.op(eng, lambda e: e.tensor_scalar(out, a, s1, None, o1), waits)
        return self.P.op(eng, lambda e: e.tensor_scalar(out, a, s1, s2, o1, o2), waits)

    def stt(self, out, a, s, b, o1, o2, *waits, eng="dve"):
        return self.P.op(eng, lambda e: e.scalar_tensor_tensor(out=out, in0=a, scalar=s, in1=b, op0=o1, op1=o2),
                         waits)

    def red(self, out, a, op, *waits):
        return self.P.op("dve", lambda e: e.tensor_reduce(out, a, AXX, op), waits)

    def rec(self, out, a, *waits):
        return self.P.op("dve", lambda e: e.reciprocal(out, a), waits)

    def zero(self, out, *waits, value=0.0, eng="dve"):
        return self.P.op(eng, lambda e: e.memset(out, value), waits)

    def at(self, name, shape, dt, off):
        size = int(np.prod(shape[1:])) * (2 if dt == BF16 else 4)
        assert off % 32 == 0 and off + size <= self.end, (name, off, size, self.end)
        return self.nc.alloc_sbuf_tensor_at(name, list(shape), dt, offset=off)

    class Region:
        def __init__(self, k, off, end, tag):
            self.k, self.off, self.end, self.tag = k, off, end, tag

        def new(self, name, shape, dt=F32):
            t = self.k.at(f"{self.tag}_{name}", shape, dt, self.off)
            size = int(np.prod(shape[1:])) * (2 if dt == BF16 else 4)
            self.off += (size + 31) // 32 * 32
            assert self.off <= self.end, (self.tag, name, self.off - self.end)
            return t

    def take(self, ring):
        b = self.rings[ring][self.ring_at.get(ring, 0) % len(self.rings[ring])]
        self.ring_at[ring] = self.ring_at.get(ring, 0) + 1
        n = b if isinstance(b, tuple) else (b,)
        waits = []
        for x in n:
            assert self.free[x] is not None, ("bank in use", ring, x)
            waits.append(self.free[x])
            self.free[x] = None
        return n, waits

    def give(self, banks, *toks):
        for x in banks:
            self.free[x] = list(toks)

    def weight(self, pieces):
        n = self.wn
        self.wn += 1
        s = n % NS
        assert n < NS or self.wfree.get(n - NS) is not None, "slot in use"
        freed = self.wfree.pop(n - NS, None)
        w = 0
        for c, ap in pieces:
            ww = int(np.prod(ap.shape[1:]))
            dst = self.wst[:, s, c:c + ww]
            if len(ap.shape) == 3:
                dst = dst.rearrange("p (a b) -> p a b", a=ap.shape[1])
            t = self.P.dma("sp", dst, ap, freed, sem=f"w{s}")
            w = max(w, c + ww)
        hi = self.P.op("pool", lambda e: e.tensor_copy(self.whi[:, s, 0:w], self.wst[:, s, 0:w]), t)
        lo = self.P.op("pool", lambda e: e.tensor_tensor(
            self.wlo[:, s, 0:w], self.wst[:, s, 0:w], self.whi[:, s, 0:w], ALU.subtract), hi)
        return n, s, lo

    def release(self, ws, tok):
        for n, _, _ in ws:
            self.wfree[n] = tok

    def raw_weight(self, ap):
        n = self.wn
        self.wn += 1
        s = n % NS
        assert n < NS or self.wfree.get(n - NS) is not None, "slot in use"
        t = self.P.dma("sp", self.wst[:, s, :], ap, self.wfree.pop(n - NS, None), sem=f"w{s}")
        return n, s, t

    def borrow(self):
        while self.wn % NS:
            self.wfree[self.wn] = self.wfree.pop(self.wn - NS)
            self.wn += 1
        held = list(range(self.wn, self.wn + NS))
        for n in held:
            assert self.wfree.pop(n - NS) is not None
        self.wn += NS
        return held

    def give_back(self, held, toks):
        for n in held:
            self.wfree[n] = toks

    def tiles(self, nk, src, w, items, terms, ready, evac, ring, lag, nb=4):
        ws = self.ahead + [self.weight(src(k)) for k in range(len(self.ahead), nk)]
        self.ahead = []
        nb = 1 if lag else nb
        for q in range(0, len(items), nb):
            blk = items[q:q + nb]
            banks = [self.take(ring) for _ in blk]
            toks = [None] * len(blk)
            end = q + nb >= len(items)
            for k in range(nk):
                for i, it in enumerate(blk):
                    b, fw = banks[i]
                    for n, (x, y) in enumerate(terms(it, k, ws[k][1])):
                        first, fin = k == 0 and n == 0, k == nk - 1 and n == 2
                        tok = self.P.op(
                            "pe", lambda e, o=self.ps[:, b[0], 0:w], x=x, y=y, first=first, fin=fin:
                            e.matmul(o, x, y, start=first, stop=fin),
                            ws[k][2] if n == 0 else None, self.kready[k] if self.kready and n == 0 else None,
                            (fw, None if self.kready else ready(q + i) if callable(ready) else ready[q + i]) if first else None,
                            mark=fin or (end and n == 2 and i == len(blk) - 1))
                        if fin:
                            toks[i] = tok
                if end:
                    self.wfree[ws[k][0]] = tok
            self.last_mm = tok
            rest = [evac(it, banks[i][0], self.ps[:, banks[i][0][0], 0:w], toks[i]) for i, it in enumerate(blk)]
            self.advance(rest)
            if lag and q == 1:
                self.prefetch()

    def prefetch(self):
        if self.soon is not None:
            while len(self.ahead) < 8 and self.wfree.get(self.wn - NS) is not None:
                self.ahead.append(self.weight(self.soon(len(self.ahead))))
            self.soon = None

    def advance(self, rest):
        if self.late_n:
            self.late[:self.late_n], old = [], self.late[:self.late_n]
            for f in old:
                f()
        else:
            self.late = [g for f in self.late for g in [f()] if g is not None]
        self.late += [g for f in rest if f is not None for g in [f()] if g is not None]

    def flush(self):
        while self.late:
            self.advance([])

    def drain(self):
        while any(not isinstance(f, Tail) or f.j < 5 for f in self.late):
            self.late = [g for f in self.late for g in [f if isinstance(f, Tail) and f.j >= 5 else f()] if g is not None]

    def open(self):
        f = self.fence()
        self.late.append(lambda: f.extend(self.fence()))
        return f

    def proj_nat(self, nk, src, w, sels, ready, evac, act=None, ring="proj", lag=0):
        hi, lo = act or (self.thi, self.tlo)

        def terms(j, k, s):
            h, l = sels[j](hi, k), sels[j](lo, k)
            return (h, self.whi[:, s, 0:w]), (h, self.wlo[:, s, 0:w]), (l, self.whi[:, s, 0:w])

        self.tiles(nk, src, w, list(range(len(sels))), terms, ready, evac, ring, lag)

    def proj_T(self, nk, src, nm, ready, evac, act=None, ring="proj", lag=0, nb=4):
        hi, lo = act or (self.thi, self.tlo)

        def terms(it, k, s):
            c = slice(it[0] * 128, it[0] * 128 + 128)
            r = slice(it[1] * 512, it[1] * 512 + 512)
            return (self.whi[:, s, c], hi[:, k, r]), (self.whi[:, s, c], lo[:, k, r]), (self.wlo[:, s, c], hi[:, k, r])

        items = [(m, hf) for m0 in range(0, nm, 2) for m in range(m0, min(m0 + 2, nm)) for hf in range(2)]
        if nb == 2:
            items = [(m, hf) for m0 in range(0, nm, 2) for hf in range(2) for m in (m0, m0 + 1)]
        half = ready if callable(ready) else lambda hf: ready[hf]
        self.tiles(nk, src, 512, items, terms, lambda i: half(items[i][1]),
                   lambda it, b, ps, tok: evac(it[0], it[1], b, ps, tok), ring, lag, nb)

    def split(self, hi, lo, src, *waits):
        a = self.copy(hi, src, waits)
        d = self.tt(lo, src, hi.bitcast(F32), ALU.subtract, a)
        return a, d

    def to_T(self, blocks, j, tok, ring="tr", kt0=0):
        toks = []
        js = slice(j * 128, j * 128 + 128)
        done = []
        for q in range(0, len(blocks), 4):
            part = blocks[q:q + 4]
            b, fw = self.take(ring)
            for i, blk in enumerate(part):
                t = self.tr(self.ps[:, b[0], i * 128:i * 128 + 128], blk, fw if i == 0 else None, tok,
                            mark=(i == len(part) - 1))
            done.append((q, len(part), b, t))
        for q, n, b, t in done:
            src = self.ps[:, b[0], 0:128 * n].rearrange("p (a b) -> p a b", a=n)
            k = slice(kt0 + q, kt0 + q + n)
            pair = self.split(self.thi[:, k, js], self.tlo[:, k, js], src, t, done[-1][3])
            self.give(b, *pair)
            toks += pair
        return toks

    def small(self, n):
        w = (n + 3) // 4 * 4
        if self.sm_at + w > self.sm_n:
            self.sm_at = 0
        i = self.sm_at
        self.sm_at += w
        return self.sm[:, i:i + n]

    def rms_scale(self, ss, n, eps, tok):
        sd = self.small(ss.shape[1])
        r = self.small(ss.shape[1])
        t = self.act(sd, ss, ACT.Sqrt, tok, scale=1.0 / n, bias=self.eps[eps])
        return r, self.rec(r, sd, t)

    def build(self):
        nc = self.nc
        with ExitStack() as ctx:
            self.ctx = ctx
            P = self.P = Prog(nc, ctx)
            base = (nc.sbuf_base + 31) // 32 * 32
            self.end = nc.sbuf_usable_end // 32 * 32
            self.ps = ctx.enter_context(nc.psum_tensor("ps", [128, 8, 512], F32))
            self.free = {b: [] for b in range(8)}
            self.rings = {"proj": [0, 1, 2, 3], "tr": [4, 5], "tr4": [4, 5, 6, 7], "s1": [0, 1, 2],
                          "t1": [3, 4, 5], "o1": [6, 7], "s2": [(0, 1), (2, 3)], "t2": [(4, 5)], "o2": [6, 7],
                          "all": [0, 1, 2, 3, 4, 5, 6, 7]}
            self.ring_at = {}
            off = base
            self.thi = self.at("thi", [128, 9, 1024], F32R, off)
            self.tfi = self.at("tfi", [128, 9, 1024], F32, off)
            off += 36864
            self.tlo = self.at("tlo", [128, 9, 1024], F32R, off)
            self.tfl = self.at("tfl", [128, 9, 1024], F32, off)
            self.t_lo_off = off
            off += 36864
            self.w_off = off
            self.whi = self.at("whi", [128, NS, 512], F32R, off)
            off += NS * 2048
            self.wlo = self.at("wlo", [128, NS, 512], F32R, off)
            self.wst = self.at("wst", [128, NS, 512], F32, off)
            off += NS * 2048
            self.wn, self.wfree, self.late, self.late_n, self.kready = 0, {}, [], None, None
            self.ahead, self.soon = [], None
            cr = Kernel.Region(self, off, off + 10240, "cst")
            self.ident = cr.new("ident", [128, 128])
            self.ones = cr.new("ones", [128, 128])
            self.sm_n, self.sm_at = 512, 0
            self.sm = cr.new("sm", [128, 16 * 32])
            self.epst = cr.new("eps", [128, 2])
            self.eps = {1e-5: self.epst[:, 0:1], 1e-6: self.epst[:, 1:2]}
            self.rope = cr.new("rope", [128, 8, 2, 16])
            self.rope2 = cr.new("rope2", [128, 8, 2, 8])
            self.idb = cr.new("idb", [128, 128], BF16)
            self.cmask = cr.new("cmask", [128, 128], BF16)
            self.lamt = cr.new("lam", [128, 8])
            self.cc = cr.new("cc", [128, 16])
            self.lamt_va = cr.new("va", [128, 64])
            self.cb = cr.new("cb", [128, 8, 128])
            off += 10240
            mr = Kernel.Region(self, off, off + 16384, "mod")
            self.mod_off = off
            self.gate = [mr.new("g0", [128, 1024]), None]
            self.msh = mr.new("sh", [128, 1024])
            self.msc = mr.new("sc", [128, 1024])
            self.gate[1] = mr.new("g1", [128, 1024])
            off += 16384
            self.gen = off
            self.rot_tok = None

            self.d_y = nc.dram_tensor("scr_y", [1024, 3, 396], F32, kind="Internal").ap()
            self.d_v = nc.dram_tensor("scr_v", [3, 6, 512], F32, kind="Internal").ap()
            self.d_x = [nc.dram_tensor(f"scr_x{i}", [8, 128, 1024], F32, kind="Internal").ap() for i in range(5)]
            self.d_tok = [[None] * 8 for _ in range(5)]
            self.all_dram = []

            self.setup()
            self.block1_a()
            if self.stop > 1:
                self.block1_b()
            for l in range(2):
                if self.stop > 2 + 2 * l:
                    self.block2_mix(l)
                if self.stop > 3 + 2 * l:
                    self.block2_mlp(l)
            self.flush()
            P.op("sp", lambda e: e.nop(), self.all_dram, mark=False)

            block = ctx.enter_context(nc.Block())

            @block.tensor
            def _(e):
                P.emit("pe", e)

            @block.vector
            def _(e):
                P.emit("dve", e)

            @block.scalar
            def _(e):
                P.emit("act", e)

            @block.gpsimd
            def _(e):
                P.emit("pool", e)

            @block.sync
            def _(e):
                P.emit("sp", e)

    def fence(self):
        return [(e, n) for e, n in self.P.n.items() if n]

    def region(self, tag, mod=False):
        return Kernel.Region(self, self.mod_off if mod else self.gen, self.end, tag)

    def bc(self, out, row, *waits, e="act"):
        return self.P.dma(e, out, row.partition_broadcast(128), waits)

    def setup(self):
        P, I = self.P, self.I
        t = [P.dma("act", self.ident[:], I["k_ident"])]
        cT = self.lamt
        tc = P.dma("act", cT[:], I["c"].rearrange("o (p k) -> p (o k)", k=8))
        self.ctok = self.act(self.cc[:, 0:8], cT[:], ACT.Silu, tc)
        for i, l in ((self.rope, "k_rope"), (self.rope2, "k_rope2")):
            t.append(P.dma("act", i[:], I[l]))
        a = self.zero(self.ones[:], value=1.0)
        e1 = self.zero(self.epst[:, 0:1], value=1e-5)
        e2 = self.zero(self.epst[:, 1:2], value=1e-6)
        self.base_tok = [t, a, e1, e2]
        self.cb_tok = self.vcopy(self.cb[:], self.cc[:, 0:8].unsqueeze(2).to_broadcast([128, 8, 128]), self.ctok)

    def ada_start(self, layer, *waits):
        self.mod_dst = [self.msh, self.msc, self.gate[layer]]
        self.mod_bias = [self.bc(d[:], self.I["ada_b"][layer, n * 1024:n * 1024 + 1024], waits) if layer or n == 2 else None
                         for n, d in enumerate(self.mod_dst)]
        self.mod_tok = {0: [], 1: [], 2: []}

    def ada(self, layer, parts):
        src = self.I["ada_w"][layer].rearrange("(p k) n -> p k n", k=8)
        for which, half in parts:
            n = which * 1024 + half * 512
            ws = [self.raw_weight(src[:, k, n:n + 512]) for k in range(8)]
            b, fw = self.take("proj")
            m = self.mm(self.ps[:, b[0], :], [(self.cb[:, k, :], self.wst[:, s, :], t) for k, (_, s, t) in enumerate(ws)],
                        fw, self.cb_tok)
            self.release(ws, m)
            o = self.mod_dst[which][:, half * 512:half * 512 + 512]
            z = self.stt(o, self.ps[:, b[0], :], 1.0 if which == 1 else 0.0, o, ALU.add, ALU.add, m,
                         self.mod_bias[which])
            self.give(b, z)
            self.mod_tok[which].append(z)

    def first_mla(self, k):
        return [(0, self.I["b_w_in"][0][k * 128:k * 128 + 128, 0:416])]

    def first_mix(self, l):
        return lambda k: [(0, self.I["w_in_2"][l][k * 128:k * 128 + 128, 0:512])]

    def up(self, l, c):
        wu = self.I["w_up_2"][l]

        def f(k):
            r, fo = slice(k * 128, k * 128 + 128), c * 256
            return [(0, wu[r, fo:fo + 128]), (128, wu[r, 2816 + fo:2816 + fo + 128]),
                    (256, wu[r, fo + 128:fo + 256]), (384, wu[r, 2816 + fo + 128:2816 + fo + 256])]
        return f

    def block1_a(self):
        P, I = self.P, self.I
        V = Kernel.Region(self, self.mod_off + 4096, self.mod_off + 16384, "tp")
        ohs = V.new("oh", [32, 3, 512])
        mk = V.new("mk", [6, 3, 512])
        rb = self.lamt_va[0:32, 0:18]
        R = self.region("xin")
        xT = R.new("xT", [128, 8, 1024])
        xb = [R.new(f"x{i}", [128, 1024]) for i in range(4)]
        ab = R.new("ab", [16, 128])
        mc = R.new("mc", [128, 16])
        mrow = R.new("mrow", [128, 2048])
        tb = P.dma("act", ab[:], I["ada_b"][0, 0:2048].rearrange("(t p) -> t p", p=128))
        freed = [None] * 4
        xt = []
        for j in range(8):
            x = xb[j % 4]
            t = P.dma("act", x[:], I["x"][0, j * 128:j * 128 + 128, :], freed[j % 4])
            for q in range(2):
                b, fw = self.take("tr4")
                for i in range(4):
                    k = 4 * q + i
                    m = self.tr(self.ps[:, b[0], i * 128:i * 128 + 128], x[:, k * 128:k * 128 + 128], fw, t, self.base_tok,
                                mark=(i == 3))
                d = self.vcopy(xT[:, 4 * q:4 * q + 4, j * 128:j * 128 + 128],
                               self.ps[:, b[0], :].rearrange("p (a b) -> p a b", a=4), m)
                self.give(b, d)
                xt.append(d)
            freed[j % 4] = m
        tv = [P.dma("act", ohs[:], I["k_oh"]), P.dma("act", rb, I["rel_bias"]), P.dma("act", mk[:], I["k_msk"])]
        b, fw = self.take("tr4")
        m = self.tr(self.ps[:, b[0], 0:16], ab[:], fw, tb, self.base_tok)
        d = self.vcopy(mc[:], self.ps[:, b[0], 0:16], m)
        self.give(b, d)
        src = I["ada_w"][0].rearrange("(p k) n -> p k n", k=8)
        ready = []
        for half in range(2):
            ct = []
            for which in range(2):
                n = which * 1024 + half * 512
                ws = [self.raw_weight(src[:, k, n:n + 512]) for k in range(8)]
                b, fw = self.take("proj")
                for k, (_, w, wt) in enumerate(ws):
                    m = P.op("pe", lambda e, b=b, k=k, w=w: e.matmul(
                        self.ps[0:1, b[0], :], self.cc[:, k:k + 1], self.wst[:, w, :], start=(k == 0), stop=(k == 7)),
                        wt, fw, self.ctok)
                    self.release(ws[k:k + 1], m)
                row = mrow[0:1, (2 * half + which) * 512:(2 * half + which) * 512 + 512]
                c = self.copy(row, self.ps[0:1, b[0], :], m)
                self.give(b, c)
                b, fw = self.take("tr4")
                for i in range(4):
                    m = self.mm(self.ps[:, b[0], i:i + 1],
                                [(row[:, i * 128:i * 128 + 128], self.ones[0:1, 0:1])], fw, c, self.base_tok)
                n = which * 8 + half * 4
                o = mc[:, n:n + 4]
                ct.append(self.stt(o, self.ps[:, b[0], 0:4], float(which), o, ALU.add, ALU.add, m, d))
                self.give(b, ct[-1])
            for k in range(half * 4, half * 4 + 4):
                t = self.ts(xT[:, k, :], xT[:, k, :], mc[:, 8 + k:9 + k], mc[:, k:k + 1], ALU.mult, ALU.add, ct, xt)
                ready.append(self.split(self.thi[:, k, :], self.tlo[:, k, :], xT[:, k, :], t))
        halves = [ready, ready]
        self.kready = ready
        self.ada_start(0)

        f0 = self.fence()
        R = self.region("da")
        qT = R.new("q", [128, 3, 1024])
        kT = R.new("k", [128, 3, 1024])
        v = R.new("v", [128, 9, 384])
        sg = R.new("sg", [128, 8, 384])
        bias = R.new("bias", [128, 6, 320])
        yb = [R.new(f"y{i}", [128, 396]) for i in range(2)]
        sb = [R.new(f"s{i}", [128, 256]) for i in range(3)]
        pt = [R.new(f"p{i}", [128, 256]) for i in range(2)]
        f1 = [f0]
        vt = []
        dv = self.d_v

        def toeplitz(g, off0, w):
            a = dv[g]
            return bass.AP(a.tensor, a.offset + 256 - off0 - w, [[1, 128], [512, 6], [1, w]])

        dils = (1, 4, 8)
        win = I["a_w_in"][0]
        units_end = None
        ytok = []
        y_free = [None, None]
        sb_free, pt_free = [None] * 3, [None] * 2
        stn = 0
        for g in range(3):
            dil = dils[g]
            L = 1024 // dil
            fz = [f1, units_end]
            bt = []

            def bias_tile():
                off, w = ((-64, 256), (-128, 320), (0, 128))[g]
                bt.append(P.dma("act", bias[:, :, 0:w], toeplitz(g, off, w), fz, vt))

            if g > 0:
                bias_tile()

            def cols(c0):
                return lambda k: [(0, win[k * 128:k * 128 + 128, c0:c0 + 384])]

            qk_tok = {}

            def evac_T(dst, name):
                def f(m, hf, b, src, tok):
                    if dil == 1:
                        o, s = dst[:, m, hf * 512:hf * 512 + 512], src
                    else:
                        o = dst[:, m, :].rearrange("p (r i) -> p r i", r=dil)[:, :, hf * (L // 2):(hf + 1) * (L // 2)]
                        s = src.rearrange("p (i r) -> p r i", r=dil)
                    t = (self.copy if name == "q" else self.vcopy)(o, s, tok, fz)
                    self.give(b, t)
                    qk_tok.setdefault((name, m), []).append(t)
                return f

            self.proj_T(8, cols(g * 384), 3, halves, evac_T(qT, "q"))
            if g == 0:
                self.kready = None
                self.ada(0, [(2, 0), (2, 1)])
                for n in range(3):
                    b, fw = self.take("proj")
                    m = self.mm(self.ps[0:6, b[0], :], [(rb[:, n * 6:n * 6 + 6], ohs[:, n, :])], fw, tv)
                    d = self.stt(mk[:, n, :], self.ps[0:6, b[0], :], 8.0, mk[:, n, :], ALU.mult, ALU.add, m, tv)
                    self.give(b, d)
                    vt.append(P.dma("act", self.d_v[n], mk[:, n, :], d))
                self.all_dram += vt
                bias_tile()
            self.proj_T(8, cols(1152 + g * 384), 3, halves, evac_T(kT, "k"))

            def rows(t):
                if dil == 1:
                    return lambda a, k: a[:, k, t * 128:t * 128 + 128]
                if dil == 4:
                    r, i0 = t // 2, 128 * (t % 2)
                    return lambda a, k: a[:, k, r + 4 * i0:r + 4 * (i0 + 127) + 1:4]
                return lambda a, k: a[:, k, t:1024:8]

            if g == 0:
                starts = [0, 64, 192, 320, 448, 576, 704, 832, 896]
                vsel = [lambda a, k, s=s: a[:, k, s:s + 128] for s in starts]
            else:
                vsel = [rows(t) for t in range(8)]
            v_tok = [None] * 9

            def evac_v(j, b, src, tok):
                v_tok[j] = self.copy(v[:, j, :], src, tok, fz)
                self.give(b, v_tok[j])

            self.proj_nat(8, cols(2304 + g * 384), 384, vsel, [ready] * 9, evac_v)
            sg_tok = [None] * 8

            def evac_g(j, b, src, tok):
                sg_tok[j] = self.act(sg[:, j, :], src, ACT.Silu, tok, fz)
                self.give(b, sg_tok[j])

            self.proj_nat(8, cols(3456 + g * 384), 384, [rows(t) for t in range(8)], [ready] * 8, evac_g)

            def geometry(j):
                if g == 0:
                    if j == 0:
                        return 0, 192, 64, [(0, 64, 0), (64, 128, 1)]
                    if j == 7:
                        return 832, 192, 0, [(0, 64, 7), (64, 128, 8)]
                    return 128 * j - 64, 256, 0, [(0, 128, j), (128, 128, j + 1)]
                if g == 1:
                    if j % 2 == 0:
                        return 128 * j, 192, 128, [(0, 128, j), (128, 64, j + 1)]
                    return 128 * j - 128, 256, 0, [(0, 128, j - 1), (128, 128, j)]
                return 128 * j, 128, 0, [(0, 128, j)]

            units = [(j, h) for j in range(8) for h in range(6)]
            st = [dict() for _ in units]
            ob = {}

            def s_qk(i):
                j, h = units[i]
                k0, W, _, _ = geometry(j)
                p = slice(64 * (h % 2), 64 * (h % 2) + 64)
                b, fw = self.take("s1")
                st[i]["b"] = b
                st[i]["qk"] = self.mm(self.ps[:, b[0], 0:W],
                                      [(qT[p, h // 2, j * 128:j * 128 + 128], kT[p, h // 2, k0:k0 + W])],
                                      fw, qk_tok["q", h // 2], qk_tok["k", h // 2])

            def s_max(i):
                j, h = units[i]
                _, W, c0, _ = geometry(j)
                b = st[i]["b"]
                y = yb[j % 2]
                s = sb[i % 3]
                n = (256, 320, 128)[g]
                e1 = n - c0 - W
                bv = bias[:, h, n - 1 - c0:e1 - 1 if e1 else None:-1]
                t = P.op("dve", lambda e: e.tensor_tensor_reduce(
                    s[:, 0:W], self.ps[:, b[0], 0:W], bv, -0.125, 3.0e38, ALU.add, ALU.min,
                    y[:, 384 + h:385 + h]), st[i]["qk"], bt, sb_free[i % 3], y_free[j % 2], fz)
                self.give(b, t)
                st[i]["e"] = self.act(s[:, 0:W], s[:, 0:W], ACT.Exp, t, scale=-1.0,
                                      bias=y[:, 384 + h:385 + h], accum_out=y[:, 390 + h:391 + h])

            def s_tr(i):
                j, h = units[i]
                _, W, _, ch = geometry(j)
                b, fw = self.take("t1")
                for n, (c, w, _) in enumerate(ch):
                    t = self.tr(self.ps[0:w, b[0], n * 128:n * 128 + 128], sb[i % 3][:, c:c + w], fw, st[i]["e"],
                                mark=(n == len(ch) - 1))
                sb_free[i % 3] = t
                cp = self.vcopy if i % 2 else self.copy
                rows_ = [w for _, w, _ in ch]
                if min(rows_) == 128 or len(rows_) == 1:
                    x = cp(pt[i % 2][:, 0:128 * len(ch)], self.ps[:, b[0], 0:128 * len(ch)], t, pt_free[i % 2], fz)
                else:
                    for n, w in enumerate(rows_):
                        x = cp(pt[i % 2][0:w, n * 128:n * 128 + 128], self.ps[0:w, b[0], n * 128:n * 128 + 128], t,
                               pt_free[i % 2], fz)
                self.give(b, x)
                st[i]["pt"] = x

            def s_pv(i):
                j, h = units[i]
                _, _, _, ch = geometry(j)
                if h == 0:
                    ob[j] = self.take("o1")
                b, fw = ob[j]
                t = self.mm(self.ps[:, b[0], h * 64:h * 64 + 64],
                            [(pt[i % 2][0:w, n * 128:n * 128 + 128], v[0:w, vt_, h * 64:h * 64 + 64], v_tok[vt_])
                             for n, (_, w, vt_) in enumerate(ch)], fw, st[i]["pt"])
                pt_free[i % 2] = t
                if h == 5:
                    y = yb[j % 2]
                    d = self.tt(y[:, 0:384], self.ps[:, b[0], 0:384], sg[:, j, :], ALU.mult, t, sg_tok[j])
                    self.give(b, d)
                    if dil == 1:
                        dst = self.d_y[j * 128:j * 128 + 128, g, :]
                    elif dil == 4:
                        r, i0 = j // 2, 128 * (j % 2)
                        dst = self.d_y.rearrange("(i r) g n -> r i g n", r=4)[r, i0:i0 + 128, g, :]
                    else:
                        dst = self.d_y.rearrange("(i r) g n -> r i g n", r=8)[j, :, g, :]
                    w = P.dma("act", dst, y[:], d, st[i]["e"])
                    y_free[j % 2] = w
                    ytok.append(w)
                    st[i]["end"] = d

            n = len(units)
            if g == 2:
                self.mod0 = self.mod_tok[2]
                self.ada_start(1, ready, vt)
            for i in range(n + 4):
                if i < n:
                    s_qk(i)
                    s_max(i)
                if g == 2 and i % 10 == 9 and i < 40:
                    self.ada(1, [(i // 20, i // 10 % 2)])
                if 2 <= i < n + 2:
                    s_tr(i - 2)
                if 3 <= i < n + 3:
                    s_pv(i - 3)
            units_end = [st[n - 1]["end"], self.fence()]
        self.all_dram += ytok

        f2 = self.fence()
        R = self.region("mix")
        z = self.z = R.new("z", [128, 8, 1024])
        G = Kernel.Region(self, self.gen, self.gen + 32768, "gt")
        yr = [G.new(f"yr{i}", [128, 1188]) for i in range(3)]
        sa = G.new("sa", [128, 8, 3, 12])
        sl = G.new("sl", [128, 8, 3, 6])
        se = G.new("se", [128, 8, 3, 6])
        s1 = G.new("s1", [128, 8, 6])
        lg = R.new("lg", [128, 1024])
        lb = R.new("lb", [128, 1024])
        fac = self.at("mix_fac", [128, 8, 3, 6], F32, (self.end - 576) // 32 * 32)
        st_ = [P.dma("act", sa[:, :, g, :], self.d_y[:, g, 384:396].rearrange("(j p) n -> p j n", p=128), f2, ytok)
               for g in range(3)]
        self.ada(1, [(2, 0), (2, 1)])
        t = self.act(sl[:], sa[:, :, :, 6:12], ACT.Ln, st_)
        t = self.tt(sl[:], sl[:], sa[:, :, :, 0:6], ALU.subtract, t, st_)
        t = self.tt(s1[:], sl[:, :, 0, :], sl[:, :, 1, :], ALU.max, t)
        t = self.tt(s1[:], s1[:], sl[:, :, 2, :], ALU.max, t)
        t = self.tt(sl[:], sl[:], s1[:].unsqueeze(2).to_broadcast([128, 8, 3, 6]), ALU.subtract, t)
        te = self.act(se[:], sl[:], ACT.Exp, t)
        t = self.tt(s1[:], se[:, :, 0, :], se[:, :, 1, :], ALU.add, te)
        t = self.tt(s1[:], s1[:], se[:, :, 2, :], ALU.add, t)
        t = self.tt(sl[:], sa[:, :, :, 6:12], s1[:].unsqueeze(2).to_broadcast([128, 8, 3, 6]), ALU.mult, t)
        t = self.rec(sl[:], sl[:], t)
        tf = self.tt(fac[:], se[:], sl[:], ALU.mult, t)
        yT = []
        yt = {}

        def yload(j, *w):
            if j < 8:
                yt[j] = P.dma("act", yr[j % 3][:], self.d_y[j * 128:j * 128 + 128].rearrange("p g n -> p (g n)"), f2,
                              ytok, w)

        def scale(j):
            y4 = yr[j % 3][:].rearrange("p (g n) -> p g n", g=3)[:, :, 0:384].rearrange("p g (h e) -> p g h e", h=6)
            return [self.tt(y4[:, g], y4[:, g], fac[:, j, g, :].unsqueeze(2).to_broadcast([128, 6, 64]), ALU.mult,
                            yt[j], tf) for g in range(3)]

        for j in range(3):
            yload(j)
        d = scale(0)
        for j in range(8):
            after = scale(j + 1) if j < 7 else None
            y = yr[j % 3]
            tk = self.to_T([y[:, (q // 3) * 396 + (q % 3) * 128:(q // 3) * 396 + (q % 3) * 128 + 128]
                            for q in range(9)], j, d, ring="tr4")
            d = after
            yload(j + 3, tk)
            yT.append(tk)

        f3 = self.fence()
        tg = [self.bc(lg[:], I["ln_g"][0], f3), self.bc(lb[:], I["ln_b"][0], f3)]
        self.rows_start(R, f3, lambda j: (I["x"][0, j * 128:j * 128 + 128, :], None), 0)
        tmp = R.new("lt", [128, 1024])
        t = self.tt(tmp[:], lb[:], self.msc[:], ALU.mult, tg, f3, self.mod_tok[1])
        t = self.tt(self.msh[:], self.msh[:], tmp[:], ALU.add, t, self.mod_tok[0])
        t2 = self.tt(self.msc[:], self.msc[:], lg[:], ALU.mult, tg, t)
        self.mod_tok[0] = self.mod_tok[1] = [t, t2]
        wo = I["a_w_out"][0]

        def evac(half):
            def f(j, b, src, tok):
                c = slice(half * 512, half * 512 + 512)
                d = self.tt(z[:, j, c], src, self.gate[0][:, c], ALU.mult, tok, f3, self.mod0)
                self.give(b, d)
                self.zt[j].append(d)
                if half == 1:
                    return lambda: self.ln_rows(j, lg, lb, tg)
            return f

        sels = [lambda a, k, j=j: a[:, k, j * 128:j * 128 + 128] for j in range(8)]
        self.sels = sels
        for half in range(2):
            self.soon = self.first_mla if half and self.stop > 1 else None
            self.proj_nat(9, lambda k: [(0, wo[k * 128:k * 128 + 128, half * 512:half * 512 + 512])], 512, sels, yT,
                          evac(half), lag=2 * half)
        self.drain()
        self.uT = self.ut

    def rows_start(self, R, f, xsrc, xout):
        self.xr = R if isinstance(R, list) else [R.new(f"xr{i}", [128, 1024])[:] for i in range(2)]
        self.inplace = isinstance(R, list)
        self.hb = self.xr if self.inplace else [R.new(f"hb{i}", [128, 1024])[:] for i in range(3)]
        self.hfree = [None] * 3
        self.xsrc, self.xout, self.pf = xsrc, xout, f
        self.xt, self.xf = {}, [None] * len(self.xr)
        self.ut, self.zt = [], [[] for _ in range(8)]
        for j in range(len(self.xr)):
            self.xload(j)

    def xload(self, j):
        if j < 8:
            x = j % len(self.xr)
            ap, w = self.xsrc(j)
            self.xt[j] = self.P.dma("act", self.xr[x], ap, self.pf, self.xf[x], w)

    def store(self, j, z, tok):
        w = self.P.dma("act", self.d_x[self.xout][j] if self.xout is not None else
                       self.out[0, j * 128:j * 128 + 128, :], z, tok)
        self.all_dram.append(w)
        if self.xout is not None:
            self.d_tok[self.xout][j] = w

    def row_tail(self, j, z, h, t, stored):
        x = self.to_T([h[:, k * 128:k * 128 + 128] for k in range(8)], j, t, ring="tr4")
        self.store(j, z, stored)
        self.hfree[j % 3] = x
        self.ut.append(x)
        if self.inplace:
            self.xf[j % 3] = x
            self.xload(j + 3)

    def ln_rows(self, j, lg, lb, tg):
        P = self.P
        z = self.z[:, j, :]
        t = self.stt(z, self.xr[j % len(self.xr)], ALPHA, z, ALU.mult, ALU.add, self.zt[j], self.xt[j])
        self.xf[j % len(self.xr)] = t
        st = self.small(12)
        mv = self.small(2)
        a = P.op("dve", lambda e: e.bn_stats(st[:, 0:6], z[:, 0:512]), t)
        b = P.op("dve", lambda e: e.bn_stats(st[:, 6:12], z[:, 512:1024]), t)
        t = P.op("dve", lambda e: e.bn_aggr(mv, st), a, b)
        sd, r = self.small(1), self.small(1)
        self.xload(j + 2)
        s = self.act(sd, mv[:, 1:2], ACT.Sqrt, t, bias=self.eps[1e-5])
        return lambda: self.ln_rows2(j, lg, lb, tg, mv, sd, r, t, s)

    def ln_rows2(self, j, lg, lb, tg, mv, sd, r, t, s):
        z = self.z[:, j, :]
        s = self.rec(r, sd, s)
        nb = self.small(1)
        s = self.stt(nb, mv[:, 0:1], -1.0, r, ALU.mult, ALU.mult, s)
        t = self.act(z, z, ACT.Identity, s, t, scale=r, bias=nb)
        return lambda: self.ln_rows3(j, lg, lb, tg, t)

    def ln_rows3(self, j, lg, lb, tg, t):
        z = self.z[:, j, :]
        h = self.hb[j % 3]
        if self.xout == 0:
            m = self.tt(h, z, self.msc[:], ALU.mult, t, self.mod_tok[1], self.hfree[j % 3], self.pf, eng="pool" if j < 5 else "dve")
            d = self.tt(h, h, self.msh[:], ALU.add, m, self.mod_tok[0])

            def tail():
                x = self.tt(z, z, lg[:], ALU.mult, t, tg, m, eng="pool")
                x = self.tt(z, z, lb[:], ALU.add, x, eng="pool")
                self.row_tail(j, z, h, d, x)
            return Tail(j, tail)
        t = self.tt(z, z, lg[:], ALU.mult, t, tg, eng="pool")
        t = self.tt(z, z, lb[:], ALU.add, t, eng="pool")
        return lambda: self.pre_rows(j, t)

    def pre_rows(self, j, tok):
        z = self.z[:, j, :]
        ss = self.small(1)
        t = self.act(self.junk[:], z, ACT.Square, tok, self.pf, accum_out=ss)
        sd = self.small(1)
        t = self.act(sd, ss, ACT.Sqrt, t, scale=1.0 / 1024, bias=self.eps[1e-6])
        return lambda: self.pre_rows2(j, tok, sd, t)

    def pre_rows2(self, j, stored, sd, t):
        r = self.small(1)
        t = self.rec(r, sd, t)
        h = self.hb[j % 3]
        d = self.stt(h, self.z[:, j, :], r, self.gpre[0][:], ALU.mult, ALU.mult, t, self.gpre[1], self.hfree[j % 3],
                     self.pf)
        return Tail(j, lambda z=self.z[:, j, :]: self.row_tail(j, z, h, d, stored))

    def rotate(self, x1, x2, co, si, tmp, tok):
        a = self.tt(tmp[0], x1, si, ALU.mult, tok, self.rot_tok)
        b = self.tt(tmp[1], x2, si, ALU.mult, tok)
        c = self.tt(x1, x1, co, ALU.mult, a)
        d = self.tt(x2, x2, co, ALU.mult, b)
        c = self.tt(x1, x1, tmp[1], ALU.subtract, c, b)
        d = self.tt(x2, x2, tmp[0], ALU.add, d, a)
        self.rot_tok = [c, d]
        return [c, d]

    def block1_b(self):
        P, I = self.P, self.I
        f0 = self.open()
        R = self.region("mla")
        cqh, cql = R.new("cqh", [128, 2, 1024], F32R), R.new("cql", [128, 2, 1024], F32R)
        ckh, ckl = R.new("ckh", [128, 1, 1024], F32R), R.new("ckl", [128, 1, 1024], F32R)
        kh = [R.new(f"kh{i}", [128, 1024], F32R) for i in range(2)]
        kl = [R.new(f"kl{i}", [128, 1024], F32R) for i in range(2)]
        B = R.off
        v = [R.new(f"v{i}", [128, 8, 128]) for i in range(2)]
        qs = [R.new(f"qs{i}", [128, 512]) for i in range(2)]
        qh, ql = [self.thi[:, 4 + i, :] for i in range(2)], [self.tlo[:, 4 + i, :] for i in range(2)]
        pp = [self.tfi[:, 6 + i, :] for i in range(3)]
        pt = [self.tfl[:, 6 + i, :] for i in range(2)]
        T = Kernel.Region(self, B, self.end, "ml0")
        g0 = T.new("g0", [128, 8, 512])
        cn = [g0[:, j, :] for j in range(8)]
        cfree = [None] * 8
        tmp = T.new("tmp", [128, 4, 16])
        jk = self.msc[:, 384:640]
        qg = self.msc[:, 0:256]
        kg = self.msc[:, 256:384]
        tg = [self.bc(qg, I["b_q_norm"][0], f0), self.bc(kg, I["b_kv_norm"][0], f0)]
        qtab = self.msh
        tq = P.dma("act", qtab[:], I["k_qtab"], f0)
        win = I["b_w_in"][0]
        ready = self.uT
        lat = {"q": [], "c": [], "r": []}

        def evac_c(j, b, src, tok):
            x = cn[j]
            js = slice(j * 128, j * 128 + 128)
            t = self.copy(x[:, 0:416], src, tok, f0)
            self.give(b, t)

            def mid():
                s1, s2 = self.small(1), self.small(1)
                a1 = self.act(jk[:, 0:256], x[:, 0:256], ACT.Square, t, accum_out=s1)
                a2 = self.act(jk[:, 0:128], x[:, 256:384], ACT.Square, t, a1, accum_out=s2)
                r1, t1 = self.rms_scale(s1, 256, 1e-6, a1)
                r2, t2 = self.rms_scale(s2, 128, 1e-6, a2)
                t1 = self.stt(x[:, 0:256], x[:, 0:256], r1, qg, ALU.mult, ALU.mult, t1, tg)
                t2 = self.stt(x[:, 256:384], x[:, 256:384], r2, kg, ALU.mult, ALU.mult, t2, tg)
                ro = self.rotate(x[:, 384:400], x[:, 400:416], self.rope[:, j, 0, :], self.rope[:, j, 1, :],
                                 [tmp[:, i, :] for i in range(4)], [t, self.base_tok])
                t3 = self.vcopy(x[:, 416:448], x[:, 384:416], ro)
                z = self.zero(x[:, 448:512], t)

                def tail():
                    bb, fw = self.take("tr4")
                    for i in range(3):
                        m = self.tr(self.ps[:, bb[0], i * 128:i * 128 + 128], x[:, i * 128:i * 128 + 128], fw, t1, t2,
                                    mark=False)
                    m = P.op("pe", lambda e: e.transpose(self.ps[:, bb[0], 384:512], x[:, 320:448], self.ident[:]), t3, z)
                    p = self.ps
                    pq = p[:, bb[0], 0:256].rearrange("p (a b) -> p a b", a=2)
                    pk = p[:, bb[0], 256:384]
                    cfree[j] = m
                    kr = p[64:128, bb[0], 384:512]
                    k1 = self.copy(kh[0][64:128, js], kr, m, f0)
                    k2 = self.copy(kh[1][64:128, js], kr)
                    a1 = self.copy(cqh[:, :, js], pq)
                    a2 = self.copy(ckh[:, 0, js], pk)
                    k1, k2 = [[k, self.tt(kl[i][64:128, js], kr, kh[i][64:128, js].bitcast(F32), ALU.subtract, k, a1, a2, f0)]
                              for i, k in enumerate((k1, k2))]
                    d1 = self.tt(cql[:, :, js], pq, cqh[:, :, js].bitcast(F32), ALU.subtract, a1, a2)
                    d2 = self.tt(ckl[:, 0, js], pk, ckh[:, 0, js].bitcast(F32), ALU.subtract, a2)
                    q1, q2 = [a1, d1], [a2, d2]
                    self.give(bb, k1, k2, q1, q2)
                    lat["q"].append(q1)
                    lat["c"].append(q2)
                    lat["r"].append([k1, k2])
                return tail
            return mid

        self.proj_nat(8, self.first_mla, 416, self.sels, ready, evac_c)
        gt = [[], []]

        def evac_g(half):
            def f(j, b, src, tok):
                js = slice(j * 128, j * 128 + 128)
                if half == 0:
                    o = g0[:, j, :].rearrange("p (a b) -> p a b", a=4)
                else:
                    o = self.tfi[:, 0:4, js]
                t = self.act(o, src.rearrange("p (a b) -> p a b", a=4), ACT.Silu, tok, f0, cfree[j])
                self.give(b, t)
                gt[half].append(t)
                if half == 1:
                    gt[0][j] = self.P.dma("act", self.tfl[:, 0:4, js], g0[:, j, :].rearrange("p (a b) -> p a b", a=4),
                                          gt[0][j], tok)
            return f

        for half in range(2):
            c0 = 416 + 512 * half
            self.proj_nat(8, lambda k: [(0, win[k * 128:k * 128 + 128, c0:c0 + 512])], 512, self.sels, ready,
                          evac_g(half))

        self.flush()
        f1 = [self.fence()]
        uq = I["b_w_uq"][0]
        ukv = I["b_w_ukv"][0]
        scale = 96.0 ** -0.5
        hs = [[] for _ in range(16)]
        vst = [[] for _ in range(8)]
        kfree, qfree, vfree, sfree = [None, None], [None, None], [None, None], [None, None]
        pfree, tfree = [None] * 3, [None] * 2
        lq = [lat["q"][0:4], lat["q"][4:8]]
        lc = [lat["c"][0:4], lat["c"][4:8]]

        def head(h):
            pc = []
            for k in range(2):
                r = uq[k * 128:k * 128 + 128, h * 96:h * 96 + 96]
                pc += [(k * 128, r), (k * 128 + 96, r[:, 80:96]), (k * 128 + 112, r[:, 64:80])]
            pc.append((256, ukv[:, h * 128:h * 128 + 128]))
            if h % 2 == 0:
                pc.append((384, ukv[:, h * 128 + 64:h * 128 + 128]))
                pc.append((448, ukv[:, h * 128 + 192:h * 128 + 256]))
            w = self.weight(pc)
            _, s, wt = w
            hs[h].append(lat["r"])
            x = h % 2
            for hf in range(2):
                r = slice(hf * 512, hf * 512 + 512)
                b, fw = self.take("o2")
                terms = []
                for k in range(2):
                    c = slice(k * 128, k * 128 + 128)
                    terms += [(self.whi[:, s, c], cqh[:, k, r], wt), (self.whi[:, s, c], cql[:, k, r]),
                              (self.wlo[:, s, c], cqh[:, k, r])]
                m = self.mm(self.ps[:, b[0], :], terms, fw, lq[hf])
                t = self.tt(qs[hf][:], self.ps[:, b[0], :], qtab[:, r], ALU.mult, m, tq, sfree[hf], f1)
                self.give(b, t)
                pair = self.split(qh[x][:, r], ql[x][:, r], qs[hf][:], t, qfree[x], f1)
                sfree[hf] = pair
                hs[h] += pair
                yield
                b, fw = self.take("o2")
                c = slice(256, 384)
                m = self.mm(self.ps[:, b[0], :], [(self.whi[:, s, c], ckh[:, 0, r], wt), (self.whi[:, s, c], ckl[:, 0, r]),
                                                  (self.wlo[:, s, c], ckh[:, 0, r])], fw, lc[hf])
                pair = self.split(kh[x][0:64, r], kl[x][0:64, r], self.ps[0:64, b[0], :], m, kfree[x], f0)
                self.give(b, *pair)
                hs[h] += pair
                yield
            if h % 2 == 0:
                c = slice(384, 512)
                for q in range(2):
                    b, fw = self.take("o2")
                    for i in range(4):
                        j = 4 * q + i
                        js = slice(j * 128, j * 128 + 128)
                        m = self.mm(self.ps[:, b[0], i * 128:i * 128 + 128],
                                    [(ckh[:, 0, js], self.whi[:, s, c], wt), (ckh[:, 0, js], self.wlo[:, s, c]),
                                     (ckl[:, 0, js], self.whi[:, s, c])], fw, lat["c"][j])
                    t = self.copy(v[h // 2 % 2][:, 4 * q:4 * q + 4, :],
                                  self.ps[:, b[0], :].rearrange("p (a b) -> p a b", a=4), m, vfree[h // 2 % 2], f1)
                    self.give(b, t)
                    vst[h // 2].append(t)
                    if q == 0:
                        yield
            self.release([w], m)

        units = [(h, j) for h in range(16) for j in range(8)]
        st = [dict() for _ in units]
        ytok = [[] for _ in range(8)]

        def s_qk(i):
            h, j = units[i]
            x = h % 2
            js = slice(j * 128, j * 128 + 128)
            b, fw = self.take("s2")
            for c in range(2):
                r = slice(c * 512, c * 512 + 512)
                t = self.mm(self.ps[:, b[c], :], [(qh[x][:, js], kh[x][:, r]), (qh[x][:, js], kl[x][:, r]),
                                                  (ql[x][:, js], kh[x][:, r])], fw, hs[h])
            kfree[x] = qfree[x] = t
            st[i]["b"] = b
            sv = ps2(b)
            st[i]["m"] = m = self.small(4)
            t = self.red(m[:, 0:1], sv, ALU.max, t)
            t = self.ts(m[:, 1:2], m[:, 0:1], -scale, None, ALU.mult, None, t)
            t = self.act(pp[i % 3], sv, ACT.Exp, t, pfree[i % 3], f1, scale=scale, bias=m[:, 1:2],
                         accum_out=m[:, 2:3])
            self.give(b, t)
            st[i]["e"] = t

        def ps2(b):
            return self.ps[:, b[0]:b[0] + 2, :].rearrange("p a b -> p (a b)")

        def s_tr(i):
            b, fw = self.take("t2")
            for k in range(8):
                t = self.tr(self.ps[:, b[k // 4], k % 4 * 128:k % 4 * 128 + 128], pp[i % 3][:, k * 128:k * 128 + 128],
                            fw, st[i]["e"], mark=(k % 4 == 3))
                if k == 3:
                    x1 = self.copy(pt[i % 2][:, 0:512], self.ps[:, b[0], :], t, tfree[i % 2], f1)
            x2 = self.vcopy(pt[i % 2][:, 512:1024], self.ps[:, b[1], :], t, tfree[i % 2], f1)
            pfree[i % 3] = t
            self.give(b[0:1], x1)
            self.give(b[1:2], x2)
            m = st[i]["m"]
            st[i]["r"] = self.rec(m[:, 3:4], m[:, 2:3], st[i]["e"])
            st[i]["pt"] = [x1, x2]

        def s_pv(i):
            h, j = units[i]
            b, fw = self.take("o2")
            o = self.ps[:, b[0], 0:64]
            t = self.mm(o, [(pt[i % 2][:, k * 128:k * 128 + 128], v[h // 2 % 2][:, k, h % 2 * 64:h % 2 * 64 + 64])
                            for k in range(8)], fw, st[i]["pt"], vst[h // 2])
            tfree[i % 2] = t
            vfree[h // 2 % 2] = t
            kt = h // 2
            y = (self.tfl if kt < 4 else self.tfi)[:, kt % 4, j * 128 + h % 2 * 64:j * 128 + h % 2 * 64 + 64]
            d = self.stt(y, o, st[i]["m"][:, 3:4], y, ALU.mult, ALU.mult, t, st[i]["r"], gt[0][j], gt[1][j])
            self.give(b, d)
            ytok[j].append(d)

        n = len(units)
        for _ in head(0):
            pass
        pieces = iter(())
        for i in range(n + 3):
            if i < n:
                if i % 8 == 0:
                    pieces = head(i // 8 + 1) if i // 8 < 15 else iter(())
                s_qk(i)
            if 2 <= i < n + 2:
                s_tr(i - 2)
            if i % 8 < 7:
                next(pieces, None)
            if 3 <= i < n + 3:
                s_pv(i - 3)

        yT = []
        for j in range(8):
            js = slice(j * 128, j * 128 + 128)
            blocks = [(self.tfl if k < 4 else self.tfi)[:, k % 4, js] for k in range(8)]
            yT.append(self.to_T(blocks, j, ytok[j], ring="tr4"))

        f2 = self.fence()
        R = self.region("mlo")
        z = self.z = R.new("z", [128, 8, 1024])
        lg, lb = R.new("lg", [128, 1024]), R.new("lb", [128, 1024])
        self.junk, gp = self.msc, self.msh
        self.gpre = (gp, self.bc(gp[:], I["norm_mix_pre_2"][0], f2))
        tg = [self.bc(lg[:], I["ln_g"][1], f2), self.bc(lb[:], I["ln_b"][1], f2)]
        self.rows_start(R, f2, lambda j: (self.d_x[0][j], self.d_tok[0][j]), 1)
        wo = I["b_w_out"][0]

        def evac(half):
            def f(j, b, src, tok):
                c = slice(half * 512, half * 512 + 512)
                d = self.tt(z[:, j, c], src, self.gate[1][:, c], ALU.mult, tok, f2, self.mod_tok[2])
                self.give(b, d)
                self.zt[j].append(d)
                if half == 1:
                    return lambda: self.ln_rows(j, lg, lb, tg)
            return f

        for half in range(2):
            self.soon = self.first_mix(0) if half and self.stop > 2 else None
            self.proj_nat(8, lambda k: [(0, wo[k * 128:k * 128 + 128, half * 512:half * 512 + 512])], 512, self.sels,
                          yT, evac(half), lag=2 * half)
        self.drain()
        self.uT = self.ut

    def block2_mix(self, l):
        P, I = self.P, self.I
        f0 = self.open()
        p = self.ps
        R = self.region(f"c{l}", mod=True)
        qT, kT = R.new("q", [128, 4, 1024]), R.new("k", [128, 4, 1024])
        v = R.new("v", [128, 8, 512])
        C0 = R.off
        rn = R.new("rn", [128, 8, 512])
        gr = R.new("gr", [128, 8, 256])
        pu = R.new("pu", [128, 2, 1040])
        nt = [rn[:, i, :] for i in range(8)]
        tmp = self.tfl[:, 8, 512:1024].rearrange("p (a b) -> p a b", a=4)
        win = I["w_in_2"][l]
        nfree = [None] * 8
        ready = self.uT
        qk_tok = {"q": [], "k": []}

        def cols(c0, w=512):
            return lambda k: [(0, win[k * 128:k * 128 + 128, c0:c0 + w])]

        def evac_qk(dst, name):
            def f(j, b, src, tok):
                i = j
                x = nt[i]
                js = slice(j * 128, j * 128 + 128)
                t = self.copy(x, src, tok, nfree[i], f0)
                self.give(b, t)
                xv = x.rearrange("p (m e) -> p m e", e=64)
                co = self.rope2[:, j, 0:1, :].to_broadcast([128, 8, 8])
                si = self.rope2[:, j, 1:2, :].to_broadcast([128, 8, 8])
                tv = [tmp[:, a, 0:64].rearrange("p (m e) -> p m e", e=8) for a in range(4)]
                def mid():
                    d = self.rotate(xv[:, :, 0:8], xv[:, :, 8:16], co, si, tv, [t, f0])

                    def tail():
                        b, fw = self.take("tr4")
                        for h in range(4):
                            m = self.tr(p[:, b[0], h * 128:h * 128 + 128], x[:, h * 128:h * 128 + 128], fw, d,
                                        mark=(h == 3))
                        nfree[i] = m
                        c = self.copy(dst[:, :, js], p[:, b[0], :].rearrange("p (a b) -> p a b", a=4), m, f0)
                        self.give(b, c)
                        qk_tok[name].append(c)
                    return tail
                return mid
            return f

        self.proj_nat(8, cols(0), 512, self.sels, ready, evac_qk(qT, "q"))
        tl = self.lam(l, f0)
        self.proj_nat(8, cols(512), 512, self.sels, ready, evac_qk(kT, "k"))
        v_tok, r_tok, g_tok = [], [], []

        def evac_v(j, b, src, tok):
            t = self.copy(v[:, j, :], src, tok, f0)
            self.give(b, t)
            v_tok.append(t)

        self.proj_nat(8, cols(1024), 512, self.sels, ready, evac_v)

        def evac_r(j, b, src, tok):
            t = self.copy(rn[:, j, :], src, tok, f0, nfree[j])
            self.give(b, t)
            xv = rn[:, j, 0:256].rearrange("p (m e) -> p m e", e=32)
            co = self.rope[:, j, 0:1, :].to_broadcast([128, 8, 16])
            si = self.rope[:, j, 1:2, :].to_broadcast([128, 8, 16])
            tv = [tmp[:, a, :].rearrange("p (m e) -> p m e", e=16) for a in range(4)]
            r_tok.append([t, self.rotate(xv[:, :, 0:16], xv[:, :, 16:32], co, si, tv, [t, f0])])

        self.proj_nat(8, cols(1536), 512, self.sels, ready, evac_r)

        def evac_g(j, b, src, tok):
            t = self.act(gr[:, j, :], src, ACT.Silu, tok, f0)
            self.give(b, t)
            g_tok.append(t)

        self.proj_nat(8, cols(2048, 256), 256, self.sels, ready, evac_g)
        pu_tok = [self.zero(pu[:, :, 0:16], f0)]

        def evac_p(m, hf, b, src, tok):
            t = self.copy(pu[:, m, 16 + hf * 512:16 + hf * 512 + 512], src, tok, f0)
            self.give(b, t)
            pu_tok.append(t)

        self.proj_T(8, cols(2304, 256), 2, [ready[0:4], ready[4:8]], evac_p)

        self.flush()
        f1 = self.fence()
        held = self.borrow()
        S = Kernel.Region(self, self.w_off, self.w_off + NS * 2048, f"r{l}")
        lo = self.w_off + NS * 2048
        S2 = Kernel.Region(self, lo, lo + 7 * 2048, f"s{l}")
        S3 = Kernel.Region(self, lo + 7 * 2048, lo + 11 * 2048, f"p{l}")
        dec = S.new("dec", [128, 512])
        xi, ze, blk, cd = S.new("xi", [128, 128]), S.new("ze", [128, 128]), S.new("blk", [128, 256]), S.new("cd", [128, 8])
        inv = S.new("inv", [128, 2, 17])
        rg = S.new("rg", [128, 256])
        pw = S.new("pw", [128, 2, 128])
        psc = S.new("psc", [128, 8])
        tc = [P.dma("sp", a, I[b], f1) for a, b in (
            (dec[:], "k_decay2"), (xi[:], "k_xi"), (ze[:], "k_zeta"), (blk[:], "k_blk"), (cd[:, 0:1], "k_cd"),
            (inv[:], "k_inv"))]
        tc.append(self.bc(rg[:], I["ret_norm_2"][l], f1, e="sp"))
        tz = self.zero(pw[:], f1)
        tp = []
        for g in range(4):
            q = 64 * (g % 2)
            tp.append(P.dma("sp", pw[q:q + 64, g // 2, q:q + 64], I["pool_w_2"][l, g], tz))
        for t in range(2):
            tp.append(P.dma("sp", psc[:, t:t + 1], I["pool_scale_2"][l, t * 128:t * 128 + 128].rearrange("(p o) -> p o", o=1), f1))
        kt_ = [S.new(f"kt{i}", [128, 128]) for i in range(2)]
        qx = [S.new(f"qx{i}", [128, 128]) for i in range(2)]
        kz = [S.new(f"kz{i}", [128, 128]) for i in range(2)]
        um = S.new("um", [128, 256])
        sq = S.new("sq", [128, 256])
        state = [S.new(f"st{i}", [128, 256]) for i in range(2)]
        qb = [S.new(f"qb{i}", [128, 512]) for i in range(2)]
        it = [S.new(f"it{i}", [128, 512]) for i in range(2)]
        wa = S2.new("wa", [128, 1040])
        wb = S2.new("wb", [128, 1040])
        zq = [self.zero(q[:], f1) for q in qb]
        zs = self.zero(state[0][:], f1)
        tw = [self.zero(wa[:, 0:16], f1), self.zero(wb[:, 0:16], f1)]
        mix = [[] for _ in range(8)]
        rt = {"st": zs, "o": [], "n": []}
        va, sd = self.lamt_va[:, 0:32], self.lamt_va[:, 32:64]
        on = [rn[:, i, 256:512] for i in range(8)]

        def retention():
            it_free, qb_free, x_free = [None, None], [None, None], [None, None]
            for i in range(8):
                a = i % 2
                b, fw = self.take("o2")
                m = self.tr(p[:, b[0], 0:128], rn[:, i, 0:128], fw, r_tok[i], mark=False)
                m = self.tr(p[:, b[0], 128:256], rn[:, i, 128:256])
                t1 = self.copy(kt_[a][:], p[:, b[0], 128:256], m, x_free[a], f1)
                tq = []
                for h in range(4):
                    hp = slice(32 * h, 32 * h + 32)
                    tq.append(self.copy(qb[a][hp, h * 128:h * 128 + 128], p[hp, b[0], 0:128], m, zq[a], qb_free[a]))
                t2 = self.tt(qx[a][:], p[:, b[0], 0:128], xi[:], ALU.mult, m, tq, tc, x_free[a], f1)
                self.give(b, t1, tq, t2)
                t3 = self.tt(kz[a][:], rn[:, i, 128:256], ze[:], ALU.mult, r_tok[i], tc, x_free[a], f1)
                yield
                b, fw = self.take("o2")
                m = self.mm(p[:, b[0], :], [(kt_[a][:], qb[a][:])], fw, t1, tq)
                qb_free[a] = m
                t4 = self.tt(it[a][:], p[:, b[0], :], dec[:], ALU.mult, m, tc, it_free[a], f1)
                self.give(b, t4)
                yield
                b, fw = self.take("o2")
                cross = P.op("pe", lambda e, b=b, a=a, s=state[i % 2]: e.matmul(
                    p[:, b[0], 0:256], qx[a][:], s[:], start=True, stop=False, skip_group_check=True),
                    fw, t2, rt["st"], mark=True)
                for h in range(4):
                    m = P.op("pe", lambda e, b=b, a=a, h=h, i=i: e.matmul(
                        p[:, b[0], h * 64:h * 64 + 64], it[a][:, h * 128:h * 128 + 128],
                        rn[:, i, 256 + h * 64:320 + h * 64], start=False, stop=(h == 3), skip_group_check=True),
                        t4, r_tok[i], mark=(h == 3))
                it_free[a] = m
                if i < 7:
                    b2, fw = self.take("o2")
                    m2 = self.mm(p[:, b2[0], 0:256], [(kz[a][:], rn[:, i, 256:512])], fw, t3)
                    x_free[a] = [m2, cross]
                    t = self.tt(um[:], p[:, b2[0], 0:256], blk[:], ALU.mult, m2, tc, rt["st"])
                    self.give(b2, t)
                    rt["st"] = self.stt(state[1 - a][:], state[a][:], cd[:, 0:1], um[:], ALU.mult, ALU.add, t,
                                        rt["st"], zs, cross)
                    m = m2
                t = self.copy(on[i], p[:, b[0], 0:256], m)
                self.give(b, t)
                o3 = on[i].rearrange("p (h e) -> p h e", h=4)
                q3 = sq[:].rearrange("p (h e) -> p h e", h=4)
                mu = self.small(4)
                t = self.red(mu, o3, ALU.add, t)
                t = self.ts(mu, mu, 1.0 / 64, None, ALU.mult, None, t)
                t = self.tt(o3, o3, mu.unsqueeze(2).to_broadcast([128, 4, 64]), ALU.subtract, t)
                t2 = self.tt(q3, o3, o3, ALU.mult, t, rt["n"][-1:], f1)
                rt["n"].append(self.red(va[:, i * 4:i * 4 + 4], q3, ALU.add, t2))
                rt["o"].append(t)
                yield

        def ret_scale():
            t = self.act(sd, va, ACT.Sqrt, rt["n"], scale=1.0 / 64, bias=self.eps[1e-6])
            tr_ = self.rec(va, sd, t)
            for i in range(8):
                o3 = on[i].rearrange("p (h e) -> p h e", h=4)
                t = self.tt(o3, o3, va[:, i * 4:i * 4 + 4].unsqueeze(2).to_broadcast([128, 4, 64]), ALU.mult, tr_,
                            rt["o"][i])
                t = self.tt(on[i], on[i], rg[:], ALU.mult, t, tc, eng="pool")
                rt["o"][i] = self.tt(on[i], on[i], gr[:, i, :], ALU.mult, t, g_tok, eng="pool")

        def ret_out():
            for j in range(8):
                mix[j] += self.to_T([on[j][:, 0:128], on[j][:, 128:256]], j, rt["o"][j], kt0=4, ring="o2")
                yield

        def pool():
            lastp = None
            t = [tw, pu_tok]
            for m_ in range(2):
                u = pu[:, m_, :]

                def add(o, x, y, *w):
                    return self.tt(o, x, y, ALU.add, w, eng="pool")

                def cp(o, x, *w):
                    return self.P.op("pool", lambda e: e.tensor_copy(o, x), w)

                a = add(wa[:, 16:1040], u[:, 16:1040], u[:, 15:1039], t, lastp, f1)
                if m_ == 0:
                    b2 = add(wb[64:128, 16:1040], wa[64:128, 16:1040], wa[64:128, 14:1038], a, tw)
                    b1 = cp(wb[0:64, 16:1040], wa[0:64, 16:1040], a, tw)
                else:
                    b1 = add(wb[:, 16:1040], wa[:, 16:1040], wa[:, 14:1038], a, tw)
                    a = add(wa[:, 16:1040], wb[:, 16:1040], wb[:, 12:1036], b1)
                    b2 = add(wb[64:128, 16:1040], wa[64:128, 16:1040], wa[64:128, 8:1032], a)
                    b1 = cp(wb[0:64, 16:1040], wa[0:64, 16:1040], a)
                pl = wa[:, 16:1040]
                mul = ALU.mult
                t1 = self.tt(pl[:, 16:1024], wb[:, 32:1040], inv[:, m_, 16:17].to_broadcast([128, 1008]), mul, b1, b2, tc,
                             eng="pool")
                t2 = self.tt(pl[:, 0:16], wb[:, 16:32], inv[:, m_, 0:16], mul, b1, b2, tc, eng="pool")
                t1 = self.tt(pl, pl, u[:, 16:1040], ALU.subtract, t1, t2, eng="pool")
                yield
                for hf in range(2):
                    r = slice(hf * 512, hf * 512 + 512)
                    b, fw = self.take("o2")
                    mm_ = self.mm(p[:, b[0], :], [(pw[:, m_, :], pl[:, r])], fw, t1, tp)
                    s = self.act(self.thi[:, 6 + m_, r], p[:, b[0], :], ACT.Copy, mm_, tp, scale=psc[:, m_:m_ + 1])
                    d = self.stt(self.tlo[:, 6 + m_, r], p[:, b[0], :], psc[:, m_:m_ + 1],
                                 self.thi[:, 6 + m_, r].bitcast(F32), ALU.mult, ALU.subtract, s, tp)
                    self.give(b, d)
                    for j in range(4):
                        mix[4 * hf + j] += [s, d]
                    lastp = mm_
                    yield

        p1 = [self.tfl[:, i, :] for i in range(3)]
        p2 = [S3.new(f"p{i}", [128, 1024]) for i in range(2)]
        aT = [self.tfl[:, 3, :], self.tfi[:, 8, :]]
        ob = self.tfi[:, 0:4, :].rearrange("p a (j e) -> p j a e", e=128)
        sgm = self.tfl[:, 8, 0:128]
        ssq = self.tfl[:, 8, 128:160].rearrange("p (h j) -> p h j", h=4)
        rr = self.tfl[:, 8, 192:224].rearrange("p (h j) -> p h j", h=4)
        jk = self.tfl[:, 8, 256:384]
        lam_init = 0.8 - 0.6 * math.exp(-0.3 * l)
        ts_ = self.bc(sgm, I["diff_subln_2"][l], f1, e="sp")
        ts_ = self.ts(sgm, sgm, 1.0 - lam_init, None, ALU.mult, None, ts_)
        units = [(h, j) for h in range(4) for j in range(7, -1, -1)]
        st = [dict() for _ in units]
        p1_free, p2_free, tfree = [None] * 3, [None] * 2, [None] * 2
        scale = 64.0 ** -0.5
        otok = [[] for _ in range(4)]
        on_tok = [[None] * 8 for _ in range(4)]

        def s_qk(i):
            h, j = units[i]
            W = 128 * (j + 1)
            js = slice(j * 128, j * 128 + 128)
            m = st[i]["m"] = self.small(8)
            st[i]["e"] = []
            for mp in range(2):
                b, fw = self.take("s2")
                q = slice(64 * mp, 64 * mp + 64)
                for c in range(0, W, 512):
                    w = min(512, W - c)
                    last = c + w == W
                    t = P.op("pe", lambda e, b=b, c=c, w=w, q=q, last=last: e.matmul(
                        p[:, b[c // 512], 0:w], qT[q, h, js], kT[q, h, c:c + w], start=True, stop=not last,
                        skip_group_check=True), fw, qk_tok["q"][j], qk_tok["k"][:j + 1], mark=False)
                    if last:
                        t = P.op("pe", lambda e, b=b, c=c, w=w: e.matmul(
                            p[:, b[c // 512], w - 128:w], self.idb[:], self.cmask[:], start=False, stop=True,
                            skip_group_check=True), tl)
                sv = p[:, b[0]:b[0] + 2, :].rearrange("p a b -> p (a b)")[:, 0:W]
                t = self.red(m[:, mp:mp + 1], sv, ALU.max, t)
                t = self.ts(m[:, 2 + mp:3 + mp], m[:, mp:mp + 1], -scale, None, ALU.mult, None, t)
                dst, fr = (p1[i % 3], p1_free[i % 3]) if mp == 0 else (p2[i % 2][:], p2_free[i % 2])
                t = self.act(dst[:, 0:W], sv, ACT.Exp, t, fr, f1, scale=scale, bias=m[:, 2 + mp:3 + mp],
                             accum_out=m[:, 4 + mp:5 + mp])
                self.give(b, t)
                st[i]["e"].append(t)

        def s_mix(i):
            h, j = units[i]
            W = 128 * (j + 1)
            m = st[i]["m"]
            t = self.rec(m[:, 6:8], m[:, 4:6], st[i]["e"])
            t2 = self.stt(m[:, 7:8], m[:, 4:5], m[:, 7:8], self.lamt[:, 2:3], ALU.mult, ALU.mult, t, tl)
            a = p1[i % 3][:, 0:W]
            st[i]["a"] = p2_free[i % 2] = self.stt(a, p2[i % 2][:, 0:W], m[:, 7:8], a, ALU.mult, ALU.add, t2)

        def s_tr(i):
            h, j = units[i]
            W = 128 * (j + 1)
            b, fw = self.take("t2")
            for k in range(j + 1):
                x = self.tr(p[:, b[k // 4], k % 4 * 128:k % 4 * 128 + 128], p1[i % 3][:, k * 128:k * 128 + 128], fw,
                            st[i]["a"], mark=(k == j or k == 3))
                if k == min(j, 3):
                    c = [self.copy(aT[i % 2][:, 0:min(W, 512)], p[:, b[0], 0:min(W, 512)], x, tfree[i % 2], f1)]
            p1_free[i % 3] = x
            if W > 512:
                c.append(self.vcopy(aT[i % 2][:, 512:W], p[:, b[1], 0:W - 512], x, tfree[i % 2], f1))
            self.give(b[0:1], c[0])
            self.give(b[1:2], c[-1])
            st[i]["t"] = c

        def s_pv(i):
            h, j = units[i]
            b, fw = self.take("o2")
            o = p[:, b[0], 0:128]
            t = self.mm(o, [(aT[i % 2][:, k * 128:k * 128 + 128], v[:, k, h * 128:h * 128 + 128], v_tok[k])
                            for k in range(j + 1)], fw, st[i]["t"])
            tfree[i % 2] = t
            d = self.act(ob[:, j, h, :], o, ACT.Copy, t, f1, scale=st[i]["m"][:, 6:7])
            d2 = self.act(jk, ob[:, j, h, :], ACT.Square, d, accum_out=ssq[:, h, j:j + 1])
            self.give(b, d)
            otok[h] += [d, d2]

        def head_scale(h):
            t = self.act(rr[:, h], ssq[:, h], ACT.Sqrt, otok[h], scale=1.0 / 128, bias=self.eps[1e-6])
            t = self.rec(rr[:, h], rr[:, h], t)
            for j in range(8):
                on_tok[h][j] = self.stt(ob[:, j, h, :], ob[:, j, h, :], rr[:, h, j:j + 1], sgm, ALU.mult, ALU.mult, t,
                                        ts_)

        nn = len(units)
        ret, pol, out = retention(), pool(), ret_out()
        for i in range(nn + 3):
            if i < nn:
                s_qk(i)
            if 1 <= i <= 25:
                next(ret, None)
            if i in (1, 5, 6, 7, 11, 12, 13):
                next(pol, None)
            if 28 <= i < 32:
                next(out)
                next(out)
            if 1 <= i < nn + 1:
                s_mix(i - 1)
            if 2 <= i < nn + 2:
                s_tr(i - 2)
            if 3 <= i < nn + 3:
                s_pv(i - 3)
                if (i - 3) % 8 == 7:
                    head_scale((i - 3) // 8)
            if i == 26:
                ret_scale()
            if i == 32:
                self.give_back(held[:7], self.fence())
        self.give_back(held[7:], self.fence())
        for q in range(2):
            r = slice(q * 512, q * 512 + 512)
            for h in range(4):
                b, fw = self.take("tr4")
                for k in range(4):
                    t = self.tr(p[:, b[0], k * 128:k * 128 + 128], ob[:, 4 * q + k, h, :], fw, on_tok[h][4 * q + k],
                                mark=(k == 3))
                pair = self.split(self.thi[:, h, r], self.tlo[:, h, r], p[:, b[0], :], t)
                self.give(b, *pair)
                for k in range(4):
                    mix[4 * q + k] += pair

        f5 = self.fence()
        R = self.region(f"m{l}", mod=True)
        z = self.z = R.new("z", [128, 8, 1024])
        g1, g2 = R.new("g1", [128, 1024]), R.new("g2", [128, 1024])
        self.junk = R.new("junk", [128, 1024])
        self.post(R, g1, g2, f5, I["norm_mix_post_2"][l], I["norm_mlp_pre_2"][l], 1 + 2 * l, 2 + 2 * l)
        wo = I["w_out_2"][l]

        def evac(half):
            def f(j, b, src, tok):
                c = slice(half * 512, half * 512 + 512)
                t = self.copy(z[:, j, c], src, tok, f5)
                self.give(b, t)
                self.zt[j].append(t)
                if half == 1:
                    return lambda: self.post_rows(j)
            return f

        for half in range(2):
            self.soon = self.up(l, 0) if half and self.stop > 3 + 2 * l else None
            self.proj_nat(8, lambda k: [(0, wo[k * 128:k * 128 + 128, half * 512:half * 512 + 512])], 512, self.sels,
                          mix, evac(half), lag=2 * half)
        self.drain()
        self.uT = self.ut

    def tf_off(self):
        return self.t_lo_off - 36864

    def lam(self, l, f0):
        P, I = self.P, self.I
        t = []
        names = ("lambda_q1_2", "lambda_k1_2", "lambda_q2_2", "lambda_k2_2")
        for i, nme in enumerate(names):
            t.append(P.dma("act", self.lamt[0:64, 4 + i:5 + i], I[nme][l].rearrange("(p o) -> p o", o=1), f0))
        a = self.tt(self.lamt[0:64, 4:5], self.lamt[0:64, 4:5], self.lamt[0:64, 5:6], ALU.mult, t)
        a2 = self.tt(self.lamt[0:64, 5:6], self.lamt[0:64, 6:7], self.lamt[0:64, 7:8], ALU.mult, t, a)
        b, fw = self.take("proj")
        m = self.mm(self.ps[:, b[0], 0:2], [(self.ones[0:64, :], self.lamt[0:64, 4:6])], fw, a, a2, self.base_tok)
        e = self.act(self.lamt[:, 0:2], self.ps[:, b[0], 0:2], ACT.Exp, m, f0)
        self.give(b, e)
        lam_init = 0.8 - 0.6 * math.exp(-0.3 * l)
        d = self.tt(self.lamt[:, 2:3], self.lamt[:, 1:2], self.lamt[:, 0:1], ALU.subtract, e)
        d = self.ts(self.lamt[:, 2:3], self.lamt[:, 2:3], -lam_init, None, ALU.add, None, d)
        if l == 0:
            cm = self.tfl[:, 8, 0:128]
            c = P.dma("act", cm, I["k_causal"], f0)
            c = self.vcopy(self.cmask[:], cm, c)
            c2 = self.vcopy(self.idb[:], self.ident[:], self.base_tok)
            self.mask_tok = [c, c2]
        return [d, self.mask_tok]

    def post(self, R, g1, g2, f, gpost, gpre, xin, xout):
        self.g1 = (g1, self.bc(g1[:], gpost, f))
        if gpre is not None:
            self.gpre = (g2, self.bc(g2[:], gpre, f))
        self.rows_start(R, f, lambda j: (self.d_x[xin][j], self.d_tok[xin][j]), xout)

    def post_rows(self, j):
        ss, sd = self.small(1), self.small(1)
        t = self.act(self.junk[:], self.z[:, j, :], ACT.Square, self.zt[j], self.pf, accum_out=ss)
        t = self.act(sd, ss, ACT.Sqrt, t, scale=1.0 / 1024, bias=self.eps[1e-6])
        return lambda: self.post_rows2(j, sd, t)

    def post_rows2(self, j, sd, t):
        z = self.z[:, j, :]
        r = self.small(1)
        t = self.rec(r, sd, t)
        t = self.stt(z, z, r, self.g1[0][:], ALU.mult, ALU.mult, t, self.g1[1])
        t = self.tt(z, z, self.xr[j % len(self.xr)], ALU.add, t, self.xt[j])
        self.xf[j % len(self.xr)] = t
        if self.xout is None:
            self.xload(j + 3)
            return lambda: self.store(j, z, t)
        if not self.inplace:
            self.xload(j + 2)
        return self.pre_rows(j, t)

    def block2_mlp(self, l):
        P, I = self.P, self.I
        f0 = self.open()
        p = self.ps
        R = self.region(f"f{l}", mod=True)
        z = self.z = R.new("z", [128, 8, 1024])
        gh = [R.new(f"gh{i}", [128, 2, 1024], F32R) for i in range(2)]
        gh_at = (R.off - 16384, R.off - 8192)
        gl = [R.new(f"gl{i}", [128, 2, 1024], F32R) for i in range(2)]
        gl_at = (R.off - 16384, R.off - 8192)
        ta = R.new("ta", [128, 1024])
        tb = R.new("tb", [128, 1024])
        ua = R.new("ua", [128, 1026])
        ub = self.at(f"f{l}_ub", [128, 1026], F32, R.off) if R.off + 4128 <= self.end else None
        assert ub is not None
        cw = self.tfi[:, 8, 0:132].rearrange("p (a b) -> p a b", a=3)
        cb = self.tfi[:, 8, 132:176]
        tcw = P.dma("act", self.tfi[:, 8, 0:176], I["conv"][l], f0)
        tz = [self.zero(ua[:, 0:2], f0), self.zero(ub[:, 0:2], f0)]
        wu, wd = I["w_up_2"][l], I["w_down_2"][l]
        ready = self.uT
        halves = lambda hf: ready[4 * hf:4 * hf + 4]
        g_tok = {}
        down_tok = {}
        free = {"ua": None, "ub": None, "ta": None, "tb": None}
        self.zt = [[None, None] for _ in range(8)]

        def wdown(e, half):
            return lambda k: [(0, wd[e * 256 + k * 128:e * 256 + k * 128 + 128, half * 512:half * 512 + 512])]

        def down(e, half):
            def f(j, b, src, tok):
                cc = slice(half * 512, half * 512 + 512)
                if e == 0:
                    t = self.copy(z[:, j, cc], src, tok, f0)
                else:
                    t = self.tt(z[:, j, cc], src, z[:, j, cc], ALU.add, tok, self.zt[j][half])
                self.zt[j][half] = t
                self.give(b, t)
            return f

        for c in range(11):
            if c < 11:
                fo = c * 256
                hold = {}

                def conv(u, name, tile, dst, t):
                    t = self.stt(dst[:], u[:, 1:1025], cw[:, 1, tile:tile + 1], dst[:], ALU.mult, ALU.add, t)
                    t = self.stt(dst[:], u[:, 0:1024], cw[:, 0, tile:tile + 1], dst[:], ALU.mult, ALU.add, t)
                    free[name] = t
                    return t

                def evac(m, hf, b, src, tok, c=c):
                    u, name = (ua, "ua") if m % 2 == 0 else (ub, "ub")
                    t = self.copy(u[:, 2 + hf * 512:2 + hf * 512 + 512], src, tok, free[name], f0)
                    tile = 22 * (m % 2) + 2 * c + m // 2
                    dst = (ta, tb)[m % 2]
                    t2 = self.act(dst[:, hf * 512:hf * 512 + 512], src, ACT.Identity, tok, tcw, tz,
                                  free["t" + name[1]], f0, scale=cw[:, 2, tile:tile + 1], bias=cb[:, tile:tile + 1])
                    self.give(b, t2)
                    hold.setdefault(m, []).extend([t, t2])
                    if hf == 1:
                        return (lambda: rest(m)) if m < 2 else lambda: lambda: rest(m)

                def rest(m, c=c):
                    u, name = (ua, "ua") if m % 2 == 0 else (ub, "ub")
                    ft = 2 * c + m // 2
                    if m % 2 == 0:
                        t = conv(u, name, ft, ta, hold[m])
                        hold["g"] = self.act(ta[:], ta[:], ACT.Gelu_apprx_tanh, t)
                    else:
                        t = conv(u, name, 22 + ft, tb, hold[m])
                        x = c % 2
                        t = self.tt(tb[:], tb[:], ta[:], ALU.mult, t, hold["g"])
                        free["ta"] = t
                        a = self.copy(gh[x][:, m // 2, :], tb[:], t, down_tok.get(c - 2), f0)
                        d = self.tt(gl[x][:, m // 2, :], tb[:], gh[x][:, m // 2, :].bitcast(F32), ALU.subtract, a,
                                    down_tok.get(c - 2), f0)
                        free["tb"] = [a, d]
                        g_tok.setdefault(c, []).append([a, d])

                self.late_n = 1 if c else None
                self.proj_T(8, self.up(l, c), 4, halves, evac, ring="all", nb=4 if c else 2)
                if c == 0:
                    self.flush()
            if 1 <= c <= 9:
                e = c - 1
                for half in range(2):
                    self.proj_nat(2, wdown(e, half), 512, self.sels, [g_tok[e]] * 8, down(e, half),
                                  act=(gh[e % 2], gl[e % 2]), ring="all")
                self.late_n = None
                down_tok[e] = self.last_mm
        self.late_n = None
        self.flush()
        fe = self.fence()
        self.junk = ta
        xr = [ua[:, 0:1024], ub[:, 0:1024], self.tfl[:, 8, :]]
        nxt = I["norm_mix_pre_2"][l + 1] if l == 0 else None
        zt = self.zt
        self.post(xr, tb, self.tfi[:, 8, :], fe, I["norm_mlp_post_2"][l], nxt, 2 + 2 * l, 3 if l == 0 else None)
        self.zt = zt
        ws = {(e, half): [self.weight(wdown(e, half)(k)) for k in range(2)] for e in (9, 10) for half in range(2)}
        for group in ((0, 1), (2,), (3,), (4,), (5,), (6,), (7,)):
            jobs = [(j, half, *self.take("proj")) for j in group for half in range(2)]
            toks = []
            for e in (9, 10):
                for j, half, b, fw in jobs:
                    for k in range(2):
                        _, w, wt = ws[e, half][k]
                        x, y = self.sels[j](gh[e % 2], k), self.sels[j](gl[e % 2], k)
                        for n, (u, v) in enumerate(((x, self.whi[:, w, :]), (x, self.wlo[:, w, :]), (y, self.whi[:, w, :]))):
                            fin = e == 10 and k == 1 and n == 2
                            tok = P.op("pe", lambda e, b=b, u=u, v=v, first=(e == 9 and k == 0 and n == 0), fin=fin:
                                       e.matmul(p[:, b[0], :], u, v, start=first, stop=fin), fw, wt, g_tok[e], mark=fin)
                            if fin:
                                toks.append(tok)
            for (j, half, b, _), tok in zip(jobs, toks):
                down(10, half)(j, b, p[:, b[0], :], tok)
            for j in group:
                self.advance([lambda j=j: self.post_rows(j)])
            if group == (2,) and l == 0 and self.stop > 4:
                self.soon = self.first_mix(1)
                self.prefetch()
        for w in ws.values():
            self.release(w, tok)
        self.drain()
        self.uT = self.ut


def build_program(nc, I, out, stop=9):
    Kernel(nc, I, out, stop).build()


_INS = ["x", "c", "rel_bias", "ada_w", "ada_b", "ln_g", "ln_b", "a_w_in", "a_w_out", "b_w_in", "b_q_norm", "b_w_uq",
        "b_kv_norm", "b_w_ukv", "b_w_out", "norm_mix_pre_2", "norm_mix_post_2", "w_in_2", "lambda_q1_2", "lambda_k1_2",
        "lambda_q2_2", "lambda_k2_2", "diff_subln_2", "ret_norm_2", "pool_w_2", "pool_scale_2", "w_out_2",
        "norm_mlp_pre_2", "norm_mlp_post_2", "w_up_2", "conv_w_2", "conv_b_2", "w_down_2"]


def declare(nc, inputs, stop=9):
    arrays = {n: np.ascontiguousarray(inputs[n]) for n in _INS}
    conv = np.concatenate([arrays.pop("conv_w_2"), arrays.pop("conv_b_2")[:, None]], 1)
    arrays["conv"] = np.ascontiguousarray(conv.reshape(2, 4, 44, 128).transpose(0, 3, 1, 2).reshape(2, 128, 176))
    arrays.update(host_constants())
    I = {n: nc.dram_tensor("in_" + n, list(a.shape), mybir.dt.from_np(a.dtype), kind="ExternalInput").ap()
         for n, a in arrays.items()}
    I["k_decay2"] = I["k_decay"].rearrange("p h q -> p (h q)")
    out = nc.dram_tensor("out_0", [1, 1024, 1024], F32, kind="ExternalOutput").ap()
    build_program(nc, I, out, stop)
    return {"in_" + n: a for n, a in arrays.items()}


def kernel(**inputs):
    import concourse.bacc as bacc
    from concourse.bass_utils import run_bass_kernel_spmd

    nc = bacc.Bacc("TRN2", target_bir_lowering=False, num_devices=1)
    arrays = declare(nc, inputs)
    r = run_bass_kernel_spmd(nc, [arrays], core_ids=[0])
    return r.results[0]["out_0"]
```
